# Optimizing a Trainium2 kernel written in Bass

```python
import jax, jax.numpy as jnp
from jax import lax
import numpy as np

D_MODEL = 1024
BATCH = 1
SEQ = 512
DEPTH = 2
DEC_BATCH = 8
DEC_SEQ = 4
PAST_LEN = 2048
PAGE_SIZE = 128

HEAD_DIM = 64
D_A = D_MODEL // 2
D_B = D_MODEL // 2
N_HEADS_B = D_B // HEAD_DIM
CONV_A = 3
D_C = D_MODEL
CONV_C = 31
D_FF = ((8 * D_MODEL // 3 + 127) // 128) * 128
CONV_FFN = 3
Q_BLOCK = 128
N_EVEN = (DEPTH + 1) // 2
N_ODD = DEPTH // 2
EPS = 1e-6
D_IN0 = 3 * D_A + 3 * D_B + N_HEADS_B

kernel_name = 'hybrid_shortconv_fox_conformer_convffn_step'

def rmsnorm(x, g):
    xf = x.astype(jnp.float32)
    y = xf * lax.rsqrt(jnp.mean(xf * xf, axis=-1, keepdims=True) + EPS)
    return (y * g.astype(jnp.float32)).astype(x.dtype)

def layernorm(x, g, b):
    xf = x.astype(jnp.float32)
    mu = jnp.mean(xf, axis=-1, keepdims=True)
    xc = xf - mu
    y = xc * lax.rsqrt(jnp.mean(xc * xc, axis=-1, keepdims=True) + EPS)
    return (y * g.astype(jnp.float32) + b.astype(jnp.float32)).astype(x.dtype)

def causal_dwconv(u, hist, w):
    ext = jnp.concatenate([hist.astype(u.dtype), u], axis=1)
    y = lax.conv_general_dilated(ext, w[:, None, :].astype(u.dtype), window_strides=(1,),
                                 padding='VALID', dimension_numbers=('NWC', 'WIO', 'NWC'),
                                 feature_group_count=u.shape[-1])
    return y, ext[:, ext.shape[1] - (w.shape[0] - 1):]

def ab_inputs(x, hist, norm_g, w_in, b_f, conv_w, q_g, k_g):
    bsz, t = x.shape[0], x.shape[1]
    h = rmsnorm(x, norm_g) @ w_in
    splits = [D_A, 2 * D_A, 3 * D_A, 3 * D_A + D_B, 3 * D_A + 2 * D_B, 3 * D_A + 3 * D_B]
    gb, gc, hv, q, k, v, fl = jnp.split(h, splits, axis=-1)
    yc, new_hist = causal_dwconv(gc * hv, hist, conv_w)
    y_a = gb * yc
    q = rmsnorm(q.reshape(bsz, t, N_HEADS_B, HEAD_DIM), q_g)
    k = rmsnorm(k.reshape(bsz, t, N_HEADS_B, HEAD_DIM), k_g)
    v = v.reshape(bsz, t, N_HEADS_B, HEAD_DIM)
    logf = jax.nn.log_sigmoid((fl + b_f).astype(jnp.float32))
    return y_a, q, k, v, logf, new_hist

def fox_attend(q, k, v, cq, ck, q_pos, k_pos):
    s = jnp.einsum('bqhd,bkhd->bhqk', q, k, preferred_element_type=jnp.float32) * (HEAD_DIM ** -0.5)
    s = s + (jnp.transpose(cq, (0, 2, 1))[:, :, :, None] - jnp.transpose(ck, (0, 2, 1))[:, :, None, :])
    s = jnp.where(k_pos[None, :] <= q_pos[:, None], s, -jnp.inf)
    p = jax.nn.softmax(s, axis=-1)
    return jnp.einsum('bhqk,bkhd->bqhd', p.astype(v.dtype), v)

def fox_prompt(q, k, v, logf):
    bsz, s_len, h, d = q.shape
    c = jnp.cumsum(logf, axis=1)
    nb = s_len // Q_BLOCK
    qb = q.reshape(bsz, nb, Q_BLOCK, h, d).transpose(1, 0, 2, 3, 4)
    cb = c.reshape(bsz, nb, Q_BLOCK, h).transpose(1, 0, 2, 3)
    k_pos = jnp.arange(s_len)

    def block(args):
        qi, ci, i = args
        q_pos = i * Q_BLOCK + jnp.arange(Q_BLOCK)
        return fox_attend(qi, k, v, ci, c, q_pos, k_pos)

    out = lax.map(block, (qb, cb, jnp.arange(nb)))
    return out.transpose(1, 0, 2, 3, 4).reshape(bsz, s_len, h * d)

def fox_sample(q, k_new, v_new, logf_new, k_pool, v_pool, logf_pool, page_table):
    bsz, t, h, d = q.shape
    p_len = page_table.shape[1] * PAGE_SIZE
    k_all = jnp.concatenate([k_pool[page_table].reshape(bsz, p_len, h, d).astype(k_new.dtype), k_new], axis=1)
    v_all = jnp.concatenate([v_pool[page_table].reshape(bsz, p_len, h, d).astype(v_new.dtype), v_new], axis=1)
    lf_all = jnp.concatenate([logf_pool[page_table].reshape(bsz, p_len, h).astype(jnp.float32), logf_new], axis=1)
    c = jnp.cumsum(lf_all, axis=1)
    q_pos = p_len + jnp.arange(t)
    k_pos = jnp.arange(p_len + t)
    out = fox_attend(q, k_all, v_all, c[:, p_len:], c, q_pos, k_pos)
    return out.reshape(bsz, t, h * d)

def conformer_conv(x, hist, norm_g, w_pw1, b_pw1, conv_w, conv_b, ln_g, ln_b, w_pw2):
    a, g = jnp.split(rmsnorm(x, norm_g) @ w_pw1 + b_pw1, 2, axis=-1)
    u = a * jax.nn.sigmoid(g)
    y, new_hist = causal_dwconv(u, hist, conv_w)
    y = layernorm(y + conv_b, ln_g, ln_b)
    return jax.nn.silu(y) @ w_pw2, new_hist

def conv_ffn(x, hist, norm_g, w_up, conv_w, w_down):
    gate, val = jnp.split(rmsnorm(x, norm_g) @ w_up, 2, axis=-1)
    gconv, new_hist = causal_dwconv(gate, hist, conv_w)
    return (jax.nn.silu(gconv) * val) @ w_down, new_hist

def setup_inputs(seed: int = 0) -> dict:
    key = jax.random.key(seed)
    ks = jax.random.split(key, 32)
    n_pages = PAST_LEN // PAGE_SIZE
    n_used = DEC_BATCH * n_pages
    n_pool = n_used + n_used // 4

    def nrm(k, shape, scale):
        return jax.random.normal(k, shape, jnp.float32) * scale

    return {
        'x_prompt': nrm(ks[0], (BATCH, SEQ, D_MODEL), 1.0),
        'x_sample': nrm(ks[1], (DEC_BATCH, DEC_SEQ, D_MODEL), 1.0),
        'cache_k': nrm(ks[2], (N_EVEN, n_pool, PAGE_SIZE, N_HEADS_B, HEAD_DIM), 1.0),
        'cache_v': nrm(ks[3], (N_EVEN, n_pool, PAGE_SIZE, N_HEADS_B, HEAD_DIM), 1.0),
        'cache_logf': jax.nn.log_sigmoid(3.0 + nrm(ks[4], (N_EVEN, n_pool, PAGE_SIZE, N_HEADS_B), 1.0)),
        'page_table': jax.random.permutation(ks[5], n_pool)[:n_used].reshape(DEC_BATCH, n_pages).astype(jnp.int32),
        'state_conv_a': nrm(ks[6], (N_EVEN, DEC_BATCH, CONV_A - 1, D_A), 1.0),
        'state_conv_c': nrm(ks[7], (N_ODD, DEC_BATCH, CONV_C - 1, D_C), 1.0),
        'state_ffn': nrm(ks[8], (DEPTH, DEC_BATCH, CONV_FFN - 1, D_FF), 1.0),
        'norm_mix0': 1.0 + nrm(ks[9], (N_EVEN, D_MODEL), 0.02),
        'w_in0': nrm(ks[10], (N_EVEN, D_MODEL, D_IN0), D_MODEL ** -0.5),
        'b_forget': 3.0 + nrm(ks[11], (N_EVEN, N_HEADS_B), 0.1),
        'conv_a_w': nrm(ks[12], (N_EVEN, CONV_A, D_A), CONV_A ** -0.5),
        'q_norm': 1.0 + nrm(ks[13], (N_EVEN, HEAD_DIM), 0.02),
        'k_norm': 1.0 + nrm(ks[14], (N_EVEN, HEAD_DIM), 0.02),
        'w_out0': nrm(ks[15], (N_EVEN, D_A + D_B, D_MODEL), (D_A + D_B) ** -0.5),
        'norm_mix1': 1.0 + nrm(ks[16], (N_ODD, D_MODEL), 0.02),
        'w_pw1': nrm(ks[17], (N_ODD, D_MODEL, 2 * D_C), D_MODEL ** -0.5),
        'b_pw1': nrm(ks[18], (N_ODD, 2 * D_C), 0.02),
        'conv_c_w': nrm(ks[19], (N_ODD, CONV_C, D_C), CONV_C ** -0.5),
        'conv_c_b': nrm(ks[20], (N_ODD, D_C), 0.02),
        'ln_c_g': 1.0 + nrm(ks[21], (N_ODD, D_C), 0.02),
        'ln_c_b': nrm(ks[22], (N_ODD, D_C), 0.02),
        'w_pw2': nrm(ks[23], (N_ODD, D_C, D_MODEL), D_C ** -0.5),
        'norm_ffn': 1.0 + nrm(ks[24], (DEPTH, D_MODEL), 0.02),
        'w_up': nrm(ks[25], (DEPTH, D_MODEL, 2 * D_FF), D_MODEL ** -0.5),
        'conv_ffn_w': nrm(ks[26], (DEPTH, CONV_FFN, D_FF), CONV_FFN ** -0.5),
        'w_down': nrm(ks[27], (DEPTH, D_FF, D_MODEL), D_FF ** -0.5),
    }

def reference(x_prompt, x_sample, cache_k, cache_v, cache_logf, page_table, state_conv_a,
              state_conv_c, state_ffn, norm_mix0, w_in0, b_forget, conv_a_w, q_norm, k_norm,
              w_out0, norm_mix1, w_pw1, b_pw1, conv_c_w, conv_c_b, ln_c_g, ln_c_b, w_pw2,
              norm_ffn, w_up, conv_ffn_w, w_down):
    yp, ys = x_prompt, x_sample
    pca, sca, pk, sk, pv, sv, plf, slf, pcc, scc, pff, sff = ([] for _ in range(12))
    for layer in range(DEPTH):
        i = layer // 2
        if layer % 2 == 0:
            zero_a = jnp.zeros((yp.shape[0], CONV_A - 1, D_A), yp.dtype)
            ya, q, k, v, lf, ha = ab_inputs(yp, zero_a, norm_mix0[i], w_in0[i], b_forget[i],
                                            conv_a_w[i], q_norm[i], k_norm[i])
            yb = fox_prompt(q, k, v, lf)
            yp = yp + jnp.concatenate([ya, yb.astype(ya.dtype)], axis=-1) @ w_out0[i]
            pca.append(ha); pk.append(k); pv.append(v); plf.append(lf)
            ya, q, k, v, lf, ha = ab_inputs(ys, state_conv_a[i], norm_mix0[i], w_in0[i], b_forget[i],
                                            conv_a_w[i], q_norm[i], k_norm[i])
            yb = fox_sample(q, k, v, lf, cache_k[i], cache_v[i], cache_logf[i], page_table)
            ys = ys + jnp.concatenate([ya, yb.astype(ya.dtype)], axis=-1) @ w_out0[i]
            sca.append(ha); sk.append(k); sv.append(v); slf.append(lf)
        else:
            zero_c = jnp.zeros((yp.shape[0], CONV_C - 1, D_C), yp.dtype)
            mp, hc = conformer_conv(yp, zero_c, norm_mix1[i], w_pw1[i], b_pw1[i], conv_c_w[i],
                                    conv_c_b[i], ln_c_g[i], ln_c_b[i], w_pw2[i])
            yp = yp + mp
            pcc.append(hc)
            ms, hc = conformer_conv(ys, state_conv_c[i], norm_mix1[i], w_pw1[i], b_pw1[i], conv_c_w[i],
                                    conv_c_b[i], ln_c_g[i], ln_c_b[i], w_pw2[i])
            ys = ys + ms
            scc.append(hc)
        zero_f = jnp.zeros((yp.shape[0], CONV_FFN - 1, D_FF), yp.dtype)
        fp, hf = conv_ffn(yp, zero_f, norm_ffn[layer], w_up[layer], conv_ffn_w[layer], w_down[layer])
        yp = yp + fp
        pff.append(hf)
        fs, hf = conv_ffn(ys, state_ffn[layer], norm_ffn[layer], w_up[layer], conv_ffn_w[layer], w_down[layer])
        ys = ys + fs
        sff.append(hf)
    return (yp, ys,
            jnp.stack(pca), jnp.stack(sca),
            jnp.stack(pk), jnp.stack(sk),
            jnp.stack(pv), jnp.stack(sv),
            jnp.stack(plf), jnp.stack(slf),
            jnp.stack(pcc), jnp.stack(scc),
            jnp.stack(pff), jnp.stack(sff))


_drawn_inputs = setup_inputs


def setup_inputs(seed=0):
    import zlib

    import numpy as np

    out = dict(_drawn_inputs(seed))
    spreads = {}
    factors = {'q_norm': 8.0,
     'k_norm': 2.933,
     'b_pw1': 2.722,
     'conv_c_b': 3.29,
     'ln_c_g': 5.359,
     'ln_c_b': 6.418}
    for name, (base, spread) in spreads.items():
        noise = np.random.default_rng([zlib.crc32(name.encode()), seed]).standard_normal(out[name].shape)
        drawn = base * np.exp(spread * noise) if base else spread * noise
        out[name] = __import__('jax').numpy.asarray(drawn.astype(out[name].dtype))
    for name, factor in factors.items():
        out[name] = (out[name] * factor).astype(out[name].dtype)
    return out
```

```python
from contextlib import ExitStack, contextmanager

import concourse.bass as bass
from concourse import mybir

F32 = mybir.dt.float32
F32R = mybir.dt.float32r
I32 = mybir.dt.int32
ALU = mybir.AluOpType
ACT = mybir.ActivationFunctionType
AX = mybir.AxisListType
ds = bass.ds

P = 128
D = 1024
DC = D // P
TP = 512
NB, NT = 8, 4
TS = NB * NT
T = TP + TS
HT = T // 2
NH, HD = 8, 64
PG = 16
NPOOL = 160
DFF = 2816
FC = DFF // P
HALF = (12, 10)
CA, CF, CC = 3, 3, 31
EPS = 1e-6
MASKED = -1e30
SLOTS = 4
KS = 8
SCRATCH = 1024
NQ = T - TP
UT = (CC - 1) + TS
FT = 2 + 2 * NB


class Steps:

    def __init__(self):
        self.base, self.local, self.i, self.per = 0, 0, None, 0

    def tick(self):
        self.local += 1
        return self.now()

    def now(self):
        at = self.base + self.local
        return at if self.i is None else self.i * self.per + at

    @contextmanager
    def loop(self, eng, start, end, per):
        self.base += self.local - start * per
        self.local = 0
        with eng.Fori(start, end) as i:
            self.i, self.per = i, per
            yield i
        assert self.local == per, (self.local, per)
        self.base += end * per
        self.local, self.i, self.per = 0, None, 0


class Phase:

    def __init__(self, name, slab0, group0, turns, tiles, per_group, residual):
        self.name, self.slab0, self.group0 = name, slab0, group0
        self.turns, self.tiles, self.per_group = turns, tiles, per_group
        self.slabs = 4 * turns
        self.slab1 = slab0 + self.slabs
        self.group1 = group0 + self.slabs // per_group
        self.residual = residual

    def slab(self, i, j):
        return i * 4 + (self.slab0 + j)

    def group(self, i, j):
        return i * (4 // self.per_group) + (self.group0 + j // self.per_group)


def plan():
    phases, slab = {}, 0
    groups = {False: 0, True: DC}
    rows = [("qkv", 3, DC, 1), ("gates", 3, DC, 1), ("out", 2, DC, 1)]
    ffn = lambda l: [(f"up{l}0", HALF[0] // 2, DC, 1), (f"down{l}0", 4, HALF[0] // 2, 2),
                     (f"up{l}1", HALF[1] // 2, DC, 1), (f"down{l}1", 4, HALF[1] // 2, 2)]
    rows += ffn(0) + [("pw1", 4, DC, 1), ("pw2", 2, DC, 1)] + ffn(1)
    for name, turns, tiles, per in rows:
        residual = name in ("out", "pw2") or name.startswith("down")
        p = phases[name] = Phase(name, slab, groups[residual], turns, tiles, per, residual)
        slab, groups[residual] = p.slab1, p.group1
    return phases


def param_rows():
    at, rows = 0, {}
    for name, n in (("mix0", DC), ("qk", 2), ("conv_a", CA * 4), ("ffn", 2 * DC), ("conv_f", 2 * CF * FC),
                    ("mix1", DC), ("b_pw1", 2 * DC), ("conv_cb", DC), ("ln_g", DC), ("ln_b", DC),
                    ("conv_c", CC * DC)):
        rows[name] = (at, n)
        at += n
    return rows, at


def row_blocks(r0, n):
    out = []
    while n:
        k = min(n, P - r0 % P)
        out.append((r0, k))
        r0, n = r0 + k, n - k
    return out


def build(nc, a, o):
    ph = plan()
    order = list(ph.values())
    prow, n_rows = param_rows()
    with ExitStack() as ctx:
        sem = lambda name: ctx.enter_context(nc.semaphore(name))

        top = [SCRATCH]

        def place(name, shape, dt, at=None):
            size = 4
            for n in shape[1:]:
                size *= n
            if at is None:
                at = top[0]
                top[0] += (size + 31) // 32 * 32
            assert at + size <= 229344, name
            return nc.alloc_sbuf_tensor_at(name, shape, dt, offset=at), at

        CH = T * 4
        x, _ = place("x", [P, DC, T], F32)
        xa_h, xa_at = place("xa_h", [P, DC, T], F32R)
        xa_l, _ = place("xa_l", [P, DC, T], F32R)
        h_h, hh_at = place("h_h", [P, HALF[0], T], F32R)
        h_l, hl_at = place("h_l", [P, HALF[0], T], F32R)
        w_raw, raw_at = place("w_raw", [P, SLOTS, DC * P], F32)
        w_h, wh_at = place("w_h", [P, SLOTS, DC * P], F32R)
        w_l, wl_at = place("w_l", [P, SLOTS, DC * P], F32R)
        ident, _ = place("ident", [P, P], F32)
        ones, _ = place("ones", [P, P], F32)
        head_ones, _ = place("head_ones", [P, P], F32)
        causal, _ = place("causal", [P, P], F32)
        later, _ = place("later", [P, P], F32)
        params, _ = place("params", [P, n_rows], F32)
        r_all, _ = place("r_all", [P, T], F32)
        ssum, ss_at = place("ssum", [P, T], F32)
        sq, sq_at = place("sq", [P, 2, T], F32)
        tmp, tmp_at = place("tmp", [P, 2, T], F32)
        base = top[0]
        x_rows, _ = place("x_rows", [P, 5, D], F32, hh_at)
        p_rows, _ = place("p_rows", [P, 4, P], F32, hh_at + 5 * D * 4)
        qkv, _ = place("qkv", [P, 12, T], F32)
        kt, kt_at = place("kt", [P, 4, 4 * P], F32)
        v_tok, vt_at = place("v_tok", [P, 4, 4 * P], F32)
        sc, sc_at = place("sc", [P, PG + 1, 32], F32)
        pr, pr_at = place("pr", [P, PG + 1, 32], F32)
        dk, _ = place("dk", [P, NB, PG, NH], F32)
        cn_all, _ = place("cn_all", [P, NH, NB, NT], F32)
        q_diag, _ = place("q_diag", [P, 4, NB, 8], F32)
        nbias, _ = place("nbias", [TS, NB, NH, NT], F32)
        small, _ = place("small", [P, 224], F32)
        fw, _ = place("fw", [P, DC, NH], F32)
        fw_h, _ = place("fw_h", [P, DC, NH], F32R)
        fw_l, _ = place("fw_l", [P, DC, NH], F32R)
        ext_a, _ = place("ext_a", [P, 4, NB, CA - 1 + NT], F32)
        tail_a, _ = place("tail_a", [P, 4, FT], F32)
        lf_row, _ = place("lf_row", [P, 5, NH], F32)
        m1, gmax, diag = small[:, 0:32], small[0:32, 32:33], small[0:32, 64:96]
        p_sum, rec = small[:, 96:128], small[:, 128:160]
        cq = small[:, 160:192]
        cns = small[0:TS, 192:200]
        b_f = small[0:NH, 200:201]
        rmax, rsum, rinv = small[:, 204:208], small[:, 208:212], small[:, 212:216]
        k_pg, _ = place("k_pg", [P, KS, 4 * P], F32, xa_at)
        cb, _ = place("cb", [P, NH, TP], F32, xa_at + KS * 2048)
        v_pg, _ = place("v_pg", [P, PG, 4 * P], F32, wh_at)
        u4, _ = place("u4", [P, 4, T], F32, hh_at + 8 * CH)
        g4, _ = place("g4", [P, 4, T], F32, hl_at + 8 * CH)
        lf_pg, _ = place("lf_pg", [P, D], F32, kt_at)
        lf_k, _ = place("lf_k", [P, NH * NB, PG], F32, kt_at + 4096)
        suf, _ = place("suf", [P, NH * NB, PG], F32, vt_at)
        pgix, _ = place("pgix", [P, 1], I32, vt_at + 4096)
        fz, _ = place("fz", [NH, T], F32, kt_at)
        fe, _ = place("fe", [NH, T], F32, kt_at + CH)
        seg, _ = place("seg", [NH, T], F32, kt_at + 2 * CH)
        cmask, _ = place("cmask", [NH, 2, TP], F32, kt_at)
        logf, _ = place("logf", [NH, T], F32, vt_at)
        cum, _ = place("cum", [NH, T], F32, vt_at + CH)
        cnm, _ = place("cnm", [NH, NH, TS], F32, vt_at + 2 * CH)
        k_row, _ = place("k_row", [P, 2, 4 * P], F32, hh_at + 8 * CH)
        s_row, _ = place("s_row", [TS, 2, 4 * P], F32, hh_at + 8 * CH + 4096)
        a_row, _ = place("a_row", [2 * NB, 4 * P], F32, pr_at)
        a_out, _ = place("a_out", [FT, 4 * P], F32, sc_at)
        sb, _ = place("sb", [P, 4, TP], F32, hl_at + 8 * CH)
        pt, _ = place("pt", [P, 2, TP], F32, ss_at)
        q_s, _ = place("q_s", [P, TP], F32, ss_at + 4096)
        k_s, _ = place("k_s", [P, TP], F32, ss_at + 6144)
        v_s, _ = place("v_s", [P, 4, P], F32, ss_at + 8192)
        top[0] = base
        gate, _ = place("gate", [P, 2, T], F32)
        cv, _ = place("cv", [P, 2, T], F32)
        sl, _ = place("sl", [P, 2, T], F32)
        sr, sr_at = place("sr", [P, 2, T], F32)
        ext_f, _ = place("ext_f", [P, FC, NB, CF - 1 + NT], F32)
        tail_f, _ = place("tail_f", [P, FC, FT], F32)
        f_row, fr_at = place("f_row", [FT, DFF], F32)
        yc, yc_at = place("yc", [P, DC, T], F32)
        y_row, _ = place("y_row", [P, 2, D], F32, yc_at)
        ua, _ = place("ua", [P, 2, T], F32, base)
        u, _ = place("u", [P, 2, T], F32, base + 2 * CH)
        sg, _ = place("sg", [P, 2, T], F32, base + 4 * CH)
        prod, _ = place("prod", [P, TS, CC], F32, sr_at)
        ext_c, _ = place("ext_c", [P, DC, NB, CC - 1 + NT], F32, hh_at + 8 * CH)
        c_row, _ = place("c_row", [4 * (CC - 1), 2, D], F32, hl_at + 8 * CH)
        tail_c, _ = place("tail_c", [P, DC, UT], F32, fr_at)
        u_row, _ = place("u_row", [UT, D], F32, fr_at + 4096)

        pair = [nc.alloc_psum_tensor(f"pair{n}", [P, 2, 512], F32) for n in range(2)]
        psum_s = nc.alloc_psum_tensor("psum_s", [P, 2, 512], F32)
        bank = [nc.alloc_psum_tensor(f"bank{n}", [P, 512], F32) for n in range(2)]
        pb = [pair[0][:, 0, :], pair[0][:, 1, :], pair[1][:, 0, :], pair[1][:, 1, :]]

        s_raw = [sem(f"raw{j}") for j in range(SLOTS)]
        s_hi, s_lo = sem("hi"), sem("lo")
        s_slab = sem("slab")
        s_free = sem("free")
        s_prm, s_xld, s_st, s_fw, s_ix, s_lf = (sem(n) for n in (
            "params_in", "x_in", "state_in", "fw_in", "index_in", "logf_in"))
        s_cst = sem("constants")
        s_tp = sem("x_turned")
        s_xnew = sem("x_new")
        s_sq, s_ss, s_stat = sem("squares"), sem("added"), sem("sums")
        s_xhi, s_xlo = sem("xa_high"), sem("xa_low")
        s_var, s_rt, s_r = sem("variance"), sem("root"), sem("inv_root")
        s_dve = sem("dve_step")
        s_ya, s_cv, s_sl, s_sr, s_hhi, s_hlo = (sem(n) for n in (
            "y_a", "conv", "silu", "silu_r", "h_high", "h_low"))
        s_out, s_rowdma, s_aout = sem("written"), sem("row_written"), sem("a_written")
        s_misc, s_miscd = sem("short"), sem("short_read")
        s_suf, s_fz, s_fe, s_cum, s_cm, s_cbp, s_cb = (sem(n) for n in (
            "later_pages", "forget_in", "forget_ln", "cum", "c_masked", "c_spread", "c_copied"))
        s_qsq, s_hv, s_hrt, s_qk, s_tail = (sem(n) for n in ("qk_squares", "qk_var", "qk_root", "qk_normed", "tail"))
        s_k = [sem(f"k{n}") for n in range(KS)]
        s_v = [sem(f"v{n}") for n in range(PG)]
        s_tr, s_kt, s_sp, s_sc, s_sev = (sem(n) for n in (
            "page_turned", "page_copied", "page_scored", "batch_scored", "scores_read"))
        s_m1, s_mt, s_dg, s_mb = (sem(n) for n in ("max_keys", "max_turned", "max_diag", "max_spread"))
        s_sm, s_p, s_lp, s_l = (sem(n) for n in ("shifted", "exps", "exps_added", "exps_summed"))
        s_pvp, s_oev, s_rec = sem("page_valued"), sem("values_read"), sem("inv_sum")
        s_qs, s_s, s_sb, s_pe = (sem(n) for n in ("pair_copied", "p_scored", "p_biased", "p_exp"))
        s_sbr, s_pn, s_ptt, s_ptc, s_po, s_pod = (sem(n) for n in (
            "p_read", "p_norm", "p_turned", "p_tcopied", "p_valued", "p_out"))
        s_rows, s_rowsd = sem("rows_turned"), sem("rows_read")
        s_fst, s_fstd = sem("state_turned"), sem("state_read")
        s_sig, s_u, s_ux, s_mu, s_xc, s_ty, s_s32 = (sem(n) for n in (
            "u_sig", "u", "u_kept", "mean", "centred", "scaled", "swish"))
        n_out = [0]

        halves = lambda ap: ap.rearrange("p (h t) -> p h t", h=2)
        gview = lambda b: pair[b][:, :, 0:HT]
        par = lambda name, k: params[:, ds(k + prow[name][0], 1)]
        R = {}
        at = 0
        for name, n in (("kv", 10), ("ffn0", 6), ("conv_c", 2), ("ffn1", 6), ("y", 10)):
            R[name] = at
            at += n
        XN = dict(init=0, **{p.name: p.group0 for p in order if p.residual})
        NORM = dict(init=0, out=1, down01=2, pw2=3)
        SUM = dict(init=0, out=1, down01=2, mean=3, var=4, pw2=5)
        SQ = dict(init=0, out=1, down01=2, var=3, pw2=4)
        GAIN = dict(init=("mix0", 0), out=("ffn", 0), down01=("mix1", 0), pw2=("ffn", DC))
        HB = dict(out=0, up0=8, pw2=8 + FC, up1=16 + FC)

        block = ctx.enter_context(nc.Block())

        def slab_tiles(s):
            for p in order:
                if p.slab0 <= s < p.slab1:
                    return p.tiles

        def turns(eng, phase, body, peel=0):
            for i in range(peel):
                body(i, False)
            if phase.turns - 1 > peel:
                with eng.Fori(peel, phase.turns - 1) as i:
                    body(i, False)
            body(phase.turns - 1, True)

        def ahead(split, phase, i, j, last):
            turn, slot = i + (phase.slab0 // 4 + (j + 3) // 4), (j + 3) % 4
            tiles = phase.tiles
            if last and j >= 1:
                tiles = slab_tiles(phase.slab1 + j - 1)
                if tiles is None or phase is ph["gates"]:
                    return
            split(turn, slot, tiles)

        @block.sync
        def _(sp):
            for k in range(4):
                sp.dma_start(x_rows[:, k, :], a["x_prompt"][0, k * P:(k + 1) * P, :]).then_inc(s_xld, 16)
            sp.dma_start(x_rows[0:TS, 4, :], a["x_sample"].rearrange("b t d -> (b t) d")).then_inc(s_xld, 16)
            chunks = lambda ap: ap.rearrange("a (c p) -> (a c) p", p=P)
            sources = dict(mix0=chunks(a["norm_mix0"]), conv_a=chunks(a["conv_a_w"].rearrange("a k d -> (a k) d")),
                           ffn=chunks(a["norm_ffn"]), conv_f=chunks(a["conv_ffn_w"].rearrange("l k d -> (l k) d")),
                           mix1=chunks(a["norm_mix1"]), b_pw1=chunks(a["b_pw1"]), conv_cb=chunks(a["conv_c_b"]),
                           ln_g=chunks(a["ln_c_g"]), ln_b=chunks(a["ln_c_b"]),
                           conv_c=chunks(a["conv_c_w"].rearrange("a k d -> (a k) d")))
            for name, (r0, n) in prow.items():
                if name == "qk":
                    for r, g in enumerate(("q_norm", "k_norm")):
                        for hh in range(2):
                            sp.dma_start(p_rows[r0 + r:r0 + r + 1, 0, hh * HD:(hh + 1) * HD], a[g]).then_inc(s_prm, 16)
                    continue
                for at, k in row_blocks(r0, n):
                    done = at - r0
                    sp.dma_start(p_rows[at % P:at % P + k, at // P, :], sources[name][done:done + k, :])\
                      .then_inc(s_prm, 16)

            def load(phase, i, j, src):
                s = phase.slab(i, j)
                if not (isinstance(s, int) and s < SLOTS):
                    sp.wait_ge(s_lo, s - (SLOTS - 1))
                sp.dma_start(w_raw[:, j, 0:phase.tiles * P].rearrange("p (k n) -> p k n", n=P), src)\
                  .then_inc(s_raw[j], 16)

            def cols(w, at, tiles=DC, k0=0):
                return w.rearrange("(k p) n -> p k n", p=P)[:, k0:k0 + tiles, ds(at, P)]

            def out(dst, src, signal=None):
                sp.dma_start(dst, src).then_inc(signal or s_out, 16)
                if signal is None:
                    n_out[0] += 1

            w_in, w_out = a["w_in0"][0], a["w_out0"][0]
            for j in range(4):
                load(ph["qkv"], 0, j, cols(w_in, 1536 + j * P))
            sp.dma_start(pgix[:, :], a["page_table"].rearrange("b (p a) -> (b p) a", a=1)).then_inc(s_ix, 16)
            sp.dma_start(a_row[:, :], a["state_conv_a"][0].rearrange("b t d -> (b t) d")).then_inc(s_st, 16)
            sp.dma_start(fw[:, :, :], w_in.rearrange("(k p) n -> p k n", p=P)[:, :, 3072:3080]).then_inc(s_fw, 16)
            sp.dma_start(b_f, a["b_forget"].rearrange("a h -> h a")).then_inc(s_fw, 16)
            with sp.Fori(1, 3) as i:
                for j in range(4):
                    load(ph["qkv"], i, j, cols(w_in, i * 512 + (1536 + j * P)))
            for i, at in enumerate((512, 1024, 0)):
                for j in range(4):
                    load(ph["gates"], i, j, cols(w_in, at + j * P))
            for j in range(4):
                load(ph["out"], 0, j, cols(w_out, j * P))
            out(o["s_conv_c"][0, :, 0:CC - 1 - NT, :], a["state_conv_c"][0, :, NT:CC - 1, :])

            sp.wait_ge(s_slab, ph["gates"].slab1)

            def page(b, p, cache, slots, done, first):
                pid = sp.value_load(a["page_table"][ds(b, 1), p:p + 1], min_val=0, max_val=NPOOL - 1)
                place_, arrived = ((k_pg, s_k) if cache == "cache_k" else (v_pg, s_v))
                if not first:
                    sp.wait_ge(done, b * PG + (p - slots + 1))
                sp.dma_start(place_[:, p % slots, :], a[cache][0, ds(pid, 1)].rearrange("a k h d -> (a k) (h d)"))\
                  .then_inc(arrived[p % slots], 16)

            for p in range(PG):
                page(0, p, "cache_v", PG, s_pvp, True)
            for p in range(KS):
                page(0, p, "cache_k", KS, s_tr, True)
            for t in range(4):
                sp.wait_ge(s_rowsd, R["kv"] + 2 * t + 1)
                out(o["p_k"][0, 0, t * P:(t + 1) * P].rearrange("t h d -> t (h d)"), k_row[:, t % 2, :], s_rowdma)
                sp.wait_ge(s_rowsd, R["kv"] + 2 * t + 2)
                out(o["p_v"][0, 0, t * P:(t + 1) * P].rearrange("t h d -> t (h d)"), v_tok[:, t, :])
            sp.wait_ge(s_rowsd, R["kv"] + 10)
            out(o["s_k"][0].rearrange("b t h d -> (b t) (h d)"), s_row[:, 0, :])
            out(o["s_v"][0].rearrange("b t h d -> (b t) (h d)"), s_row[:, 1, :])
            sp.wait_ge(s_miscd, 9)
            with nc.allow_non_contiguous_dma(reason="32-byte rows of log forgets"):
                out(o["p_logf"][0, 0].rearrange("(t p) h -> p t h", p=P), lf_row[:, 0:4, :])
                out(o["s_logf"][0].rearrange("b t h -> (b t) h"), lf_row[0:TS, 4, :])
            out(o["p_conv_a"][0, 0], a_out[0:2, :], s_aout)
            out(o["s_conv_a"][0].rearrange("b t d -> (b t) d"), a_out[2:FT, :], s_aout)
            for p in range(KS, PG):
                page(0, p, "cache_k", KS, s_tr, False)
            with sp.Fori(1, NB) as b:
                for p in range(PG):
                    page(b, p, "cache_k", KS, s_tr, False)
                for p in range(PG):
                    page(b, p, "cache_v", PG, s_pvp, False)
            for j in range(4):
                load(ph["out"], 1, j, cols(w_out, 512 + j * P))

            def ffn(l):
                up, down = a["w_up"][l], a["w_down"][l]
                sp.wait_ge(s_xhi, 8 * NORM["out" if l == 0 else "pw2"] + 1)
                sp.wait_ge(s_out, 16 * n_out[0])
                sp.dma_start(f_row[0:2 * NB, :], a["state_ffn"][l].rearrange("b t d -> (b t) d")).then_inc(s_st, 16)
                for half in range(2):
                    pu, pd, k0 = ph[f"up{l}{half}"], ph[f"down{l}{half}"], half * HALF[0]
                    with sp.Fori(0, pu.turns) as i:
                        for j in range(4):
                            load(pu, i, j, cols(up, i * (2 * P) + ((j % 2) * DFF + (k0 + j // 2) * P)))
                    with sp.Fori(0, pd.turns) as i:
                        for j in range(4):
                            load(pd, i, j, cols(down, i * (2 * P) + (j // 2) * P, pd.tiles,
                                                k0 + (j % 2) * pd.tiles))
                sp.wait_ge(s_rowsd, R[f"ffn{l}"] + 6)
                out(o["p_ffn"][l, 0], f_row[0:2, :])
                out(o["s_ffn"][l].rearrange("b t d -> (b t) d"), f_row[2:FT, :])

            ffn(0)
            n_out.append(n_out[0])
            sp.wait_ge(s_slab, ph["down01"].slab1)
            for k in range(2):
                sp.dma_start(c_row[:, k, :], a["state_conv_c"][0, 4 * k:4 * k + 4].rearrange("b t d -> (b t) d"))\
                  .then_inc(s_st, 16)
            with sp.Fori(0, ph["pw1"].turns) as i:
                for j in range(4):
                    load(ph["pw1"], i, j, cols(a["w_pw1"][0], i * (2 * P) + ((j % 2) * D + (j // 2) * P)))
            for i in range(2):
                for j in range(4):
                    load(ph["pw2"], i, j, cols(a["w_pw2"][0], i * 512 + j * P))
            sp.wait_ge(s_rowsd, R["conv_c"] + 2)
            out(o["p_conv_c"][0, 0], u_row[0:CC - 1, :])
            for b in range(NB):
                out(o["s_conv_c"][0, b, CC - 1 - NT:CC - 1, :],
                    u_row[CC - 1 + NT * b:CC - 1 + NT * (b + 1), :])
            ffn(1)
            for t in range(5):
                sp.wait_ge(s_rowsd, R["y"] + 2 * t + 2)
                if t < 4:
                    out(o["y_prompt"][0, t * P:(t + 1) * P, :], y_row[:, t % 2, :], s_rowdma)
                else:
                    out(o["y_sample"].rearrange("b t d -> (b t) d"), y_row[0:TS, 0, :])
            sp.wait_ge(s_rowdma, 16 * 8)
            sp.wait_ge(s_aout, 16 * 2)
            sp.wait_ge(s_out, 16 * n_out[0])

        @block.gpsimd
        def _(pool):
            g = nc.gpsimd
            g.memset(ident[:, :], 0.0).then_inc(s_cst, 1)
            g.memset(ones[:, :], 1.0).then_inc(s_cst, 1)
            g.memset(head_ones[:, :], 0.0).then_inc(s_cst, 1)
            g.memset(causal[:, :], 0.0).then_inc(s_cst, 1)
            g.memset(later[:, :], 1.0).then_inc(s_cst, 1)
            g.memset(nbias[:, :, :, :], 0.0).then_inc(s_cst, 1)
            g.memset(q_diag[:, :, :, :], 0.0).then_inc(s_cst, 1)
            g.memset(sc[:, PG, :], MASKED).then_inc(s_cst, 1)
            pool.wait_ge(s_cst, 8)
            g.memset(head_ones[0:HD, 0:HD], 1.0).then_inc(s_cst, 1)
            g.memset(head_ones[HD:P, HD:P], 1.0).then_inc(s_cst, 1)
            pool.wait_ge(s_cst, 10)
            g.affine_select(out=ident[:, :], in_=ident[:, :], compare_op=ALU.not_equal, fill=1.0, base=0,
                            pattern=[[-1, P]], channel_multiplier=1).then_inc(s_cst, 1)
            g.affine_select(out=causal[:, :], in_=causal[:, :], compare_op=ALU.is_ge, fill=MASKED, base=0,
                            pattern=[[-1, P]], channel_multiplier=1).then_inc(s_cst, 1)
            g.affine_select(out=later[:, :], in_=later[:, :], compare_op=ALU.is_gt, fill=0.0, base=0,
                            pattern=[[-1, P]], channel_multiplier=1).then_inc(s_cst, 1)
            g.affine_select(out=nbias[:, :, :, :], in_=nbias[:, :, :, :], compare_op=ALU.is_ge, fill=MASKED, base=0,
                            pattern=[[-NT, NB], [0, NH], [0, NT]], channel_multiplier=1).then_inc(s_cst, 1)
            pool.wait_ge(s_cst, 14)
            g.affine_select(out=nbias[:, :, :, :], in_=nbias[:, :, :, :], compare_op=ALU.is_ge, fill=MASKED, base=0,
                            pattern=[[NT, NB], [0, NH], [1, NT]], channel_multiplier=-1).then_inc(s_cst, 1)
            pool.wait_ge(s_ix, 16)
            g.indirect_dma_start(out=lf_pg[:, :], out_offset=None,
                                 in_=a["cache_logf"][0].rearrange("n k h -> n (k h)"),
                                 in_offset=bass.IndirectOffsetOnAxis(ap=pgix[:, 0:1], axis=0)).then_inc(s_lf, 16)
            pool.wait_ge(s_fw, 33)
            g.tensor_tensor(fw_l[:, :, :], fw[:, :, :], fw_h[:, :, :].bitcast(F32), ALU.subtract).then_inc(s_fw, 1)

            def split_low(turn, slot, tiles):
                n = tiles * P
                pool.wait_ge(s_hi, turn * 4 + (slot + 1))
                g.tensor_tensor(w_l[:, slot, 0:n], w_raw[:, slot, 0:n], w_h[:, slot, 0:n].bitcast(F32),
                                ALU.subtract).then_inc(s_lo, 1)

            for slot in range(3):
                split_low(0, slot, DC)
            for phase in (ph["qkv"], ph["gates"]):
                def turn(i, last, phase=phase):
                    for j in range(4):
                        ahead(split_low, phase, i, j, last)
                turns(pool, phase, turn)
            for slot in range(3):
                split_low(ph["out"].slab0 // 4, slot, DC)
            def turn(i, last):
                for j in range(4):
                    ahead(split_low, ph["out"], i, j, last)
            turns(pool, ph["out"], turn)

            def ffn(l):
                for half in range(2):
                    pu, pd = ph[f"up{l}{half}"], ph[f"down{l}{half}"]

                    def turn(i, last):
                        for j in range(4):
                            ahead(split_low, pu, i, j, last)
                            if j % 2:
                                k = i * 2 + (l * FC + half * HALF[0] + j // 2)
                                pool.wait_ge(s_sl, k + 1)
                                pool.wait_ge(s_r, SQ["out" if l == 0 else "pw2"] + 1)
                                pool.wait_ge(s_free, pu.group(i, j) - 3)
                                g.tensor_tensor(sr[:, j // 2, :], sl[:, j // 2, :], r_all[:, :], ALU.mult)\
                                 .then_inc(s_sr, 1)
                    turns(pool, pu, turn)

                    def turn(i, last):
                        for j in range(4):
                            ahead(split_low, pd, i, j, last)
                    turns(pool, pd, turn)
            ffn(0)
            for phase in (ph["pw1"], ph["pw2"]):
                def turn(i, last, phase=phase):
                    for j in range(4):
                        ahead(split_low, phase, i, j, last)
                turns(pool, phase, turn)
            ffn(1)

        @block.scalar
        def _(act):
            A = nc.scalar.activation

            def apart(i):
                if not isinstance(i, int):
                    act.wait_ge(s_cst, 15)

            def split_high(turn, slot, tiles):
                n = tiles * P
                act.wait_ge(s_raw[slot], turn * 16 + 16)
                if not (isinstance(turn, int) and turn == 0):
                    act.wait_ge(s_slab, turn * 4 + (slot - 3))
                A(w_h[:, slot, 0:n], w_raw[:, slot, 0:n], ACT.Copy).then_inc(s_hi, 1)

            def norm_work(stage, m, b):
                name, g0 = GAIN[stage]
                act.wait_ge(s_xnew, m + (XN[stage] + 1))
                if not (isinstance(m, int) and m < 2):
                    act.wait_ge(s_ss, m + 9 * SUM[stage])
                apart(m)
                A(sq[:, b, :], x[:, ds(m, 1), :].rearrange("p a t -> p (a t)"), ACT.Square).then_inc(s_sq, 1)
                A(xa_h[:, ds(m, 1), :].rearrange("p a t -> p (a t)"), x[:, ds(m, 1), :].rearrange("p a t -> p (a t)"),
                  ACT.Copy, scale=par(name, m + g0)).then_inc(s_xhi, 1)

            def root(k):
                act.wait_ge(s_var, k + 1)
                A(r_all[:, :], r_all[:, :], ACT.Sqrt).then_inc(s_rt, 1)

            act.wait_ge(s_miscd, 1)
            for m in range(DC):
                norm_work("init", m, m % 2)
            for slot in range(3):
                split_high(0, slot, DC)
            act.wait_ge(s_fw, 32)
            A(fw_h[:, :, :], fw[:, :, :], ACT.Copy).then_inc(s_fw, 1)
            root(0)
            for i in range(3):
                for j in range(4):
                    ahead(split_high, ph["qkv"], i, j, i == 2)
            act.wait_ge(s_fz, 1)
            A(fe[:, :], fz[:, :], ACT.Abs).then_inc(s_fe, 1)
            act.wait_ge(s_fe, 1)
            A(fe[:, :], fe[:, :], ACT.Exp, scale=-1.0).then_inc(s_fe, 1)
            act.wait_ge(s_fe, 2)
            A(fe[:, :], fe[:, :], ACT.Ln, bias=1.0).then_inc(s_fe, 1)
            for i in range(3):
                for j in range(4):
                    ahead(split_high, ph["gates"], i, j, i == 2)
                    c = 4 * i + j
                    if c < 8:
                        act.wait_ge(s_free, c + 1)
                        if c >= 2:
                            act.wait_ge(s_misc, 6 + c - 2)
                        A(sq[:, c % 2, :], qkv[:, c, :], ACT.Square).then_inc(s_qsq, 1)
                        act.wait_ge(s_hv, c + 1)
                        A(tmp[:, c % 2, :], tmp[:, c % 2, :], ACT.Sqrt).then_inc(s_hrt, 1)
                    else:
                        m = c - 8
                        act.wait_ge(s_ya, m + 1)
                        A(h_h[:, m, :], g4[:, m, :], ACT.Copy).then_inc(s_hhi, 1)
            for h in range(NH):
                act.wait_ge(s_cbp, h + 1)
                A(cb[:, h, :], bank[(h + 1) % 2][:, :], ACT.Copy).then_inc(s_cb, 1)
            for t in range(5):
                for kv in range(2):
                    n = P if t < 4 else TS
                    act.wait_ge(s_rows, R["kv"] + 2 * t + kv + 1)
                    if t == 4:
                        dst = s_row[:, kv, :]
                    elif kv:
                        dst = v_tok[:, t, :]
                    else:
                        if t >= 2:
                            act.wait_ge(s_rowdma, 16 * t)
                        dst = k_row[:, t % 2, :]
                    A(dst, bank[kv][0:n, :], ACT.Copy).then_inc(s_rowsd, 1)

            def pair_turn(i):
                if not isinstance(i, int):
                    act.wait_ge(s_po, i * 8)
                act.wait_ge(s_qk, 8)
                one = lambda ap: ap.rearrange("p a t -> p (a t)")
                A(q_s[:, :], one(qkv[:, ds(i, 1), 0:TP]), ACT.Copy, scale=HD ** -0.5).then_inc(s_qs, 1)
                A(k_s[:, :], one(qkv[:, ds(i + 4, 1), 0:TP]), ACT.Copy).then_inc(s_qs, 1)
                act.wait_ge(s_rowsd, R["kv"] + 10)
                A(v_s[:, :, :], v_tok[:, :, ds(i * P, P)], ACT.Copy).then_inc(s_qs, 1)

                def exps(w):
                    n = (w % 4 + 1) * P
                    act.wait_ge(s_sb, i * 8 + (w + 1))
                    A(sb[:, w % 4, 0:n], sb[:, w % 4, 0:n], ACT.Exp, bias=rmax[:, w % 4:w % 4 + 1],
                      accum_out=rsum[:, w % 4:w % 4 + 1]).then_inc(s_pe, 1)

                exps(0)
                for w in range(8):
                    if w < 7:
                        exps(w + 1)
                    n = (w % 4 + 1) * P
                    act.wait_ge(s_ptt, i * 8 + (w + 1))
                    if not (isinstance(i, int) and w < 2):
                        act.wait_ge(s_po, i * 8 + (w - 1))
                    A(pt[:, w % 2, 0:n], bank[w % 2][:, 0:n], ACT.Copy).then_inc(s_ptc, 1)
            pair_turn(0)
            with act.Fori(1, 4) as i:
                pair_turn(i)

            def batch_turn(b, first, scores=True):
                for p in range(PG):
                    if not (first and p < 4):
                        act.wait_ge(s_sp, b * PG + (p - 3))
                    act.wait_ge(s_tr, b * PG + (p + 1))
                    A(kt[:, p % 4, :], pb[p % 4], ACT.Copy).then_inc(s_kt, 1)
                    if p == 11 and not first:
                        exps_of(b)

            def exps_of(b):
                act.wait_ge(s_sm, b)
                if not (isinstance(b, int) and b < 2):
                    act.wait_ge(s_pvp, (b - 1) * PG)
                A(pr[:, :, :], sc[:, :, :], ACT.Exp).then_inc(s_p, 1)
            batch_turn(0, True)
            batch_turn(1, False)
            with act.Fori(2, NB) as b:
                batch_turn(b, False)
            exps_of(NB)
            act.wait_ge(s_pod, 4)
            for c in range(4):
                if c == 0:
                    act.wait_ge(s_oev, NB)
                A(h_h[:, 4 + c, :], qkv[:, c, :], ACT.Copy).then_inc(s_hhi, 1)

            act.wait_ge(s_pvp, NB * PG)
            for slot in range(3):
                split_high(ph["out"].slab0 // 4, slot, DC)

            def residual(phase, stage):
                def turn(i, last):
                    for j in range(4):
                        ahead(split_high, phase, i, j, last)
                        if stage in NORM and j % phase.per_group == phase.per_group - 1:
                            m = i * (4 // phase.per_group) + j // phase.per_group
                            norm_work(stage, m, (j // phase.per_group) % 2)
                turns(act, phase, turn, peel=1 if stage in NORM else 0)

            residual(ph["out"], "out")

            def rows_of(n, parts, group, dst):
                act.wait_ge(s_rows, group + 1)
                A(dst, bank[(group) % 2][0:parts, 0:n], ACT.Copy).then_inc(s_rowsd, 1)

            def ffn(l):
                root(SQ["out" if l == 0 else "pw2"])
                for half in range(2):
                    pu, pd = ph[f"up{l}{half}"], ph[f"down{l}{half}"]

                    def turn(i, last):
                        for j in range(4):
                            ahead(split_high, pu, i, j, last)
                            k = i * 2 + (l * FC + half * HALF[0] + j // 2)
                            b = j // 2
                            if j % 2 == 0:
                                act.wait_ge(s_cv, k + 1)
                                if not (isinstance(k, int) and k < 2):
                                    act.wait_ge(s_sr, k - 1)
                                A(sl[:, b, :], cv[:, b, :], ACT.Silu).then_inc(s_sl, 1)
                            else:
                                act.wait_ge(s_free, pu.group(i, j) + 1)
                                apart(i)
                                A(h_h[:, ds(i * 2 + b, 1), :].rearrange("p a t -> p (a t)"), tmp[:, b, :],
                                  ACT.Copy).then_inc(s_hhi, 1)
                    turns(act, pu, turn, peel=1 if l == 0 and half == 0 else 0)
                    if half == 1:
                        for q in range(6):
                            n = min(4, FC - 4 * q) * P
                            rows_of(n, FT, R[f"ffn{l}"] + q, f_row[0:FT, q * 512:q * 512 + n])
                    residual(pd, f"down{l}{half}")

            ffn(0)

            root(SQ["down01"])
            def turn(i, last):
                for j in range(4):
                    ahead(split_high, ph["pw1"], i, j, last)
                    if j % 2:
                        c, b = i * 2 + j // 2, j // 2
                        act.wait_ge(s_free, ph["pw1"].group(i, j) + 1)
                        apart(i)
                        A(sg[:, b, :], sg[:, b, :], ACT.Sigmoid, bias=par("b_pw1", c + DC)).then_inc(s_sig, 1)
            turns(act, ph["pw1"], turn)
            for q in range(2):
                rows_of(512, UT, R["conv_c"] + q, u_row[:, q * 512:q * 512 + 512])
            for m in range(DC):
                act.wait_ge(s_xc, m + 1)
                if m >= 2:
                    act.wait_ge(s_ss, 9 * SUM["var"] + m)
                A(sq[:, m % 2, :], yc[:, m, :], ACT.Square).then_inc(s_sq, 1)
            root(SQ["var"])
            for m in range(DC):
                act.wait_ge(s_ty, m + 1)
                if m >= 2:
                    act.wait_ge(s_hlo, HB["pw2"] + m - 1)
                A(tmp[:, m % 2, :], yc[:, m, :], ACT.Silu, scale=par("ln_g", m), bias=par("ln_b", m)).then_inc(s_s32, 1)
                act.wait_ge(s_s32, m + 1)
                A(h_h[:, m, :], tmp[:, m % 2, :], ACT.Copy).then_inc(s_hhi, 1)
            residual(ph["pw2"], "pw2")
            ffn(1)
            for t in range(5):
                n = P if t < 4 else TS
                for q in range(2):
                    act.wait_ge(s_rows, R["y"] + 2 * t + q + 1)
                    if t >= 2:
                        act.wait_ge(s_rowdma, 16 * (4 + t))
                    A(y_row[0:n, t % 2, q * 512:q * 512 + 512], bank[q][0:n, :], ACT.Copy).then_inc(s_rowsd, 1)

        @block.vector
        def _(dve):
            V = nc.vector
            st = Steps()
            flat = lambda ap: ap.rearrange("p a t -> p (a t)")

            def after():
                dve.wait_ge(s_dve, st.now())

            dve.wait_ge(s_misc, 1)
            V.tensor_copy(params[:, :], bank[0][:, 0:n_rows]).then_inc(s_miscd, 1)
            dve.wait_ge(s_miscd, 1)

            def clear_sum(n):
                if n:
                    dve.wait_ge(s_stat, n)
                V.memset(ssum[:, :], 0.0).then_inc(s_ss, 1)

            def norm_work(stage, m, b):
                name, g0 = GAIN[stage]
                dve.wait_ge(s_sq, m + (8 * SQ[stage] + 1))
                dve.wait_ge(s_ss, m + (9 * SUM[stage] + 1))
                V.tensor_tensor(ssum[:, :], ssum[:, :], sq[:, b, :], ALU.add).then_inc(s_ss, 1)
                dve.wait_ge(s_xhi, m + (8 * NORM[stage] + 1))
                V.scalar_tensor_tensor(flat(xa_l[:, ds(m, 1), :]), flat(x[:, ds(m, 1), :]), par(name, m + g0),
                                       flat(xa_h[:, ds(m, 1), :]).bitcast(F32), ALU.mult, ALU.subtract)\
                 .then_inc(s_xlo, 1)

            def inv_rms(k, n):
                dve.wait_ge(s_stat, n + 1)
                V.tensor_scalar(halves(r_all[:, :]), psum_s[:, :, 0:HT], 1.0 / D, EPS, ALU.mult, ALU.add)\
                 .then_inc(s_var, 1)
                dve.wait_ge(s_rt, k + 1)
                V.reciprocal(r_all[:, :], r_all[:, :]).then_inc(s_r, 1)
                dve.wait_ge(s_r, k + 1)

            def scaled(dst, s, b):
                dve.wait_ge(s_slab, s + 1)
                V.tensor_tensor(halves(dst), gview(b), halves(r_all[:, :]), ALU.mult).then_inc(s_free, 1)

            clear_sum(0)
            for m in range(DC):
                dve.wait_ge(s_tp, m + 1)
                V.tensor_copy(x[:, m, 0:TP], pair[m % 2][:, 0, :]).then_inc(s_dve, 1)
                st.tick()
                V.tensor_copy(x[:, m, TP:T], pair[m % 2][:, 1, 0:TS]).then_inc(s_xnew, 1)
                dve.wait_ge(s_xnew, m + 1)
                after()
                norm_work("init", m, m % 2)
            dve.wait_ge(s_misc, 2)
            V.tensor_copy(ext_a[:, :, :, 0:CA - 1],
                          bank[1][:, 0:8 * NB].rearrange("p (c b t) -> p c b t", c=4, b=NB)).then_inc(s_miscd, 1)
            inv_rms(0, 0)
            for g in range(4):
                scaled(qkv[:, g, :], g, g % 2)
            dve.wait_ge(s_misc, 3)
            V.tensor_copy(lf_k[:, :, :].rearrange("p (s h) g -> p s (h g)", s=2), psum_s[:, :, :]).then_inc(s_miscd, 1)
            V.memset(suf[:, :, PG - 1:PG], 0.0).then_inc(s_dve, 1)
            st.tick()
            dve.wait_ge(s_miscd, 3)
            for p in range(PG - 2, -1, -1):
                after()
                V.tensor_tensor(suf[:, :, p:p + 1], suf[:, :, p + 1:p + 2], lf_k[:, :, p + 1:p + 2], ALU.add)\
                 .then_inc(s_dve if p else s_suf, 1)
                if p:
                    st.tick()
            for g in range(4, 8):
                scaled(qkv[:, g, :], g, g % 2)
            dve.wait_ge(s_misc, 4)
            for half in range(2):
                V.tensor_copy(dk[:, :, :, 4 * half:4 * half + 4].rearrange("p b g h -> p h (b g)"),
                              psum_s[:, half, :].rearrange("p (h g) -> p h g", h=4)).then_inc(s_miscd, 1)
            V.memset(seg[:, :], 1.0).then_inc(s_dve, 1)
            st.tick()
            after()
            V.memset(seg[:, TP:T].rearrange("p (b t) -> p b t", t=NT)[:, :, 0:1], 0.0).then_inc(s_dve, 1)
            st.tick()
            for g in range(8, 12):
                scaled(qkv[:, g, :], g, g % 2)
            dve.wait_ge(s_misc, 5)
            V.tensor_tensor(halves(fz[:, :]), psum_s[0:NH, :, 0:HT], halves(r_all[0:NH, :]), ALU.mult)\
             .then_inc(s_miscd, 1)
            dve.wait_ge(s_miscd, 6)
            V.tensor_scalar(fz[:, :], fz[:, :], b_f, None, ALU.add).then_inc(s_fz, 1)
            dve.wait_ge(s_fe, 3)
            V.scalar_tensor_tensor(logf[:, :], fz[:, :], 0.0, fe[:, :], ALU.min, ALU.subtract).then_inc(s_dve, 1)
            st.tick()
            after()
            V.tensor_tensor_scan(cum[:, :], seg[:, :], logf[:, :], 0.0, ALU.mult, ALU.add).then_inc(s_cum, 1)
            dve.wait_ge(s_cum, 1)
            V.tensor_tensor(cnm[:, :, :], ident[0:NH, 0:NH].unsqueeze(2).to_broadcast([NH, NH, TS]),
                            cum[:, TP:T].unsqueeze(1).to_broadcast([NH, NH, TS]), ALU.mult).then_inc(s_cum, 1)

            def head_norm(c):
                dve.wait_ge(s_misc, 6 + c)
                if c >= 2:
                    dve.wait_ge(s_qk, c - 1)
                V.tensor_scalar(halves(tmp[:, c % 2, :]), psum_s[:, :, 0:HT], 1.0 / HD, EPS, ALU.mult, ALU.add)\
                 .then_inc(s_hv, 1)
                dve.wait_ge(s_hrt, c + 1)
                V.reciprocal(tmp[:, c % 2, :], tmp[:, c % 2, :]).then_inc(s_dve, 1)
                st.tick()
                after()
                V.scalar_tensor_tensor(qkv[:, c, :], qkv[:, c, :], params[:, prow["qk"][0] + c // 4:prow["qk"][0] + c // 4 + 1],
                                       tmp[:, c % 2, :], ALU.mult, ALU.mult).then_inc(s_qk, 1)

            for c in range(4):
                scaled(u4[:, c, :], 12 + c, c % 2)
                head_norm(c)
            for c in range(4):
                scaled(ssum[:, :], 16 + c, c % 2)
                dve.wait_ge(s_free, 17 + c)
                V.tensor_tensor(u4[:, c, :], ssum[:, :], u4[:, c, :], ALU.mult).then_inc(s_dve, 1)
                st.tick()
                after()
                V.tensor_copy(ext_a[:, c, :, CA - 1:], u4[:, c, TP:T].rearrange("p (b t) -> p b t", t=NT))\
                 .then_inc(s_dve, 1)
                st.tick()
                after()
                for tap in range(CA - 1, -1, -1):
                    k = CA - 1 - tap
                    w = params[:, prow["conv_a"][0] + tap * 4 + c:prow["conv_a"][0] + tap * 4 + c + 1]
                    yp, ys = g4[:, c, k:TP], g4[:, c, TP:T].rearrange("p (b t) -> p b t", t=NT)
                    es = ext_a[:, c, :, tap:tap + NT]
                    if k == 0:
                        V.tensor_scalar(yp, u4[:, c, 0:TP], w, None, ALU.mult).then_inc(s_dve, 1)
                        V.tensor_scalar(ys, es, w, None, ALU.mult).then_inc(s_dve, 1)
                    else:
                        V.scalar_tensor_tensor(yp, u4[:, c, 0:TP - k], w, yp, ALU.mult, ALU.add).then_inc(s_dve, 1)
                        V.scalar_tensor_tensor(ys, es, w, ys, ALU.mult, ALU.add).then_inc(s_dve, 1)
                    st.tick()
                    st.tick()
                    after()
                head_norm(4 + c)
            V.tensor_copy(tail_a[:, :, 0:2], u4[:, :, TP - 2:TP]).then_inc(s_tail, 1)
            V.tensor_copy(tail_a[:, :, 2:FT].rearrange("p c (b t) -> p c b t", b=NB), ext_a[:, :, :, NT:])\
             .then_inc(s_tail, 1)
            for c in range(4):
                scaled(ssum[:, :], 20 + c, c % 2)
                dve.wait_ge(s_free, 21 + c)
                V.tensor_tensor(g4[:, c, :], ssum[:, :], g4[:, c, :], ALU.mult).then_inc(s_ya, 1)
                dve.wait_ge(s_hhi, c + 1)
                V.tensor_tensor(h_l[:, c, :], g4[:, c, :], h_h[:, c, :].bitcast(F32), ALU.subtract).then_inc(s_hlo, 1)
                if c == 0:
                    dve.wait_ge(s_misc, 14)
                    V.tensor_copy(cq, bank[0][:, 0:32]).then_inc(s_dve, 1)
                    V.tensor_copy(cns, bank[0][0:TS, 32:40]).then_inc(s_dve, 1)
                    V.tensor_copy(lf_row[:, 0:4, :], bank[0][:, 64:96].rearrange("p (t h) -> p t h", h=NH))\
                     .then_inc(s_dve, 1)
                    for _ in range(3):
                        st.tick()
                    V.tensor_copy(lf_row[0:TS, 4, :], bank[0][0:TS, 96:104]).then_inc(s_miscd, 1)
                if c == 1:
                    dve.wait_ge(s_misc, 15)
                    V.tensor_copy(cn_all[:, :, :, :].rearrange("p h b t -> p (h b t)"), bank[1][:, 0:NH * TS])\
                     .then_inc(s_miscd, 1)
            dve.wait_ge(s_misc, 16)
            V.tensor_copy(a_out[:, :], bank[0][0:FT, :]).then_inc(s_miscd, 1)
            for h in range(NH):
                if h >= 2:
                    dve.wait_ge(s_cbp, h - 1)
                V.tensor_scalar(cmask[:, h % 2, :], cum[:, 0:TP], ident[0:NH, h:h + 1], None, ALU.mult).then_inc(s_cm, 1)
            dve.wait_ge(s_qk, 8)
            for c in range(4):
                for hh in range(2):
                    V.tensor_scalar(q_diag[HD * hh:HD * hh + HD, c, :, NT * hh:NT * hh + NT],
                                    qkv[HD * hh:HD * hh + HD, c, TP:T].rearrange("p (b t) -> p b t", t=NT),
                                    HD ** -0.5, None, ALU.mult).then_inc(s_dve, 1)
                    st.tick()
            after()
            V.tensor_tensor(nbias[:, :, :, :], nbias[:, :, :, :],
                            cns.unsqueeze(1).unsqueeze(3).to_broadcast([TS, NB, NH, NT]), ALU.subtract)\
             .then_inc(s_dve, 1)
            st.tick()
            after()
            def attended(i):
                dve.wait_ge(s_po, i * 8 + 8)
                V.tensor_scalar(flat(qkv[:, ds(i, 1), 0:TP]), psum_s[:, 0, :], 1.0, None, ALU.mult).then_inc(s_pod, 1)

            def pair_turn(i):
                def bias(w):
                    hh, qb = w // 4, w % 4
                    n = (qb + 1) * P
                    dve.wait_ge(s_s, i * 8 + (w + 1))
                    if w == 0:
                        dve.wait_ge(s_cb, NH)
                    if not (isinstance(i, int) and w < 4):
                        dve.wait_ge(s_ptt, i * 8 + (w - 3))
                    V.scalar_tensor_tensor(sb[:, w % 4, 0:n], pb[w % 4][:, 0:n], small[:, ds(i * 2 + (160 + qb * NH + hh), 1)],
                                           flat(cb[:, ds(i * 2 + hh, 1), 0:n]), ALU.add, ALU.subtract).then_inc(s_sbr, 1)
                    dve.wait_ge(s_sbr, i * 8 + (w + 1))
                    V.tensor_tensor(sb[:, w % 4, n - P:n], sb[:, w % 4, n - P:n], causal[:, :], ALU.add).then_inc(s_dve, 1)
                    st.tick()
                    after()
                    V.tensor_reduce(rmax[:, w % 4:w % 4 + 1], sb[:, w % 4, 0:n], AX.X, ALU.max, negate=True)\
                     .then_inc(s_sb, 1)

                def norm(w):
                    n = (w % 4 + 1) * P
                    dve.wait_ge(s_pe, i * 8 + (w + 1))
                    V.reciprocal(rinv[:, w % 4:w % 4 + 1], rsum[:, w % 4:w % 4 + 1]).then_inc(s_dve, 1)
                    st.tick()
                    after()
                    V.tensor_scalar(sb[:, w % 4, 0:n], sb[:, w % 4, 0:n], rinv[:, w % 4:w % 4 + 1], None, ALU.mult)\
                     .then_inc(s_pn, 1)
                for w in range(9):
                    if w < 8:
                        bias(w)
                    if w == 1 and not isinstance(i, int):
                        attended(i - 1)
                    if w >= 1:
                        norm(w - 1)
            pair_turn(0)
            with st.loop(dve, 1, 4, 16) as i:
                pair_turn(i)
            attended(3)

            wide = lambda ap, n: ap.unsqueeze(1).to_broadcast([P, n, 32])

            def logits(b):
                dve.wait_ge(s_sc, b + 1)
                V.tensor_tensor(sc[:, 0:PG, :].rearrange("p g (h q) -> p (g h) q", q=NT),
                                psum_s[:, 0, :].rearrange("p (g q) -> p g q", q=NT),
                                dk[:, ds(b, 1), :, :].rearrange("p b g h -> p (b g h)").unsqueeze(2)
                                .to_broadcast([P, PG * NH, NT]), ALU.add).then_inc(s_dve, 1)
                st.tick()
                V.tensor_tensor(sc[0:TS, PG, :], psum_s[0:TS, 1, 0:32],
                                nbias[:, ds(b, 1), :, :].rearrange("p b h q -> p (b h q)"), ALU.add).then_inc(s_sev, 1)
                dve.wait_ge(s_sev, b + 1)
                after()
                V.tensor_tensor(sc[:, :, :].rearrange("p g (h q) -> p g h q", q=NT),
                                sc[:, :, :].rearrange("p g (h q) -> p g h q", q=NT),
                                cn_all[:, :, ds(b, 1), :].rearrange("p h b t -> p (h b) t").unsqueeze(1)
                                .to_broadcast([P, PG + 1, NH, NT]), ALU.add).then_inc(s_dve, 1)
                st.tick()
                after()
                V.tensor_reduce(m1, sc[:, :, :].rearrange("p g x -> p x g"), AX.X, ALU.max).then_inc(s_m1, 1)

            def shift(b):
                dve.wait_ge(s_mt, b + 1)
                V.tensor_reduce(gmax, bank[1][0:32, 0:P], AX.X, ALU.max).then_inc(s_dve, 1)
                st.tick()
                after()
                V.tensor_scalar(diag, ident[0:32, 0:32], gmax, None, ALU.mult).then_inc(s_dg, 1)
                dve.wait_ge(s_mb, b + 1)
                V.tensor_tensor(sc[:, :, :], sc[:, :, :], wide(bank[1][:, P:P + 32], PG + 1), ALU.subtract)\
                 .then_inc(s_sm, 1)
                dve.wait_ge(s_p, b + 1)
                V.tensor_reduce(p_sum, pr[:, :, :].rearrange("p g x -> p x g"), AX.X, ALU.add).then_inc(s_lp, 1)
                dve.wait_ge(s_l, b + 1)
                V.reciprocal(rec, bank[1][:, 192:224]).then_inc(s_rec, 1)
                dve.wait_ge(s_rec, b + 1)

            def values(b):
                dve.wait_ge(s_pvp, b * PG + PG)
                for hh in range(2):
                    rows = slice(HD * hh, HD * hh + HD)
                    V.tensor_tensor(qkv[rows, 0:4, ds(b * NT + TP, NT)],
                                    bank[0][rows, 0:32].rearrange("p (c x) -> p c x", c=4)[:, :, NT * hh:NT * hh + NT],
                                    rec[rows, :].rearrange("p (c x) -> p c x", c=4)[:, :, NT * hh:NT * hh + NT],
                                    ALU.mult).then_inc(s_oev if hh else s_dve, 1)
                    if not hh:
                        st.tick()
            dve.wait_ge(s_aout, 32)
            logits(0)
            with st.loop(dve, 0, NB - 1, 4) as b0:
                shift(b0)
                logits(b0 + 1)
                values(b0)
            shift(NB - 1)
            values(NB - 1)
            after()
            for c in range(4):
                dve.wait_ge(s_hhi, 5 + c)
                V.tensor_tensor(h_l[:, 4 + c, :], qkv[:, c, :], h_h[:, 4 + c, :].bitcast(F32), ALU.subtract)\
                 .then_inc(s_hlo, 1)

            def residual(phase, stage):
                if stage in NORM:
                    clear_sum(SUM[stage])
                per_turn = 4 // phase.per_group
                with dve.Fori(0, phase.turns) as i:
                    for q in range(per_turn):
                        m = i * per_turn + q
                        dve.wait_ge(s_slab, phase.slab(i, (q + 1) * phase.per_group - 1) + 1)
                        V.tensor_tensor(halves(flat(x[:, ds(m, 1), :])), gview(q % 2), halves(flat(x[:, ds(m, 1), :])),
                                        ALU.add).then_inc(s_xnew, 1)
                        dve.wait_ge(s_xnew, m + (XN[stage] + 1))
                        if stage in NORM:
                            norm_work(stage, m, q % 2)

            residual(ph["out"], "out")

            def ffn(l):
                dve.wait_ge(s_fst, 1 + 5 * l)
                V.tensor_copy(ext_f[:, :, :, 0:CF - 1].rearrange("p c b t -> p c b t"),
                              bank[0][:, 0:FC * 2 * NB].rearrange("p (c b t) -> p c b t", c=FC, b=NB)).then_inc(s_fstd, 1)
                dve.wait_ge(s_fstd, 1 + 5 * l)
                inv_rms(SQ["out" if l == 0 else "pw2"], SUM["out" if l == 0 else "pw2"])
                for half in range(2):
                    pu, pd = ph[f"up{l}{half}"], ph[f"down{l}{half}"]
                    with st.loop(dve, 0, pu.turns, 2 * 6) as i:
                        for b in range(2):
                            kc = i * 2 + (half * HALF[0] + b)
                            k = i * 2 + (half * HALF[0] + b + HB[f"up{l}"])
                            e = lambda lo, hi: ext_f[:, ds(kc, 1), :, lo:hi].rearrange("p a b t -> p (a b) t")
                            scaled(gate[:, b, :], pu.slab(i, 2 * b), 0)
                            dve.wait_ge(s_free, pu.group(i, 2 * b) + 1)
                            V.tensor_copy(e(CF - 1, CF - 1 + NT), gate[:, b, TP:T].rearrange("p (b t) -> p b t", t=NT))\
                             .then_inc(s_dve, 1)
                            st.tick()
                            V.tensor_copy(flat(tail_f[:, ds(kc, 1), 0:2]), gate[:, b, TP - 2:TP]).then_inc(s_tail, 1)
                            after()
                            ys = cv[:, b, TP:T].rearrange("p (b t) -> p b t", t=NT)
                            for tap in range(CF - 1, -1, -1):
                                n = CF - 1 - tap
                                w = par("conv_f", kc + (l * CF * FC + tap * FC))
                                yp = cv[:, b, n:TP]
                                if n == 0:
                                    V.tensor_scalar(yp, gate[:, b, 0:TP], w, None, ALU.mult).then_inc(s_dve, 1)
                                    st.tick()
                                    V.tensor_scalar(ys, e(tap, tap + NT), w, None, ALU.mult).then_inc(s_dve, 1)
                                    st.tick()
                                    after()
                                    continue
                                V.scalar_tensor_tensor(yp, gate[:, b, 0:TP - n], w, yp, ALU.mult, ALU.add)\
                                 .then_inc(s_dve, 1)
                                st.tick()
                                if n < CF - 1:
                                    V.scalar_tensor_tensor(ys, e(tap, tap + NT), w, ys, ALU.mult, ALU.add)\
                                     .then_inc(s_dve, 1)
                                    st.tick()
                                    after()
                                else:
                                    V.scalar_tensor_tensor(ys, e(tap, tap + NT), w, ys, ALU.mult, ALU.add)\
                                     .then_inc(s_cv, 1)
                            dve.wait_ge(s_slab, pu.slab(i, 2 * b + 1) + 1)
                            dve.wait_ge(s_sr, i * 2 + (l * FC + half * HALF[0] + b + 1))
                            V.tensor_tensor(halves(tmp[:, b, :]), gview(1), halves(sr[:, b, :]), ALU.mult).then_inc(s_free, 1)
                            dve.wait_ge(s_hhi, k + 1)
                            V.tensor_tensor(flat(h_l[:, ds(i * 2 + b, 1), :]), tmp[:, b, :],
                                            flat(h_h[:, ds(i * 2 + b, 1), :]).bitcast(F32), ALU.subtract).then_inc(s_hlo, 1)
                    if half == 1:
                        V.tensor_copy(tail_f[:, :, 2:FT].rearrange("p c (b t) -> p c b t", b=NB), ext_f[:, :, :, NT:])\
                         .then_inc(s_tail, 1)
                    residual(pd, f"down{l}{half}")

            ffn(0)

            for q in range(4):
                dve.wait_ge(s_fst, 2 + q)
                V.tensor_copy(ext_c[:, 2 * q:2 * q + 2, :, 0:CC - 1],
                              bank[q % 2][:, 0:480].rearrange("p (c b t) -> p c b t", c=2, b=NB)).then_inc(s_fstd, 1)
            inv_rms(SQ["down01"], SUM["down01"])
            clear_sum(SUM["mean"])
            dve.wait_ge(s_out, 16 * n_out[1])
            taps = params[:, prow["conv_c"][0]:prow["conv_c"][0] + CC * DC].rearrange("p (k c) -> p c k", c=DC)
            with st.loop(dve, 0, ph["pw1"].turns, 2 * (CC + 7)) as i:
                for b in range(2):
                    c = i * 2 + b
                    ue = lambda lo, hi: ext_c[:, ds(c, 1), :, lo:hi].rearrange("p a b t -> p (a b) t")
                    scaled(ua[:, b, :], ph["pw1"].slab(i, 2 * b), 0)
                    dve.wait_ge(s_slab, ph["pw1"].slab(i, 2 * b + 1) + 1)
                    V.tensor_tensor(halves(sg[:, b, :]), gview(1), halves(r_all[:, :]), ALU.mult).then_inc(s_free, 1)
                    dve.wait_ge(s_sig, c + 1)
                    V.scalar_tensor_tensor(u[:, b, :], ua[:, b, :], par("b_pw1", c), sg[:, b, :], ALU.add, ALU.mult)\
                     .then_inc(s_u, 1)
                    dve.wait_ge(s_u, c + 1)
                    V.tensor_copy(flat(tail_c[:, ds(c, 1), :]), u[:, b, T - UT:T]).then_inc(s_ux, 1)
                    V.tensor_copy(ue(CC - 1, CC - 1 + NT), u[:, b, TP:T].rearrange("p (b t) -> p b t", t=NT))\
                     .then_inc(s_dve, 1)
                    st.tick()
                    after()
                    for t in range(NT):
                        V.tensor_tensor(prod[:, :, :].rearrange("p (b t) k -> p b t k", t=NT)[:, :, t, :],
                                        ue(t, t + CC), taps[:, ds(c, 1), :].to_broadcast([P, NB, CC]), ALU.mult)\
                         .then_inc(s_dve, 1)
                        st.tick()
                    after()
                    V.tensor_reduce(flat(yc[:, ds(c, 1), TP:T]), prod[:, :, :], AX.X, ALU.add).then_inc(s_dve, 1)
                    st.tick()
                    after()
                    V.tensor_scalar(flat(yc[:, ds(c, 1), TP:T]), flat(yc[:, ds(c, 1), TP:T]), par("conv_cb", c), None,
                                    ALU.add).then_inc(s_dve, 1)
                    st.tick()
                    for tap in range(CC - 1, -1, -1):
                        n = CC - 1 - tap
                        w = par("conv_c", c + tap * DC)
                        yp = flat(yc[:, ds(c, 1), n:TP])
                        if n == 0:
                            V.tensor_scalar(yp, u[:, b, 0:TP], w, par("conv_cb", c), ALU.mult, ALU.add).then_inc(s_dve, 1)
                        else:
                            V.scalar_tensor_tensor(yp, u[:, b, 0:TP - n], w, yp, ALU.mult, ALU.add).then_inc(s_dve, 1)
                        st.tick()
                        after()
                    dve.wait_ge(s_ss, c + (9 * SUM["mean"] + 1))
                    V.tensor_tensor(ssum[:, :], ssum[:, :], flat(yc[:, ds(c, 1), :]), ALU.add).then_inc(s_ss, 1)
            dve.wait_ge(s_stat, SUM["mean"] + 1)
            V.tensor_scalar(halves(r_all[:, :]), psum_s[:, :, 0:HT], 1.0 / D, None, ALU.mult).then_inc(s_mu, 1)
            dve.wait_ge(s_mu, 1)
            clear_sum(SUM["var"])
            def add_squares(m):
                dve.wait_ge(s_sq, 8 * SQ["var"] + m + 1)
                dve.wait_ge(s_ss, 9 * SUM["var"] + m + 1)
                V.tensor_tensor(ssum[:, :], ssum[:, :], sq[:, m % 2, :], ALU.add).then_inc(s_ss, 1)
            for m in range(DC):
                V.tensor_tensor(yc[:, m, :], yc[:, m, :], r_all[:, :], ALU.subtract).then_inc(s_xc, 1)
                if m:
                    add_squares(m - 1)
            add_squares(DC - 1)
            inv_rms(SQ["var"], SUM["var"])
            for m in range(DC + 1):
                if m < DC:
                    dve.wait_ge(s_xc, m + 1)
                    V.tensor_tensor(yc[:, m, :], yc[:, m, :], r_all[:, :], ALU.mult).then_inc(s_ty, 1)
                if m:
                    dve.wait_ge(s_hhi, HB["pw2"] + m)
                    V.tensor_tensor(h_l[:, m - 1, :], tmp[:, (m - 1) % 2, :], h_h[:, m - 1, :].bitcast(F32), ALU.subtract)\
                     .then_inc(s_hlo, 1)
            residual(ph["pw2"], "pw2")
            ffn(1)

        @block.tensor
        def _(pe):
            mm, tr = nc.tensor.matmul, nc.tensor.transpose
            xa = lambda t: (xa_h[:, t, :], xa_l[:, t, :])
            hid = lambda t: (h_h[:, t, :], h_l[:, t, :])

            def slab(phase, i, j, moving, ready=None):
                first, last = j % phase.per_group == 0, j % phase.per_group == phase.per_group - 1
                s, g = phase.slab(i, j), phase.group(i, j)
                pe.wait_ge(s_lo, s + 1)
                if first:
                    bank_free(phase, i, j // phase.per_group, g)
                out = pair[(j // phase.per_group) % 2]
                for t in range(phase.tiles):
                    k = t + (0 if first else phase.tiles)
                    if ready:
                        ready(k)
                    hi, lo = moving(k)
                    wh, wl = w_h[:, j, t * P:(t + 1) * P], w_l[:, j, t * P:(t + 1) * P]
                    for n, (w, v) in enumerate(((wh, hi), (wh, lo), (wl, hi))):
                        for half in range(2):
                            ins = mm(out[:, half, 0:HT], w, v[:, half * HT:(half + 1) * HT],
                                     start=first and t == 0 and n == 0,
                                     stop=last and t == phase.tiles - 1 and n == 2)
                ins.then_inc(s_slab, 1)

            def bank_free(phase, i, q, g):
                if isinstance(i, int) and i == 0 and q < 2:
                    if phase is not order[0]:
                        before = order[order.index(phase) - 1]
                        pe.wait_ge(s_xnew if before.residual else s_free, before.group1 - 1 + q)
                else:
                    pe.wait_ge(s_xnew if phase.residual else s_free, g - 1)

            def sum_channels():
                for half in range(2):
                    ins = mm(psum_s[:, half, 0:HT], ones[:, :], ssum[:, half * HT:(half + 1) * HT], start=True, stop=True)
                ins.then_inc(s_stat, 1)

            pe.wait_ge(s_cst, 15)
            pe.wait_ge(s_prm, 16 * (4 + sum(len(row_blocks(*v)) for name, v in prow.items() if name != "qk")))
            for blk in range(4):
                n = min(P, n_rows - blk * P)
                ins = tr(bank[0][:, blk * P:blk * P + n], p_rows[0:n, blk, :], ident[0:n, 0:n])
            ins.then_inc(s_misc, 1)
            pe.wait_ge(s_xld, 16 * 5)
            for m in range(DC):
                if m >= 2:
                    pe.wait_ge(s_xnew, m - 1)
                for t in range(4):
                    tr(pair[m % 2][:, 0, t * P:(t + 1) * P], x_rows[:, t, m * P:(m + 1) * P], ident[:, :])
                tr(pair[m % 2][:, 1, 0:TS], x_rows[0:TS, 4, m * P:(m + 1) * P], ident[0:TS, 0:TS]).then_inc(s_tp, 1)
            pe.wait_ge(s_st, 16)
            for c in range(4):
                ins = tr(bank[1][:, c * 2 * NB:(c + 1) * 2 * NB], a_row[:, c * P:(c + 1) * P], ident[0:2 * NB, 0:2 * NB])
            ins.then_inc(s_misc, 1)
            pe.wait_ge(s_xnew, DC)

            p = ph["qkv"]
            for i in range(3):
                for j in range(4):
                    slab(p, i, j, xa, (lambda k: pe.wait_ge(s_xlo, k + 1)) if i == j == 0 else None)
                    if i == j == 0:
                        pe.wait_ge(s_ss, 9)
                        sum_channels()
                if i == 0:
                    pe.wait_ge(s_lf, 16)
                    pe.wait_ge(s_var, 1)
                    for h in range(NH):
                        ins = tr(psum_s[:, h // 4, (h % 4) * P:(h % 4 + 1) * P],
                                 lf_pg[:, :].rearrange("p (k h) -> p h k", h=NH)[:, h, :], ident[:, :])
                    ins.then_inc(s_misc, 1)
                if i == 1:
                    pe.wait_ge(s_miscd, 3)
                    pe.wait_ge(s_suf, 1)
                    lf2, suf2 = (ap[:, :, :].rearrange("p h g -> p (h g)") for ap in (lf_k, suf))
                    for half in range(2):
                        at = slice(half * 512, half * 512 + 512)
                        mm(psum_s[:, half, :], later[:, :], lf2[:, at], start=True, stop=False)
                        ins = mm(psum_s[:, half, :], ones[:, :], suf2[:, at], start=False, stop=True)
                    ins.then_inc(s_misc, 1)
            pe.wait_ge(s_fw, 34)
            pe.wait_ge(s_miscd, 5)
            for t in range(DC):
                for n, (w, v) in enumerate(((fw_h, xa_h), (fw_h, xa_l), (fw_l, xa_h))):
                    for half in range(2):
                        ins = mm(psum_s[0:NH, half, 0:HT], w[:, t, :], v[:, t, half * HT:(half + 1) * HT],
                                 start=t == 0 and n == 0, stop=t == DC - 1 and n == 2)
            ins.then_inc(s_misc, 1)
            p = ph["gates"]
            for i in range(3):
                for j in range(4):
                    slab(p, i, j, xa)
                    c = 4 * i + j
                    if c < 8:
                        pe.wait_ge(s_qsq, c + 1)
                        if c:
                            pe.wait_ge(s_hv, c)
                        else:
                            pe.wait_ge(s_miscd, 6)
                        for half in range(2):
                            ins = mm(psum_s[:, half, 0:HT], head_ones[:, :], sq[:, c % 2, half * HT:(half + 1) * HT],
                                     start=True, stop=True)
                        ins.then_inc(s_misc, 1)
                    if c == 8:
                        pe.wait_ge(s_cum, 1)
                        pe.wait_ge(s_miscd, 2)
                        for t in range(4):
                            tr(bank[0][:, t * NH:(t + 1) * NH], cum[:, t * P:(t + 1) * P], ident[0:NH, 0:NH])
                            tr(bank[0][:, 64 + t * NH:64 + (t + 1) * NH], logf[:, t * P:(t + 1) * P], ident[0:NH, 0:NH])
                        tr(bank[0][0:TS, 32:40], cum[:, TP:T], ident[0:NH, 0:NH])
                        tr(bank[0][0:TS, 96:104], logf[:, TP:T], ident[0:NH, 0:NH]).then_inc(s_misc, 1)
                    if c == 9:
                        pe.wait_ge(s_cum, 2)
                        mm(bank[1][:, 0:NH * TS], ones[0:NH, :], cnm[:, :, :].rearrange("p h t -> p (h t)"),
                           start=True, stop=True).then_inc(s_misc, 1)
            pe.wait_ge(s_tail, 2)
            pe.wait_ge(s_miscd, 7)
            for c in range(4):
                ins = tr(bank[0][0:FT, c * P:(c + 1) * P], tail_a[:, c, :], ident[:, :])
            ins.then_inc(s_misc, 1)
            for h in range(NH):
                pe.wait_ge(s_cm, h + 1)
                pe.wait_ge(s_miscd, 8 if h == 0 else 9)
                if h >= 2:
                    pe.wait_ge(s_cb, h - 1)
                mm(bank[(h + 1) % 2][:, :], ones[0:NH, :], cmask[:, h % 2, :], start=True, stop=True).then_inc(s_cbp, 1)
            pe.wait_ge(s_qk, 8)
            pe.wait_ge(s_cb, NH)
            for t in range(5):
                for kv in range(2):
                    n = P if t < 4 else TS
                    if t:
                        pe.wait_ge(s_rowsd, 2 * t + kv - 1)
                    for c in range(4):
                        ins = tr(bank[kv][0:n, c * P:(c + 1) * P], qkv[:, 4 + 4 * kv + c, t * P:t * P + n], ident[:, :])
                    ins.then_inc(s_rows, 1)

            pe.wait_ge(s_rowsd, R["kv"] + 10)
            pe.wait_ge(s_free, ph["gates"].group1)

            def pair_turn(i):
                def score(w):
                    hh, qb = w // 4, w % 4
                    n = (qb + 1) * P
                    rows = slice(HD * hh, HD * hh + HD)
                    if not (isinstance(i, int) and w < 4):
                        pe.wait_ge(s_sbr, i * 8 + (w - 3))
                    mm(pb[w % 4][:, 0:n], q_s[rows, qb * P:(qb + 1) * P], k_s[rows, 0:n], start=True, stop=True)\
                        .then_inc(s_s, 1)
                pe.wait_ge(s_qs, i * 3 + 3)
                score(0)
                score(1)
                for w in range(8):
                    if w < 6:
                        score(w + 2)
                    hh, qb = w // 4, w % 4
                    pe.wait_ge(s_pn, i * 8 + (w + 1))
                    if not (isinstance(i, int) and w < 2):
                        pe.wait_ge(s_ptc, i * 8 + (w - 1))
                    for kb in range(qb + 1):
                        ins = tr(bank[w % 2][:, kb * P:(kb + 1) * P], sb[:, w % 4, kb * P:(kb + 1) * P], ident[:, :])
                    ins.then_inc(s_ptt, 1)
                    pe.wait_ge(s_ptc, i * 8 + (w + 1))
                    if w == 0 and not isinstance(i, int):
                        pe.wait_ge(s_pod, i)
                    for kb in range(qb + 1):
                        ins = mm(psum_s[HD * hh:HD * hh + HD, 0, qb * P:(qb + 1) * P], v_s[:, kb, HD * hh:HD * hh + HD],
                                 pt[:, w % 2, kb * P:(kb + 1) * P], start=kb == 0, stop=kb == qb)
                    ins.then_inc(s_po, 1)
            pair_turn(0)
            with pe.Fori(1, 4) as i:
                pair_turn(i)

            pe.wait_ge(s_pod, 4)

            def turn_page(b, p, first):
                pe.wait_ge(s_k[p % KS], b * 32 + 16 * (p // KS + 1))
                if not (first and p < 4):
                    pe.wait_ge(s_kt, b * PG + (p - 3))
                for c in range(4):
                    ins = tr(pb[p % 4][:, c * P:(c + 1) * P], k_pg[:, p % KS, c * P:(c + 1) * P], ident[:, :])
                ins.then_inc(s_tr, 1)

            def score_page(b, p):
                pe.wait_ge(s_kt, b * PG + (p + 1))
                for c in range(4):
                    ins = mm(psum_s[:, 0, p * 32 + c * 8:p * 32 + c * 8 + 8], kt[:, p % 4, c * P:(c + 1) * P],
                             q_diag[:, c, ds(b, 1), :].rearrange("p a x -> p (a x)"), start=True, stop=True)
                ins.then_inc(s_sp, 1)

            def max_turn(b):
                pe.wait_ge(s_m1, b + 1)
                tr(bank[1][0:32, 0:P], m1, ident[:, :]).then_inc(s_mt, 1)

            def max_spread(b):
                pe.wait_ge(s_dg, b + 1)
                mm(bank[1][:, P:P + 32], ones[0:32, :], diag, start=True, stop=True).then_inc(s_mb, 1)

            def value(b):
                pe.wait_ge(s_lp, b + 1)
                mm(bank[1][:, 192:224], ones[:, :], p_sum, start=True, stop=True).then_inc(s_l, 1)
                if not (isinstance(b, int) and b == 0):
                    pe.wait_ge(s_oev, b)
                for c in range(4):
                    mm(bank[0][:, c * 8:c * 8 + 8], s_row[:, 1, c * P:(c + 1) * P], pr[0:TS, PG, c * 8:c * 8 + 8],
                       start=c == 0, stop=False, skip_group_check=True)
                for p in range(PG):
                    pe.wait_ge(s_v[p], b * 16 + 16)
                    for c in range(4):
                        ins = mm(bank[0][:, c * 8:c * 8 + 8], v_pg[:, p, c * P:(c + 1) * P], pr[:, p, c * 8:c * 8 + 8],
                                 start=False, stop=p == PG - 1, skip_group_check=True)
                    ins.then_inc(s_pvp, 1)

            def scores(b, first):
                for p in range(PG + 2):
                    if p < PG:
                        turn_page(b, p, first)
                    if p == 2 and not first:
                        pe.wait_ge(s_sev, b)
                    if p >= 2:
                        score_page(b, p - 2)
                    if not first:
                        if p == 4:
                            max_turn(b - 1)
                        if p == 8:
                            max_spread(b - 1)
                for c in range(4):
                    ins = mm(psum_s[0:TS, 1, c * 8:c * 8 + 8], qkv[:, 4 + c, TP:T],
                             q_diag[:, c, ds(b, 1), :].rearrange("p a x -> p (a x)"), start=True, stop=True)
                ins.then_inc(s_sc, 1)
            scores(0, True)
            scores(1, False)
            value(0)
            with pe.Fori(2, NB) as b:
                scores(b, False)
                value(b - 1)
            max_turn(NB - 1)
            max_spread(NB - 1)
            value(NB - 1)

            def gemm(phase, moving, ready, between=None):
                seen = set()

                def once(k):
                    if k not in seen:
                        seen.add(k)
                        ready(k)
                for j in range(4):
                    slab(phase, 0, j, moving, once)
                    if j == 0 and between:
                        between()
                with pe.Fori(1, phase.turns) as i:
                    for j in range(4):
                        slab(phase, i, j, moving)

            def sums(n):
                def go():
                    pe.wait_ge(s_ss, 9 * n + 9)
                    sum_channels()
                return go
            low_ready = lambda base: lambda k: pe.wait_ge(s_hlo, base + k + 1)
            xa_ready = lambda n: lambda k: pe.wait_ge(s_xlo, 8 * n + k + 1)

            gemm(ph["out"], hid, low_ready(HB["out"]))

            def rows_out(group, src, parts, n, busy):
                if busy:
                    pe.wait_ge(s_rowsd, group - 1)
                for c in range(n):
                    ins = tr(bank[group % 2][0:parts, c * P:(c + 1) * P], src(c), ident[:, :])
                ins.then_inc(s_rows, 1)

            def ffn(l):
                pe.wait_ge(s_st, 16 * (2 if l == 0 else 5))
                for c in range(FC):
                    ins = tr(bank[0][:, c * 2 * NB:(c + 1) * 2 * NB], f_row[0:2 * NB, c * P:(c + 1) * P],
                             ident[0:2 * NB, 0:2 * NB])
                ins.then_inc(s_fst, 1)
                n = "out" if l == 0 else "pw2"
                for half in range(2):
                    gemm(ph[f"up{l}{half}"], xa, xa_ready(NORM[n]), sums(SUM[n]) if half == 0 else None)
                    if half == 1:
                        pe.wait_ge(s_tail, 2 + (l + 1) * (FC + 1))
                        for q in range(6):
                            rows_out(R[f"ffn{l}"] + q, lambda c: tail_f[:, 4 * q + c, :], FT, min(4, FC - 4 * q), q >= 2)
                    gemm(ph[f"down{l}{half}"], hid, low_ready(HB[f"up{l}"] + half * HALF[0]))

            ffn(0)
            pe.wait_ge(s_st, 16 * 4)
            for q in range(4):
                if q >= 2:
                    pe.wait_ge(s_fstd, 1 + q - 1)
                for c in range(2):
                    for k in range(2):
                        ins = tr(bank[q % 2][:, c * 240 + k * 120:c * 240 + k * 120 + 120],
                                 c_row[:, k, (2 * q + c) * P:(2 * q + c + 1) * P], ident[0:120, 0:120])
                ins.then_inc(s_fst, 1)
            gemm(ph["pw1"], xa, xa_ready(NORM["down01"]), sums(SUM["down01"]))
            pe.wait_ge(s_ux, DC)
            for q in range(2):
                rows_out(R["conv_c"] + q, lambda c: tail_c[:, 4 * q + c, :], UT, 4, False)
            pe.wait_ge(s_ss, 9 * SUM["mean"] + 9)
            sum_channels()
            pe.wait_ge(s_ss, 9 * SUM["var"] + 9)
            sum_channels()
            gemm(ph["pw2"], hid, low_ready(HB["pw2"]))
            ffn(1)
            pe.wait_ge(s_xnew, XN["down11"] + DC)
            for t in range(5):
                n = P if t < 4 else TS
                for q in range(2):
                    if t:
                        pe.wait_ge(s_rowsd, R["y"] + 2 * t + q - 1)
                    for c in range(4):
                        ins = tr(bank[q][0:n, c * P:(c + 1) * P], x[:, 4 * q + c, t * P:t * P + n], ident[:, :])
                    ins.then_inc(s_rows, 1)


_INS = ["x_prompt", "x_sample", "cache_k", "cache_v", "cache_logf", "page_table", "state_conv_a", "state_conv_c",
        "state_ffn", "norm_mix0", "w_in0", "b_forget", "conv_a_w", "q_norm", "k_norm", "w_out0", "norm_mix1",
        "w_pw1", "b_pw1", "conv_c_w", "conv_c_b", "ln_c_g", "ln_c_b", "w_pw2", "norm_ffn", "w_up", "conv_ffn_w",
        "w_down"]
_OUTS = [("y_prompt", (1, TP, D)), ("y_sample", (NB, NT, D)),
         ("p_conv_a", (1, 1, 2, 512)), ("s_conv_a", (1, NB, 2, 512)),
         ("p_k", (1, 1, TP, NH, HD)), ("s_k", (1, NB, NT, NH, HD)),
         ("p_v", (1, 1, TP, NH, HD)), ("s_v", (1, NB, NT, NH, HD)),
         ("p_logf", (1, 1, TP, NH)), ("s_logf", (1, NB, NT, NH)),
         ("p_conv_c", (1, 1, CC - 1, D)), ("s_conv_c", (1, NB, CC - 1, D)),
         ("p_ffn", (2, 1, 2, DFF)), ("s_ffn", (2, NB, 2, DFF))]


def kernel(**inputs):
    import numpy as np
    import concourse.bacc as bacc
    from concourse.bass_utils import run_bass_kernel_spmd

    nc = bacc.Bacc("TRN2", target_bir_lowering=False, num_devices=1, dynamic_dma_scratch_size=SCRATCH)
    arrays, a, o = {}, {}, {}
    for name in _INS:
        v = np.ascontiguousarray(inputs[name])
        arrays[f"in_{name}"] = v
        a[name] = nc.dram_tensor(f"in_{name}", v.shape, mybir.dt.from_np(v.dtype), kind="ExternalInput").ap()
    for name, shape in _OUTS:
        o[name] = nc.dram_tensor(f"out_{name}", shape, F32, kind="ExternalOutput").ap()
    build(nc, a, o)
    r = run_bass_kernel_spmd(nc, [arrays], core_ids=[0])
    return tuple(r.results[0][f"out_{name}"] for name, _ in _OUTS)
```

```python
from contextlib import ExitStack, contextmanager

import concourse.bass as bass
from concourse import mybir

F32 = mybir.dt.float32
F32R = mybir.dt.float32r
I32 = mybir.dt.int32
ALU = mybir.AluOpType
ACT = mybir.ActivationFunctionType
AX = mybir.AxisListType
ds = bass.ds

P = 128
D = 1024
DC = D // P
TP = 512
NB, NT = 8, 4
TS = NB * NT
T = TP + TS
HT = T // 2
NH, HD = 8, 64
PG = 16
NPOOL = 160
DFF = 2816
FC = DFF // P
HALF = (12, 10)
CA, CF, CC = 3, 3, 31
EPS = 1e-6
MASKED = -1e30
SLOTS = 4
KS = 8
SCRATCH = 1024
NQ = T - TP
UT = (CC - 1) + TS
FT = 2 + 2 * NB


class Steps:

    def __init__(self):
        self.base, self.local, self.i, self.per = 0, 0, None, 0

    def tick(self):
        self.local += 1
        return self.now()

    def now(self):
        at = self.base + self.local
        return at if self.i is None else self.i * self.per + at

    @contextmanager
    def loop(self, eng, start, end, per):
        self.base += self.local - start * per
        self.local = 0
        with eng.Fori(start, end) as i:
            self.i, self.per = i, per
            yield i
        assert self.local == per, (self.local, per)
        self.base += end * per
        self.local, self.i, self.per = 0, None, 0


class Phase:

    def __init__(self, name, slab0, group0, turns, tiles, per_group, residual):
        self.name, self.slab0, self.group0 = name, slab0, group0
        self.turns, self.tiles, self.per_group = turns, tiles, per_group
        self.slabs = 4 * turns
        self.slab1 = slab0 + self.slabs
        self.group1 = group0 + self.slabs // per_group
        self.residual = residual

    def slab(self, i, j):
        return i * 4 + (self.slab0 + j)

    def group(self, i, j):
        return i * (4 // self.per_group) + (self.group0 + j // self.per_group)


def plan():
    phases, slab = {}, 0
    groups = {False: 0, True: DC}
    rows = [("qkv", 3, DC, 1), ("gates", 3, DC, 1), ("out", 2, DC, 1)]
    ffn = lambda l: [(f"up{l}0", HALF[0] // 2, DC, 1), (f"down{l}0", 4, HALF[0] // 2, 2),
                     (f"up{l}1", HALF[1] // 2, DC, 1), (f"down{l}1", 4, HALF[1] // 2, 2)]
    rows += ffn(0) + [("pw1", 4, DC, 1), ("pw2", 2, DC, 1)] + ffn(1)
    for name, turns, tiles, per in rows:
        residual = name in ("out", "pw2") or name.startswith("down")
        p = phases[name] = Phase(name, slab, groups[residual], turns, tiles, per, residual)
        slab, groups[residual] = p.slab1, p.group1
    return phases


def param_rows():
    at, rows = 0, {}
    for name, n in (("mix0", DC), ("qk", 2), ("conv_a", CA * 4), ("ffn", 2 * DC), ("conv_f", 2 * CF * FC),
                    ("mix1", DC), ("b_pw1", 2 * DC), ("conv_cb", DC), ("ln_g", DC), ("ln_b", DC),
                    ("conv_c", CC * DC)):
        rows[name] = (at, n)
        at += n
    return rows, at


def row_blocks(r0, n):
    out = []
    while n:
        k = min(n, P - r0 % P)
        out.append((r0, k))
        r0, n = r0 + k, n - k
    return out


def build(nc, a, o):
    ph = plan()
    order = list(ph.values())
    prow, n_rows = param_rows()
    with ExitStack() as ctx:
        sem = lambda name: ctx.enter_context(nc.semaphore(name))

        top = [SCRATCH]

        def place(name, shape, dt, at=None):
            size = 4
            for n in shape[1:]:
                size *= n
            if at is None:
                at = top[0]
                top[0] += (size + 31) // 32 * 32
            assert at + size <= 229344, name
            return nc.alloc_sbuf_tensor_at(name, shape, dt, offset=at), at

        CH = T * 4
        x, _ = place("x", [P, DC, T], F32)
        xa_h, xa_at = place("xa_h", [P, DC, T], F32R)
        xa_l, _ = place("xa_l", [P, DC, T], F32R)
        h_h, hh_at = place("h_h", [P, HALF[0], T], F32R)
        h_l, hl_at = place("h_l", [P, HALF[0], T], F32R)
        w_raw, raw_at = place("w_raw", [P, SLOTS, DC * P], F32)
        w_h, wh_at = place("w_h", [P, SLOTS, DC * P], F32R)
        w_l, wl_at = place("w_l", [P, SLOTS, DC * P], F32R)
        ident, _ = place("ident", [P, P], F32)
        ones, _ = place("ones", [P, P], F32)
        head_ones, _ = place("head_ones", [P, P], F32)
        causal, _ = place("causal", [P, P], F32)
        later, _ = place("later", [P, P], F32)
        params, _ = place("params", [P, n_rows], F32)
        r_all, _ = place("r_all", [P, T], F32)
        ssum, ss_at = place("ssum", [P, T], F32)
        sq, sq_at = place("sq", [P, 2, T], F32)
        tmp, tmp_at = place("tmp", [P, 2, T], F32)
        base = top[0]
        x_rows, _ = place("x_rows", [P, 5, D], F32, hh_at)
        p_rows, _ = place("p_rows", [P, 4, P], F32, hh_at + 5 * D * 4)
        qkv, _ = place("qkv", [P, 12, T], F32)
        kt, kt_at = place("kt", [P, 4, 4 * P], F32)
        v_tok, vt_at = place("v_tok", [P, 4, 4 * P], F32)
        sc, sc_at = place("sc", [P, PG + 1, 32], F32)
        pr, _ = place("pr", [P, 2, PG + 1, 32], F32, hh_at + 4 * CH)
        dk, _ = place("dk", [P, NB, PG, NH], F32)
        cn_all, _ = place("cn_all", [P, NH, NB, NT], F32)
        q_diag, _ = place("q_diag", [P, 4, NB, 8], F32)
        nbias, _ = place("nbias", [TS, NB, NH, NT], F32)
        small, _ = place("small", [P, 224], F32)
        fw, _ = place("fw", [P, DC, NH], F32)
        fw_h, _ = place("fw_h", [P, DC, NH], F32R)
        fw_l, _ = place("fw_l", [P, DC, NH], F32R)
        ext_a, _ = place("ext_a", [P, 4, NB, CA - 1 + NT], F32)
        tail_a, _ = place("tail_a", [P, 4, FT], F32)
        lf_row, _ = place("lf_row", [P, 5, NH], F32)
        m1, gmax, diag = small[:, 0:32], small[0:32, 32:33], small[0:32, 64:96]
        p_sum, rec = small[:, 96:128], small[:, 128:160]
        cq = small[:, 160:192]
        cns = small[0:TS, 192:200]
        b_f = small[0:NH, 200:201]
        rmax, rsum, rinv = small[:, 204:208], small[:, 208:212], small[:, 212:216]
        k_pg, _ = place("k_pg", [P, KS, 4 * P], F32, xa_at)
        cb, _ = place("cb", [P, NH, TP], F32, xa_at + KS * 2048)
        v_pg, _ = place("v_pg", [P, PG, 4 * P], F32, wh_at)
        u4, _ = place("u4", [P, 4, T], F32, hh_at + 8 * CH)
        g4, _ = place("g4", [P, 4, T], F32, hl_at + 8 * CH)
        lf_pg, _ = place("lf_pg", [P, D], F32, kt_at)
        lf_k, _ = place("lf_k", [P, NH * NB, PG], F32, kt_at + 4096)
        suf, _ = place("suf", [P, NH * NB, PG], F32, vt_at)
        pgix, _ = place("pgix", [P, 1], I32, vt_at + 4096)
        fz, _ = place("fz", [NH, T], F32, kt_at)
        fe, _ = place("fe", [NH, T], F32, kt_at + CH)
        seg, _ = place("seg", [NH, T], F32, kt_at + 2 * CH)
        cmask, _ = place("cmask", [NH, 2, TP], F32, kt_at)
        logf, _ = place("logf", [NH, T], F32, vt_at)
        cum, _ = place("cum", [NH, T], F32, vt_at + CH)
        cnm, _ = place("cnm", [NH, NH, TS], F32, vt_at + 2 * CH)
        k_row, _ = place("k_row", [P, 2, 4 * P], F32, hh_at + 8 * CH)
        s_row, _ = place("s_row", [TS, 2, 4 * P], F32, hh_at + 8 * CH + 4096)
        a_row, _ = place("a_row", [2 * NB, 4 * P], F32, sc_at)
        a_out, _ = place("a_out", [FT, 4 * P], F32, sc_at)
        sb, _ = place("sb", [P, 4, TP], F32, hl_at + 8 * CH)
        pt, _ = place("pt", [P, 2, TP], F32, ss_at)
        q_s, _ = place("q_s", [P, TP], F32, ss_at + 4096)
        k_s, _ = place("k_s", [P, TP], F32, ss_at + 6144)
        v_s, _ = place("v_s", [P, 4, P], F32, ss_at + 8192)
        top[0] = base
        gate, _ = place("gate", [P, 2, T], F32)
        cv, _ = place("cv", [P, 2, T], F32)
        sl, _ = place("sl", [P, 2, T], F32)
        sr, sr_at = place("sr", [P, 2, T], F32)
        ext_f, _ = place("ext_f", [P, FC, NB, CF - 1 + NT], F32)
        tail_f, _ = place("tail_f", [P, FC, FT], F32)
        f_row, fr_at = place("f_row", [FT, DFF], F32)
        yc, yc_at = place("yc", [P, DC, T], F32)
        y_row, _ = place("y_row", [P, 2, D], F32, yc_at)
        ua, _ = place("ua", [P, 2, T], F32, base)
        u, _ = place("u", [P, 2, T], F32, base + 2 * CH)
        sg, _ = place("sg", [P, 2, T], F32, base + 4 * CH)
        prod, _ = place("prod", [P, TS, CC], F32, sr_at)
        ext_c, _ = place("ext_c", [P, DC, NB, CC - 1 + NT], F32, hh_at + 8 * CH)
        c_row, _ = place("c_row", [4 * (CC - 1), 2, D], F32, hl_at + 8 * CH)
        tail_c, _ = place("tail_c", [P, DC, UT], F32, fr_at)
        u_row, _ = place("u_row", [UT, D], F32, fr_at + 4096)

        pair = [nc.alloc_psum_tensor(f"pair{n}", [P, 2, 512], F32) for n in range(2)]
        psum_s = nc.alloc_psum_tensor("psum_s", [P, 2, 512], F32)
        bank = [nc.alloc_psum_tensor(f"bank{n}", [P, 512], F32) for n in range(2)]
        pb = [pair[0][:, 0, :], pair[0][:, 1, :], pair[1][:, 0, :], pair[1][:, 1, :]]

        s_raw = [sem(f"raw{j}") for j in range(SLOTS)]
        s_hi, s_lo = sem("hi"), sem("lo")
        s_slab = sem("slab")
        s_free = sem("free")
        s_prm, s_xld, s_st, s_fw, s_ix, s_lf = (sem(n) for n in (
            "params_in", "x_in", "state_in", "fw_in", "index_in", "logf_in"))
        s_cst = sem("constants")
        s_tp = sem("x_turned")
        s_xnew = sem("x_new")
        s_sq, s_ss, s_stat = sem("squares"), sem("added"), sem("sums")
        s_xhi, s_xlo = sem("xa_high"), sem("xa_low")
        s_var, s_rt, s_r = sem("variance"), sem("root"), sem("inv_root")
        s_dve = sem("dve_step")
        s_ya, s_cv, s_sl, s_sr, s_hhi, s_hlo = (sem(n) for n in (
            "y_a", "conv", "silu", "silu_r", "h_high", "h_low"))
        s_out, s_rowdma, s_aout = sem("written"), sem("row_written"), sem("a_written")
        s_misc, s_miscd = sem("short"), sem("short_read")
        s_suf, s_fz, s_fe, s_cum, s_cm, s_cbp, s_cb = (sem(n) for n in (
            "later_pages", "forget_in", "forget_ln", "cum", "c_masked", "c_spread", "c_copied"))
        s_qsq, s_hv, s_hrt, s_qk, s_tail = (sem(n) for n in ("qk_squares", "qk_var", "qk_root", "qk_normed", "tail"))
        s_k = [sem(f"k{n}") for n in range(KS)]
        s_v = [sem(f"v{n}") for n in range(PG)]
        s_tr, s_kt, s_sp, s_sc, s_sev = (sem(n) for n in (
            "page_turned", "page_copied", "page_scored", "batch_scored", "scores_read"))
        s_m1, s_mt, s_dg, s_mb = (sem(n) for n in ("max_keys", "max_turned", "max_diag", "max_spread"))
        s_sm, s_p, s_lp, s_l = (sem(n) for n in ("shifted", "exps", "exps_added", "exps_summed"))
        s_pvp, s_oev, s_rec = sem("page_valued"), sem("values_read"), sem("inv_sum")
        s_qd = sem("q_side_by_side")
        s_qs, s_s, s_sb, s_pe = (sem(n) for n in ("pair_copied", "p_scored", "p_biased", "p_exp"))
        s_sbr, s_pn, s_ptt, s_ptc, s_po, s_pod = (sem(n) for n in (
            "p_read", "p_norm", "p_turned", "p_tcopied", "p_valued", "p_out"))
        s_rows, s_rowsd = sem("rows_turned"), sem("rows_read")
        s_fst, s_fstd = sem("state_turned"), sem("state_read")
        s_sig, s_u, s_ux, s_mu, s_xc, s_ty, s_s32 = (sem(n) for n in (
            "u_sig", "u", "u_kept", "mean", "centred", "scaled", "swish"))
        n_out = [0]

        halves = lambda ap: ap.rearrange("p (h t) -> p h t", h=2)
        gview = lambda b: pair[b][:, :, 0:HT]
        par = lambda name, k: params[:, ds(k + prow[name][0], 1)]
        R = {}
        at = 0
        for name, n in (("kv", 10), ("ffn0", 6), ("conv_c", 2), ("ffn1", 6), ("y", 10)):
            R[name] = at
            at += n
        XN = dict(init=0, **{p.name: p.group0 for p in order if p.residual})
        NORM = dict(init=0, out=1, down01=2, pw2=3)
        SUM = dict(init=0, out=1, down01=2, mean=3, var=4, pw2=5)
        SQ = dict(init=0, out=1, down01=2, var=3, pw2=4)
        GAIN = dict(init=("mix0", 0), out=("ffn", 0), down01=("mix1", 0), pw2=("ffn", DC))
        HB = dict(out=0, up0=8, pw2=8 + FC, up1=16 + FC)

        block = ctx.enter_context(nc.Block())

        def slab_tiles(s):
            for p in order:
                if p.slab0 <= s < p.slab1:
                    return p.tiles

        def turns(eng, phase, body, peel=0):
            for i in range(peel):
                body(i, False)
            if phase.turns - 1 > peel:
                with eng.Fori(peel, phase.turns - 1) as i:
                    body(i, False)
            body(phase.turns - 1, True)

        def ahead(split, phase, i, j, last):
            turn, slot = i + (phase.slab0 // 4 + (j + 3) // 4), (j + 3) % 4
            tiles = phase.tiles
            if last and j >= 1:
                tiles = slab_tiles(phase.slab1 + j - 1)
                if tiles is None or phase is ph["gates"]:
                    return
            split(turn, slot, tiles)

        @block.sync
        def _(sp):
            for k in range(4):
                sp.dma_start(x_rows[:, k, :], a["x_prompt"][0, k * P:(k + 1) * P, :]).then_inc(s_xld, 16)
            sp.dma_start(x_rows[0:TS, 4, :], a["x_sample"].rearrange("b t d -> (b t) d")).then_inc(s_xld, 16)
            chunks = lambda ap: ap.rearrange("a (c p) -> (a c) p", p=P)
            sources = dict(mix0=chunks(a["norm_mix0"]), conv_a=chunks(a["conv_a_w"].rearrange("a k d -> (a k) d")),
                           ffn=chunks(a["norm_ffn"]), conv_f=chunks(a["conv_ffn_w"].rearrange("l k d -> (l k) d")),
                           mix1=chunks(a["norm_mix1"]), b_pw1=chunks(a["b_pw1"]), conv_cb=chunks(a["conv_c_b"]),
                           ln_g=chunks(a["ln_c_g"]), ln_b=chunks(a["ln_c_b"]),
                           conv_c=chunks(a["conv_c_w"].rearrange("a k d -> (a k) d")))
            for name, (r0, n) in prow.items():
                if name == "qk":
                    for r, g in enumerate(("q_norm", "k_norm")):
                        for hh in range(2):
                            sp.dma_start(p_rows[r0 + r:r0 + r + 1, 0, hh * HD:(hh + 1) * HD], a[g]).then_inc(s_prm, 16)
                    continue
                for at, k in row_blocks(r0, n):
                    done = at - r0
                    sp.dma_start(p_rows[at % P:at % P + k, at // P, :], sources[name][done:done + k, :])\
                      .then_inc(s_prm, 16)

            def load(phase, i, j, src):
                s = phase.slab(i, j)
                if not (isinstance(s, int) and s < SLOTS):
                    sp.wait_ge(s_lo, s - (SLOTS - 1))
                sp.dma_start(w_raw[:, j, 0:phase.tiles * P].rearrange("p (k n) -> p k n", n=P), src)\
                  .then_inc(s_raw[j], 16)

            def cols(w, at, tiles=DC, k0=0):
                return w.rearrange("(k p) n -> p k n", p=P)[:, k0:k0 + tiles, ds(at, P)]

            def out(dst, src, signal=None):
                sp.dma_start(dst, src).then_inc(signal or s_out, 16)
                if signal is None:
                    n_out[0] += 1

            w_in, w_out = a["w_in0"][0], a["w_out0"][0]
            for j in range(4):
                load(ph["qkv"], 0, j, cols(w_in, 1536 + j * P))
            sp.dma_start(pgix[:, :], a["page_table"].rearrange("b (p a) -> (b p) a", a=1)).then_inc(s_ix, 16)
            sp.dma_start(a_row[:, :], a["state_conv_a"][0].rearrange("b t d -> (b t) d")).then_inc(s_st, 16)
            sp.dma_start(fw[:, :, :], w_in.rearrange("(k p) n -> p k n", p=P)[:, :, 3072:3080]).then_inc(s_fw, 16)
            sp.dma_start(b_f, a["b_forget"].rearrange("a h -> h a")).then_inc(s_fw, 16)
            with sp.Fori(1, 3) as i:
                for j in range(4):
                    load(ph["qkv"], i, j, cols(w_in, i * 512 + (1536 + j * P)))
            for i, at in enumerate((512, 1024, 0)):
                for j in range(4):
                    load(ph["gates"], i, j, cols(w_in, at + j * P))
            for j in range(4):
                load(ph["out"], 0, j, cols(w_out, j * P))
            out(o["s_conv_c"][0, :, 0:CC - 1 - NT, :], a["state_conv_c"][0, :, NT:CC - 1, :])

            sp.wait_ge(s_slab, ph["gates"].slab1)

            def page_ids(b):
                return nc.values_load_multi_w_load_instructions(a["page_table"][ds(b, 1), :],
                                                                engines=(mybir.EngineType.SP,), min_val=0,
                                                                max_val=NPOOL - 1)[1]

            def page(b, p, pid, cache, slots, done, first):
                place_, arrived = ((k_pg, s_k) if cache == "cache_k" else (v_pg, s_v))
                if not first:
                    sp.wait_ge(done, b * PG + (p - slots + 1))
                sp.dma_start(place_[:, p % slots, :], a[cache][0, ds(pid, 1)].rearrange("a k h d -> (a k) (h d)"))\
                  .then_inc(arrived[p % slots], 16)

            first_ids = page_ids(0)
            for p in range(KS):
                page(0, p, first_ids[p], "cache_k", KS, s_tr, True)
            for t in range(4):
                sp.wait_ge(s_rowsd, R["kv"] + 2 * t + 1)
                out(o["p_k"][0, 0, t * P:(t + 1) * P].rearrange("t h d -> t (h d)"), k_row[:, t % 2, :], s_rowdma)
                sp.wait_ge(s_rowsd, R["kv"] + 2 * t + 2)
                out(o["p_v"][0, 0, t * P:(t + 1) * P].rearrange("t h d -> t (h d)"), v_tok[:, t, :])
            sp.wait_ge(s_rowsd, R["kv"] + 10)
            out(o["s_k"][0].rearrange("b t h d -> (b t) (h d)"), s_row[:, 0, :])
            out(o["s_v"][0].rearrange("b t h d -> (b t) (h d)"), s_row[:, 1, :])
            sp.wait_ge(s_miscd, 9)
            with nc.allow_non_contiguous_dma(reason="32-byte rows of log forgets"):
                out(o["p_logf"][0, 0].rearrange("(t p) h -> p t h", p=P), lf_row[:, 0:4, :])
                out(o["s_logf"][0].rearrange("b t h -> (b t) h"), lf_row[0:TS, 4, :])
            out(o["p_conv_a"][0, 0], a_out[0:2, :], s_aout)
            out(o["s_conv_a"][0].rearrange("b t d -> (b t) d"), a_out[2:FT, :], s_aout)
            for p in range(KS, PG):
                page(0, p, first_ids[p], "cache_k", KS, s_tr, False)
            for p in range(PG):
                page(0, p, first_ids[p], "cache_v", PG, s_pvp, True)

            def batch_pages(b, with_values=True):
                keys = page_ids(b)
                values = page_ids(b - 1) if with_values else None
                for p in range(PG):
                    page(b, p, keys[p], "cache_k", KS, s_tr, False)
                    if with_values:
                        page(b - 1, p, values[p], "cache_v", PG, s_pvp, False)
            batch_pages(1, False)
            with sp.Fori(2, NB) as b:
                batch_pages(b)
            last_ids = page_ids(NB - 1)
            for p in range(PG):
                page(NB - 1, p, last_ids[p], "cache_v", PG, s_pvp, False)
            for j in range(4):
                load(ph["out"], 1, j, cols(w_out, 512 + j * P))

            def ffn(l):
                up, down = a["w_up"][l], a["w_down"][l]
                sp.wait_ge(s_xhi, 8 * NORM["out" if l == 0 else "pw2"] + 1)
                sp.wait_ge(s_out, 16 * n_out[0])
                sp.dma_start(f_row[0:2 * NB, :], a["state_ffn"][l].rearrange("b t d -> (b t) d")).then_inc(s_st, 16)
                for half in range(2):
                    pu, pd, k0 = ph[f"up{l}{half}"], ph[f"down{l}{half}"], half * HALF[0]
                    with sp.Fori(0, pu.turns) as i:
                        for j in range(4):
                            load(pu, i, j, cols(up, i * (2 * P) + ((j % 2) * DFF + (k0 + j // 2) * P)))
                    with sp.Fori(0, pd.turns) as i:
                        for j in range(4):
                            load(pd, i, j, cols(down, i * (2 * P) + (j // 2) * P, pd.tiles,
                                                k0 + (j % 2) * pd.tiles))
                sp.wait_ge(s_rowsd, R[f"ffn{l}"] + 6)
                out(o["p_ffn"][l, 0], f_row[0:2, :])
                out(o["s_ffn"][l].rearrange("b t d -> (b t) d"), f_row[2:FT, :])

            ffn(0)
            n_out.append(n_out[0])
            sp.wait_ge(s_slab, ph["down01"].slab1)
            for k in range(2):
                sp.dma_start(c_row[:, k, :], a["state_conv_c"][0, 4 * k:4 * k + 4].rearrange("b t d -> (b t) d"))\
                  .then_inc(s_st, 16)
            with sp.Fori(0, ph["pw1"].turns) as i:
                for j in range(4):
                    load(ph["pw1"], i, j, cols(a["w_pw1"][0], i * (2 * P) + ((j % 2) * D + (j // 2) * P)))
            for i in range(2):
                for j in range(4):
                    load(ph["pw2"], i, j, cols(a["w_pw2"][0], i * 512 + j * P))
            sp.wait_ge(s_rowsd, R["conv_c"] + 2)
            out(o["p_conv_c"][0, 0], u_row[0:CC - 1, :])
            for b in range(NB):
                out(o["s_conv_c"][0, b, CC - 1 - NT:CC - 1, :],
                    u_row[CC - 1 + NT * b:CC - 1 + NT * (b + 1), :])
            ffn(1)
            for t in range(5):
                sp.wait_ge(s_rowsd, R["y"] + 2 * t + 2)
                if t < 4:
                    out(o["y_prompt"][0, t * P:(t + 1) * P, :], y_row[:, t % 2, :], s_rowdma)
                else:
                    out(o["y_sample"].rearrange("b t d -> (b t) d"), y_row[0:TS, 0, :])
            sp.wait_ge(s_rowdma, 16 * 8)
            sp.wait_ge(s_aout, 16 * 2)
            sp.wait_ge(s_out, 16 * n_out[0])

        @block.gpsimd
        def _(pool):
            g = nc.gpsimd
            g.memset(ident[:, :], 0.0).then_inc(s_cst, 1)
            g.memset(ones[:, :], 1.0).then_inc(s_cst, 1)
            g.memset(head_ones[:, :], 0.0).then_inc(s_cst, 1)
            g.memset(causal[:, :], 0.0).then_inc(s_cst, 1)
            g.memset(later[:, :], 1.0).then_inc(s_cst, 1)
            g.memset(nbias[:, :, :, :], 0.0).then_inc(s_cst, 1)
            g.memset(q_diag[:, :, :, :], 0.0).then_inc(s_cst, 1)
            g.memset(sc[:, PG, :], MASKED).then_inc(s_cst, 1)
            pool.wait_ge(s_cst, 8)
            g.memset(head_ones[0:HD, 0:HD], 1.0).then_inc(s_cst, 1)
            g.memset(head_ones[HD:P, HD:P], 1.0).then_inc(s_cst, 1)
            pool.wait_ge(s_cst, 10)
            g.affine_select(out=ident[:, :], in_=ident[:, :], compare_op=ALU.not_equal, fill=1.0, base=0,
                            pattern=[[-1, P]], channel_multiplier=1).then_inc(s_cst, 1)
            g.affine_select(out=causal[:, :], in_=causal[:, :], compare_op=ALU.is_ge, fill=MASKED, base=0,
                            pattern=[[-1, P]], channel_multiplier=1).then_inc(s_cst, 1)
            g.affine_select(out=later[:, :], in_=later[:, :], compare_op=ALU.is_gt, fill=0.0, base=0,
                            pattern=[[-1, P]], channel_multiplier=1).then_inc(s_cst, 1)
            g.affine_select(out=nbias[:, :, :, :], in_=nbias[:, :, :, :], compare_op=ALU.is_ge, fill=MASKED, base=0,
                            pattern=[[-NT, NB], [0, NH], [0, NT]], channel_multiplier=1).then_inc(s_cst, 1)
            pool.wait_ge(s_cst, 14)
            g.affine_select(out=nbias[:, :, :, :], in_=nbias[:, :, :, :], compare_op=ALU.is_ge, fill=MASKED, base=0,
                            pattern=[[NT, NB], [0, NH], [1, NT]], channel_multiplier=-1).then_inc(s_cst, 1)
            pool.wait_ge(s_ix, 16)
            g.indirect_dma_start(out=lf_pg[:, :], out_offset=None,
                                 in_=a["cache_logf"][0].rearrange("n k h -> n (k h)"),
                                 in_offset=bass.IndirectOffsetOnAxis(ap=pgix[:, 0:1], axis=0)).then_inc(s_lf, 16)
            pool.wait_ge(s_fw, 33)
            g.tensor_tensor(fw_l[:, :, :], fw[:, :, :], fw_h[:, :, :].bitcast(F32), ALU.subtract).then_inc(s_fw, 1)

            def split_low(turn, slot, tiles):
                n = tiles * P
                pool.wait_ge(s_hi, turn * 4 + (slot + 1))
                g.tensor_tensor(w_l[:, slot, 0:n], w_raw[:, slot, 0:n], w_h[:, slot, 0:n].bitcast(F32),
                                ALU.subtract).then_inc(s_lo, 1)

            for slot in range(3):
                split_low(0, slot, DC)
            for phase in (ph["qkv"], ph["gates"]):
                def turn(i, last, phase=phase):
                    for j in range(4):
                        ahead(split_low, phase, i, j, last)
                turns(pool, phase, turn)
            for slot in range(3):
                split_low(ph["out"].slab0 // 4, slot, DC)
            def turn(i, last):
                for j in range(4):
                    ahead(split_low, ph["out"], i, j, last)
            turns(pool, ph["out"], turn)

            def ffn(l):
                for half in range(2):
                    pu, pd = ph[f"up{l}{half}"], ph[f"down{l}{half}"]

                    def turn(i, last):
                        for j in range(4):
                            ahead(split_low, pu, i, j, last)
                            if j % 2:
                                k = i * 2 + (l * FC + half * HALF[0] + j // 2)
                                pool.wait_ge(s_sl, k + 1)
                                pool.wait_ge(s_r, SQ["out" if l == 0 else "pw2"] + 1)
                                pool.wait_ge(s_free, pu.group(i, j) - 3)
                                g.tensor_tensor(sr[:, j // 2, :], sl[:, j // 2, :], r_all[:, :], ALU.mult)\
                                 .then_inc(s_sr, 1)
                    turns(pool, pu, turn)

                    def turn(i, last):
                        for j in range(4):
                            ahead(split_low, pd, i, j, last)
                    turns(pool, pd, turn)
            ffn(0)
            for phase in (ph["pw1"], ph["pw2"]):
                def turn(i, last, phase=phase):
                    for j in range(4):
                        ahead(split_low, phase, i, j, last)
                turns(pool, phase, turn)
            ffn(1)

        @block.scalar
        def _(act):
            A = nc.scalar.activation

            def apart(i):
                if not isinstance(i, int):
                    act.wait_ge(s_cst, 15)

            def split_high(turn, slot, tiles):
                n = tiles * P
                act.wait_ge(s_raw[slot], turn * 16 + 16)
                if not (isinstance(turn, int) and turn == 0):
                    act.wait_ge(s_slab, turn * 4 + (slot - 3))
                A(w_h[:, slot, 0:n], w_raw[:, slot, 0:n], ACT.Copy).then_inc(s_hi, 1)

            def norm_work(stage, m, b):
                name, g0 = GAIN[stage]
                act.wait_ge(s_xnew, m + (XN[stage] + 1))
                if not (isinstance(m, int) and m < 2):
                    act.wait_ge(s_ss, m + 9 * SUM[stage])
                apart(m)
                A(sq[:, b, :], x[:, ds(m, 1), :].rearrange("p a t -> p (a t)"), ACT.Square).then_inc(s_sq, 1)
                A(xa_h[:, ds(m, 1), :].rearrange("p a t -> p (a t)"), x[:, ds(m, 1), :].rearrange("p a t -> p (a t)"),
                  ACT.Copy, scale=par(name, m + g0)).then_inc(s_xhi, 1)

            def root(k):
                act.wait_ge(s_var, k + 1)
                A(r_all[:, :], r_all[:, :], ACT.Sqrt).then_inc(s_rt, 1)

            act.wait_ge(s_miscd, 1)
            for m in range(DC):
                norm_work("init", m, m % 2)
            for slot in range(3):
                split_high(0, slot, DC)
            act.wait_ge(s_fw, 32)
            A(fw_h[:, :, :], fw[:, :, :], ACT.Copy).then_inc(s_fw, 1)
            root(0)
            for i in range(3):
                for j in range(4):
                    ahead(split_high, ph["qkv"], i, j, i == 2)
            act.wait_ge(s_fz, 1)
            A(fe[:, :], fz[:, :], ACT.Abs).then_inc(s_fe, 1)
            act.wait_ge(s_fe, 1)
            A(fe[:, :], fe[:, :], ACT.Exp, scale=-1.0).then_inc(s_fe, 1)
            act.wait_ge(s_fe, 2)
            A(fe[:, :], fe[:, :], ACT.Ln, bias=1.0).then_inc(s_fe, 1)
            for i in range(3):
                for j in range(4):
                    ahead(split_high, ph["gates"], i, j, i == 2)
                    c = 4 * i + j
                    if c < 8:
                        act.wait_ge(s_free, c + 1)
                        if c >= 2:
                            act.wait_ge(s_misc, 6 + c - 2)
                        A(sq[:, c % 2, :], qkv[:, c, :], ACT.Square).then_inc(s_qsq, 1)
                        act.wait_ge(s_hv, c + 1)
                        A(tmp[:, c % 2, :], tmp[:, c % 2, :], ACT.Sqrt).then_inc(s_hrt, 1)
                    else:
                        m = c - 8
                        act.wait_ge(s_ya, m + 1)
                        A(h_h[:, m, :], g4[:, m, :], ACT.Copy).then_inc(s_hhi, 1)
            for h in range(NH):
                act.wait_ge(s_cbp, h + 1)
                A(cb[:, h, :], bank[(h + 1) % 2][:, :], ACT.Copy).then_inc(s_cb, 1)
            for t in range(5):
                for kv in range(2):
                    n = P if t < 4 else TS
                    act.wait_ge(s_rows, R["kv"] + 2 * t + kv + 1)
                    if t == 4:
                        dst = s_row[:, kv, :]
                    elif kv:
                        dst = v_tok[:, t, :]
                    else:
                        if t >= 2:
                            act.wait_ge(s_rowdma, 16 * t)
                        dst = k_row[:, t % 2, :]
                    A(dst, bank[kv][0:n, :], ACT.Copy).then_inc(s_rowsd, 1)

            act.wait_ge(s_qk, 8)
            act.wait_ge(s_rowsd, R["kv"] + 10)
            one = lambda ap: ap.rearrange("p a t -> p (a t)")

            def batch_exps(b, par):
                act.wait_ge(s_sm, b + 1)
                A(pr[:, par, :, :], sc[:, :, :], ACT.Exp).then_inc(s_p, 1)

            def batch(i, bb):
                b = i * 2 + bb

                def turned_p(w):
                    n = (w + 1) * P
                    act.wait_ge(s_ptt, b * 4 + (w + 1))
                    if not (isinstance(b, int) and b * 4 + w < 2):
                        act.wait_ge(s_po, b * 4 + (w - 1))
                    A(pt[:, w % 2, 0:n], pb[3][:, 0:n], ACT.Copy).then_inc(s_ptc, 1)

                for p in range(PG):
                    if p % 4 == 0 and p:
                        turned_p(p // 4 - 1)
                    if not (isinstance(b, int) and b * PG + p < 4):
                        act.wait_ge(s_sp, b * PG + (p - 3))
                    act.wait_ge(s_tr, b * PG + (p + 1))
                    A(kt[:, p % 4, :], pb[p % 2], ACT.Copy).then_inc(s_kt, 1)
                    if bb == 0 and p == 0:
                        A(q_s[:, :], one(qkv[:, ds(i, 1), 0:TP]), ACT.Copy, scale=HD ** -0.5).then_inc(s_qs, 1)
                        A(k_s[:, :], one(qkv[:, ds(i + 4, 1), 0:TP]), ACT.Copy).then_inc(s_qs, 1)
                    if bb == 0 and p == 1:
                        A(v_s[:, :, :], v_tok[:, :, ds(i * P, P)], ACT.Copy).then_inc(s_qs, 1)
                    if p % 4 == 2:
                        w = p // 4
                        n = (w + 1) * P
                        act.wait_ge(s_sb, b * 4 + (w + 1))
                        A(sb[:, w, 0:n], sb[:, w, 0:n], ACT.Exp, bias=rmax[:, w:w + 1],
                          accum_out=rsum[:, w:w + 1]).then_inc(s_pe, 1)
                    if p == 6 and not (isinstance(b, int) and b == 0):
                        batch_exps(b - 1, 1 - bb)
                turned_p(3)
            batch(0, 0)
            batch(0, 1)
            with act.Fori(1, NB // 2) as i:
                batch(i, 0)
                batch(i, 1)
            batch_exps(NB - 1, 1)
            act.wait_ge(s_pod, 4)
            for c in range(4):
                if c == 0:
                    act.wait_ge(s_oev, NB)
                A(h_h[:, 4 + c, :], qkv[:, c, :], ACT.Copy).then_inc(s_hhi, 1)

            act.wait_ge(s_pvp, NB * PG)
            for slot in range(3):
                split_high(ph["out"].slab0 // 4, slot, DC)

            def residual(phase, stage):
                def turn(i, last):
                    for j in range(4):
                        ahead(split_high, phase, i, j, last)
                        if stage in NORM and j % phase.per_group == phase.per_group - 1:
                            m = i * (4 // phase.per_group) + j // phase.per_group
                            norm_work(stage, m, (j // phase.per_group) % 2)
                turns(act, phase, turn, peel=1 if stage in NORM else 0)

            residual(ph["out"], "out")

            def rows_of(n, parts, group, dst):
                act.wait_ge(s_rows, group + 1)
                A(dst, bank[(group) % 2][0:parts, 0:n], ACT.Copy).then_inc(s_rowsd, 1)

            def ffn(l):
                root(SQ["out" if l == 0 else "pw2"])
                for half in range(2):
                    pu, pd = ph[f"up{l}{half}"], ph[f"down{l}{half}"]

                    def turn(i, last):
                        for j in range(4):
                            ahead(split_high, pu, i, j, last)
                            k = i * 2 + (l * FC + half * HALF[0] + j // 2)
                            b = j // 2
                            if j % 2 == 0:
                                act.wait_ge(s_cv, k + 1)
                                if not (isinstance(k, int) and k < 2):
                                    act.wait_ge(s_sr, k - 1)
                                A(sl[:, b, :], cv[:, b, :], ACT.Silu).then_inc(s_sl, 1)
                            else:
                                act.wait_ge(s_free, pu.group(i, j) + 1)
                                apart(i)
                                A(h_h[:, ds(i * 2 + b, 1), :].rearrange("p a t -> p (a t)"), tmp[:, b, :],
                                  ACT.Copy).then_inc(s_hhi, 1)
                    turns(act, pu, turn, peel=1 if l == 0 and half == 0 else 0)
                    if half == 1:
                        for q in range(6):
                            n = min(4, FC - 4 * q) * P
                            rows_of(n, FT, R[f"ffn{l}"] + q, f_row[0:FT, q * 512:q * 512 + n])
                    residual(pd, f"down{l}{half}")

            ffn(0)

            root(SQ["down01"])
            def turn(i, last):
                for j in range(4):
                    ahead(split_high, ph["pw1"], i, j, last)
                    if j % 2:
                        c, b = i * 2 + j // 2, j // 2
                        act.wait_ge(s_free, ph["pw1"].group(i, j) + 1)
                        apart(i)
                        A(sg[:, b, :], sg[:, b, :], ACT.Sigmoid, bias=par("b_pw1", c + DC)).then_inc(s_sig, 1)
            turns(act, ph["pw1"], turn)
            for q in range(2):
                rows_of(512, UT, R["conv_c"] + q, u_row[:, q * 512:q * 512 + 512])
            for m in range(DC):
                act.wait_ge(s_xc, m + 1)
                if m >= 2:
                    act.wait_ge(s_ss, 9 * SUM["var"] + m)
                A(sq[:, m % 2, :], yc[:, m, :], ACT.Square).then_inc(s_sq, 1)
            root(SQ["var"])
            for m in range(DC):
                act.wait_ge(s_ty, m + 1)
                if m >= 2:
                    act.wait_ge(s_hlo, HB["pw2"] + m - 1)
                A(tmp[:, m % 2, :], yc[:, m, :], ACT.Silu, scale=par("ln_g", m), bias=par("ln_b", m)).then_inc(s_s32, 1)
                act.wait_ge(s_s32, m + 1)
                A(h_h[:, m, :], tmp[:, m % 2, :], ACT.Copy).then_inc(s_hhi, 1)
            residual(ph["pw2"], "pw2")
            ffn(1)
            for t in range(5):
                n = P if t < 4 else TS
                for q in range(2):
                    act.wait_ge(s_rows, R["y"] + 2 * t + q + 1)
                    if t >= 2:
                        act.wait_ge(s_rowdma, 16 * (4 + t))
                    A(y_row[0:n, t % 2, q * 512:q * 512 + 512], bank[q][0:n, :], ACT.Copy).then_inc(s_rowsd, 1)

        @block.vector
        def _(dve):
            V = nc.vector
            st = Steps()
            flat = lambda ap: ap.rearrange("p a t -> p (a t)")

            def after():
                dve.wait_ge(s_dve, st.now())

            dve.wait_ge(s_misc, 1)
            V.tensor_copy(params[:, :], bank[0][:, 0:n_rows]).then_inc(s_miscd, 1)
            dve.wait_ge(s_miscd, 1)

            def clear_sum(n):
                if n:
                    dve.wait_ge(s_stat, n)
                V.memset(ssum[:, :], 0.0).then_inc(s_ss, 1)

            def norm_work(stage, m, b):
                name, g0 = GAIN[stage]
                dve.wait_ge(s_sq, m + (8 * SQ[stage] + 1))
                dve.wait_ge(s_ss, m + (9 * SUM[stage] + 1))
                V.tensor_tensor(ssum[:, :], ssum[:, :], sq[:, b, :], ALU.add).then_inc(s_ss, 1)
                dve.wait_ge(s_xhi, m + (8 * NORM[stage] + 1))
                V.scalar_tensor_tensor(flat(xa_l[:, ds(m, 1), :]), flat(x[:, ds(m, 1), :]), par(name, m + g0),
                                       flat(xa_h[:, ds(m, 1), :]).bitcast(F32), ALU.mult, ALU.subtract)\
                 .then_inc(s_xlo, 1)

            def inv_rms(k, n):
                dve.wait_ge(s_stat, n + 1)
                V.tensor_scalar(halves(r_all[:, :]), psum_s[:, :, 0:HT], 1.0 / D, EPS, ALU.mult, ALU.add)\
                 .then_inc(s_var, 1)
                dve.wait_ge(s_rt, k + 1)
                V.reciprocal(r_all[:, :], r_all[:, :]).then_inc(s_r, 1)
                dve.wait_ge(s_r, k + 1)

            def scaled(dst, s, b):
                dve.wait_ge(s_slab, s + 1)
                V.tensor_tensor(halves(dst), gview(b), halves(r_all[:, :]), ALU.mult).then_inc(s_free, 1)

            clear_sum(0)
            for m in range(DC):
                dve.wait_ge(s_tp, m + 1)
                V.tensor_copy(x[:, m, 0:TP], pair[m % 2][:, 0, :]).then_inc(s_dve, 1)
                st.tick()
                V.tensor_copy(x[:, m, TP:T], pair[m % 2][:, 1, 0:TS]).then_inc(s_xnew, 1)
                dve.wait_ge(s_xnew, m + 1)
                after()
                norm_work("init", m, m % 2)
            dve.wait_ge(s_misc, 2)
            V.tensor_copy(ext_a[:, :, :, 0:CA - 1],
                          bank[1][:, 0:8 * NB].rearrange("p (c b t) -> p c b t", c=4, b=NB)).then_inc(s_miscd, 1)
            inv_rms(0, 0)
            for g in range(4):
                scaled(qkv[:, g, :], g, g % 2)
            dve.wait_ge(s_misc, 3)
            V.tensor_copy(lf_k[:, :, :].rearrange("p (s h) g -> p s (h g)", s=2), psum_s[:, :, :]).then_inc(s_miscd, 1)
            V.memset(suf[:, :, PG - 1:PG], 0.0).then_inc(s_dve, 1)
            st.tick()
            dve.wait_ge(s_miscd, 3)
            for p in range(PG - 2, -1, -1):
                after()
                V.tensor_tensor(suf[:, :, p:p + 1], suf[:, :, p + 1:p + 2], lf_k[:, :, p + 1:p + 2], ALU.add)\
                 .then_inc(s_dve if p else s_suf, 1)
                if p:
                    st.tick()
            for g in range(4, 8):
                scaled(qkv[:, g, :], g, g % 2)
            dve.wait_ge(s_misc, 4)
            for half in range(2):
                V.tensor_copy(dk[:, :, :, 4 * half:4 * half + 4].rearrange("p b g h -> p h (b g)"),
                              psum_s[:, half, :].rearrange("p (h g) -> p h g", h=4)).then_inc(s_miscd, 1)
            V.memset(seg[:, :], 1.0).then_inc(s_dve, 1)
            st.tick()
            after()
            V.memset(seg[:, TP:T].rearrange("p (b t) -> p b t", t=NT)[:, :, 0:1], 0.0).then_inc(s_dve, 1)
            st.tick()
            for g in range(8, 12):
                scaled(qkv[:, g, :], g, g % 2)
            dve.wait_ge(s_misc, 5)
            V.tensor_tensor(halves(fz[:, :]), psum_s[0:NH, :, 0:HT], halves(r_all[0:NH, :]), ALU.mult)\
             .then_inc(s_miscd, 1)
            dve.wait_ge(s_miscd, 6)
            V.tensor_scalar(fz[:, :], fz[:, :], b_f, None, ALU.add).then_inc(s_fz, 1)
            dve.wait_ge(s_fe, 3)
            V.scalar_tensor_tensor(logf[:, :], fz[:, :], 0.0, fe[:, :], ALU.min, ALU.subtract).then_inc(s_dve, 1)
            st.tick()
            after()
            V.tensor_tensor_scan(cum[:, :], seg[:, :], logf[:, :], 0.0, ALU.mult, ALU.add).then_inc(s_cum, 1)
            dve.wait_ge(s_cum, 1)
            V.tensor_tensor(cnm[:, :, :], ident[0:NH, 0:NH].unsqueeze(2).to_broadcast([NH, NH, TS]),
                            cum[:, TP:T].unsqueeze(1).to_broadcast([NH, NH, TS]), ALU.mult).then_inc(s_cum, 1)

            def head_norm(c):
                dve.wait_ge(s_misc, 6 + c)
                if c >= 2:
                    dve.wait_ge(s_qk, c - 1)
                V.tensor_scalar(halves(tmp[:, c % 2, :]), psum_s[:, :, 0:HT], 1.0 / HD, EPS, ALU.mult, ALU.add)\
                 .then_inc(s_hv, 1)
                dve.wait_ge(s_hrt, c + 1)
                V.reciprocal(tmp[:, c % 2, :], tmp[:, c % 2, :]).then_inc(s_dve, 1)
                st.tick()
                after()
                V.scalar_tensor_tensor(qkv[:, c, :], qkv[:, c, :], params[:, prow["qk"][0] + c // 4:prow["qk"][0] + c // 4 + 1],
                                       tmp[:, c % 2, :], ALU.mult, ALU.mult).then_inc(s_qk, 1)

            for c in range(4):
                scaled(u4[:, c, :], 12 + c, c % 2)
                head_norm(c)
            for c in range(4):
                scaled(ssum[:, :], 16 + c, c % 2)
                dve.wait_ge(s_free, 17 + c)
                V.tensor_tensor(u4[:, c, :], ssum[:, :], u4[:, c, :], ALU.mult).then_inc(s_dve, 1)
                st.tick()
                after()
                V.tensor_copy(ext_a[:, c, :, CA - 1:], u4[:, c, TP:T].rearrange("p (b t) -> p b t", t=NT))\
                 .then_inc(s_dve, 1)
                st.tick()
                after()
                for tap in range(CA - 1, -1, -1):
                    k = CA - 1 - tap
                    w = params[:, prow["conv_a"][0] + tap * 4 + c:prow["conv_a"][0] + tap * 4 + c + 1]
                    yp, ys = g4[:, c, k:TP], g4[:, c, TP:T].rearrange("p (b t) -> p b t", t=NT)
                    es = ext_a[:, c, :, tap:tap + NT]
                    if k == 0:
                        V.tensor_scalar(yp, u4[:, c, 0:TP], w, None, ALU.mult).then_inc(s_dve, 1)
                        V.tensor_scalar(ys, es, w, None, ALU.mult).then_inc(s_dve, 1)
                    else:
                        V.scalar_tensor_tensor(yp, u4[:, c, 0:TP - k], w, yp, ALU.mult, ALU.add).then_inc(s_dve, 1)
                        V.scalar_tensor_tensor(ys, es, w, ys, ALU.mult, ALU.add).then_inc(s_dve, 1)
                    st.tick()
                    st.tick()
                    after()
                head_norm(4 + c)
            V.tensor_copy(tail_a[:, :, 0:2], u4[:, :, TP - 2:TP]).then_inc(s_tail, 1)
            V.tensor_copy(tail_a[:, :, 2:FT].rearrange("p c (b t) -> p c b t", b=NB), ext_a[:, :, :, NT:])\
             .then_inc(s_tail, 1)
            for c in range(4):
                scaled(ssum[:, :], 20 + c, c % 2)
                dve.wait_ge(s_free, 21 + c)
                V.tensor_tensor(g4[:, c, :], ssum[:, :], g4[:, c, :], ALU.mult).then_inc(s_ya, 1)
                dve.wait_ge(s_hhi, c + 1)
                V.tensor_tensor(h_l[:, c, :], g4[:, c, :], h_h[:, c, :].bitcast(F32), ALU.subtract).then_inc(s_hlo, 1)
                if c == 0:
                    dve.wait_ge(s_misc, 14)
                    V.tensor_copy(cq, bank[0][:, 0:32]).then_inc(s_dve, 1)
                    V.tensor_copy(cns, bank[0][0:TS, 32:40]).then_inc(s_dve, 1)
                    V.tensor_copy(lf_row[:, 0:4, :], bank[0][:, 64:96].rearrange("p (t h) -> p t h", h=NH))\
                     .then_inc(s_dve, 1)
                    for _ in range(3):
                        st.tick()
                    V.tensor_copy(lf_row[0:TS, 4, :], bank[0][0:TS, 96:104]).then_inc(s_miscd, 1)
                if c == 1:
                    dve.wait_ge(s_misc, 15)
                    V.tensor_copy(cn_all[:, :, :, :].rearrange("p h b t -> p (h b t)"), bank[1][:, 0:NH * TS])\
                     .then_inc(s_miscd, 1)
            dve.wait_ge(s_misc, 16)
            V.tensor_copy(a_out[:, :], bank[0][0:FT, :]).then_inc(s_miscd, 1)
            for h in range(NH):
                if h >= 2:
                    dve.wait_ge(s_cbp, h - 1)
                V.tensor_scalar(cmask[:, h % 2, :], cum[:, 0:TP], ident[0:NH, h:h + 1], None, ALU.mult).then_inc(s_cm, 1)
            dve.wait_ge(s_qk, 8)
            for c in range(4):
                for hh in range(2):
                    V.tensor_scalar(q_diag[HD * hh:HD * hh + HD, c, :, NT * hh:NT * hh + NT],
                                    qkv[HD * hh:HD * hh + HD, c, TP:T].rearrange("p (b t) -> p b t", t=NT),
                                    HD ** -0.5, None, ALU.mult).then_inc(s_qd, 1)
            V.tensor_tensor(nbias[:, :, :, :], nbias[:, :, :, :],
                            cns.unsqueeze(1).unsqueeze(3).to_broadcast([TS, NB, NH, NT]), ALU.subtract)\
             .then_inc(s_dve, 1)
            st.tick()
            after()
            def attended(i):
                dve.wait_ge(s_po, i * 8 + 8)
                V.tensor_scalar(flat(qkv[:, ds(i, 1), 0:TP]), psum_s[:, 1, :], 1.0, None, ALU.mult).then_inc(s_pod, 1)

            def bias(b, w):
                n = (w + 1) * P
                dve.wait_ge(s_s, b * 4 + (w + 1))
                V.scalar_tensor_tensor(sb[:, w, 0:n], pb[2][:, 0:n], small[:, ds(b + (160 + w * NH), 1)],
                                       flat(cb[:, ds(b, 1), 0:n]), ALU.add, ALU.subtract).then_inc(s_sbr, 1)
                dve.wait_ge(s_sbr, b * 4 + (w + 1))
                V.tensor_tensor(sb[:, w, n - P:n], sb[:, w, n - P:n], causal[:, :], ALU.add).then_inc(s_dve, 1)
                st.tick()
                after()
                V.tensor_reduce(rmax[:, w:w + 1], sb[:, w, 0:n], AX.X, ALU.max, negate=True).then_inc(s_sb, 1)

            def norm(b, w):
                n = (w + 1) * P
                dve.wait_ge(s_pe, b * 4 + (w + 1))
                V.reciprocal(rinv[:, w:w + 1], rsum[:, w:w + 1]).then_inc(s_dve, 1)
                st.tick()
                after()
                V.tensor_scalar(sb[:, w, 0:n], sb[:, w, 0:n], rinv[:, w:w + 1], None, ALU.mult).then_inc(s_pn, 1)

            wide = lambda ap, n: ap.unsqueeze(1).to_broadcast([P, n, 32])

            def logits(b):
                dve.wait_ge(s_sc, b + 1)
                V.tensor_tensor(sc[:, 0:PG, :].rearrange("p g (h q) -> p (g h) q", q=NT),
                                psum_s[:, 0, :].rearrange("p (g q) -> p g q", q=NT),
                                dk[:, ds(b, 1), :, :].rearrange("p b g h -> p (b g h)").unsqueeze(2)
                                .to_broadcast([P, PG * NH, NT]), ALU.add).then_inc(s_dve, 1)
                st.tick()
                V.tensor_tensor(sc[0:TS, PG, :], bank[1][0:TS, 256:288],
                                nbias[:, ds(b, 1), :, :].rearrange("p b h q -> p (b h q)"), ALU.add).then_inc(s_sev, 1)
                dve.wait_ge(s_sev, b + 1)
                after()
                V.tensor_tensor(sc[:, :, :].rearrange("p g (h q) -> p g h q", q=NT),
                                sc[:, :, :].rearrange("p g (h q) -> p g h q", q=NT),
                                cn_all[:, :, ds(b, 1), :].rearrange("p h b t -> p (h b) t").unsqueeze(1)
                                .to_broadcast([P, PG + 1, NH, NT]), ALU.add).then_inc(s_dve, 1)
                st.tick()
                after()
                V.tensor_reduce(m1, sc[:, :, :].rearrange("p g x -> p x g"), AX.X, ALU.max).then_inc(s_m1, 1)

            def biggest(b):
                dve.wait_ge(s_mt, b + 1)
                V.tensor_reduce(gmax, bank[1][0:32, 0:P], AX.X, ALU.max).then_inc(s_dve, 1)
                st.tick()
                after()
                V.tensor_scalar(diag, ident[0:32, 0:32], gmax, None, ALU.mult).then_inc(s_dg, 1)

            def shift(b):
                dve.wait_ge(s_mb, b + 1)
                V.tensor_tensor(sc[:, :, :], sc[:, :, :], wide(bank[1][:, P:P + 32], PG + 1), ALU.subtract)\
                 .then_inc(s_sm, 1)

            def total(b, par):
                dve.wait_ge(s_p, b + 1)
                V.tensor_reduce(p_sum, pr[:, par, :, :].rearrange("p g x -> p x g"), AX.X, ALU.add).then_inc(s_lp, 1)

            def inverse(b):
                dve.wait_ge(s_l, b + 1)
                if not (isinstance(b, int) and b == 0):
                    dve.wait_ge(s_oev, b)
                V.reciprocal(rec, bank[1][:, 192:224]).then_inc(s_rec, 1)

            def values(b):
                dve.wait_ge(s_pvp, b * PG + PG)
                dve.wait_ge(s_rec, b + 1)
                for hh in range(2):
                    rows = slice(HD * hh, HD * hh + HD)
                    V.tensor_tensor(qkv[rows, 0:4, ds(b * NT + TP, NT)],
                                    bank[0][rows, 0:32].rearrange("p (c x) -> p c x", c=4)[:, :, NT * hh:NT * hh + NT],
                                    rec[rows, :].rearrange("p (c x) -> p c x", c=4)[:, :, NT * hh:NT * hh + NT],
                                    ALU.mult).then_inc(s_oev if hh else s_dve, 1)
                    if not hh:
                        st.tick()
            dve.wait_ge(s_aout, 32)

            def batch(i, bb):
                b = i * 2 + bb
                known = isinstance(b, int)
                if bb == 0 and not known:
                    attended(i - 1)
                bias(b, 0)
                if not (known and b == 0):
                    biggest(b - 1)
                norm(b, 0)
                if not (known and b == 0):
                    shift(b - 1)
                bias(b, 1)
                norm(b, 1)
                if not (known and b == 0):
                    total(b - 1, 1 - bb)
                if not known:
                    values(b - 2)
                if not (known and b == 0):
                    inverse(b - 1)
                for w in (2, 3):
                    bias(b, w)
                    norm(b, w)
                logits(b)
            batch(0, 0)
            batch(0, 1)
            with st.loop(dve, 1, NB // 2, 24) as i:
                batch(i, 0)
                batch(i, 1)
            attended(3)
            biggest(NB - 1)
            shift(NB - 1)
            total(NB - 1, 1)
            values(NB - 2)
            inverse(NB - 1)
            values(NB - 1)
            after()
            for c in range(4):
                dve.wait_ge(s_hhi, 5 + c)
                V.tensor_tensor(h_l[:, 4 + c, :], qkv[:, c, :], h_h[:, 4 + c, :].bitcast(F32), ALU.subtract)\
                 .then_inc(s_hlo, 1)

            def residual(phase, stage):
                if stage in NORM:
                    clear_sum(SUM[stage])
                per_turn = 4 // phase.per_group
                with dve.Fori(0, phase.turns) as i:
                    for q in range(per_turn):
                        m = i * per_turn + q
                        dve.wait_ge(s_slab, phase.slab(i, (q + 1) * phase.per_group - 1) + 1)
                        V.tensor_tensor(halves(flat(x[:, ds(m, 1), :])), gview(q % 2), halves(flat(x[:, ds(m, 1), :])),
                                        ALU.add).then_inc(s_xnew, 1)
                        dve.wait_ge(s_xnew, m + (XN[stage] + 1))
                        if stage in NORM:
                            norm_work(stage, m, q % 2)

            residual(ph["out"], "out")

            def ffn(l):
                dve.wait_ge(s_fst, 1 + 5 * l)
                V.tensor_copy(ext_f[:, :, :, 0:CF - 1].rearrange("p c b t -> p c b t"),
                              bank[0][:, 0:FC * 2 * NB].rearrange("p (c b t) -> p c b t", c=FC, b=NB)).then_inc(s_fstd, 1)
                dve.wait_ge(s_fstd, 1 + 5 * l)
                inv_rms(SQ["out" if l == 0 else "pw2"], SUM["out" if l == 0 else "pw2"])
                for half in range(2):
                    pu, pd = ph[f"up{l}{half}"], ph[f"down{l}{half}"]
                    with st.loop(dve, 0, pu.turns, 2 * 6) as i:
                        for b in range(2):
                            kc = i * 2 + (half * HALF[0] + b)
                            k = i * 2 + (half * HALF[0] + b + HB[f"up{l}"])
                            e = lambda lo, hi: ext_f[:, ds(kc, 1), :, lo:hi].rearrange("p a b t -> p (a b) t")
                            scaled(gate[:, b, :], pu.slab(i, 2 * b), 0)
                            dve.wait_ge(s_free, pu.group(i, 2 * b) + 1)
                            V.tensor_copy(e(CF - 1, CF - 1 + NT), gate[:, b, TP:T].rearrange("p (b t) -> p b t", t=NT))\
                             .then_inc(s_dve, 1)
                            st.tick()
                            V.tensor_copy(flat(tail_f[:, ds(kc, 1), 0:2]), gate[:, b, TP - 2:TP]).then_inc(s_tail, 1)
                            after()
                            ys = cv[:, b, TP:T].rearrange("p (b t) -> p b t", t=NT)
                            for tap in range(CF - 1, -1, -1):
                                n = CF - 1 - tap
                                w = par("conv_f", kc + (l * CF * FC + tap * FC))
                                yp = cv[:, b, n:TP]
                                if n == 0:
                                    V.tensor_scalar(yp, gate[:, b, 0:TP], w, None, ALU.mult).then_inc(s_dve, 1)
                                    st.tick()
                                    V.tensor_scalar(ys, e(tap, tap + NT), w, None, ALU.mult).then_inc(s_dve, 1)
                                    st.tick()
                                    after()
                                    continue
                                V.scalar_tensor_tensor(yp, gate[:, b, 0:TP - n], w, yp, ALU.mult, ALU.add)\
                                 .then_inc(s_dve, 1)
                                st.tick()
                                if n < CF - 1:
                                    V.scalar_tensor_tensor(ys, e(tap, tap + NT), w, ys, ALU.mult, ALU.add)\
                                     .then_inc(s_dve, 1)
                                    st.tick()
                                    after()
                                else:
                                    V.scalar_tensor_tensor(ys, e(tap, tap + NT), w, ys, ALU.mult, ALU.add)\
                                     .then_inc(s_cv, 1)
                            dve.wait_ge(s_slab, pu.slab(i, 2 * b + 1) + 1)
                            dve.wait_ge(s_sr, i * 2 + (l * FC + half * HALF[0] + b + 1))
                            V.tensor_tensor(halves(tmp[:, b, :]), gview(1), halves(sr[:, b, :]), ALU.mult).then_inc(s_free, 1)
                            dve.wait_ge(s_hhi, k + 1)
                            V.tensor_tensor(flat(h_l[:, ds(i * 2 + b, 1), :]), tmp[:, b, :],
                                            flat(h_h[:, ds(i * 2 + b, 1), :]).bitcast(F32), ALU.subtract).then_inc(s_hlo, 1)
                    if half == 1:
                        V.tensor_copy(tail_f[:, :, 2:FT].rearrange("p c (b t) -> p c b t", b=NB), ext_f[:, :, :, NT:])\
                         .then_inc(s_tail, 1)
                    residual(pd, f"down{l}{half}")

            ffn(0)

            for q in range(4):
                dve.wait_ge(s_fst, 2 + q)
                V.tensor_copy(ext_c[:, 2 * q:2 * q + 2, :, 0:CC - 1],
                              bank[q % 2][:, 0:480].rearrange("p (c b t) -> p c b t", c=2, b=NB)).then_inc(s_fstd, 1)
            inv_rms(SQ["down01"], SUM["down01"])
            clear_sum(SUM["mean"])
            dve.wait_ge(s_out, 16 * n_out[1])
            taps = params[:, prow["conv_c"][0]:prow["conv_c"][0] + CC * DC].rearrange("p (k c) -> p c k", c=DC)
            with st.loop(dve, 0, ph["pw1"].turns, 2 * (CC + 8)) as i:
                for b in range(2):
                    c = i * 2 + b
                    ue = lambda lo, hi: ext_c[:, ds(c, 1), :, lo:hi].rearrange("p a b t -> p (a b) t")
                    scaled(ua[:, b, :], ph["pw1"].slab(i, 2 * b), 0)
                    dve.wait_ge(s_slab, ph["pw1"].slab(i, 2 * b + 1) + 1)
                    V.tensor_tensor(halves(sg[:, b, :]), gview(1), halves(r_all[:, :]), ALU.mult).then_inc(s_free, 1)
                    dve.wait_ge(s_sig, c + 1)
                    V.scalar_tensor_tensor(u[:, b, :], ua[:, b, :], par("b_pw1", c), sg[:, b, :], ALU.add, ALU.mult)\
                     .then_inc(s_u, 1)
                    dve.wait_ge(s_u, c + 1)
                    V.tensor_copy(flat(tail_c[:, ds(c, 1), :]), u[:, b, T - UT:T]).then_inc(s_ux, 1)
                    V.tensor_copy(ue(CC - 1, CC - 1 + NT), u[:, b, TP:T].rearrange("p (b t) -> p b t", t=NT))\
                     .then_inc(s_dve, 1)
                    st.tick()
                    after()
                    for t in range(NT):
                        V.tensor_tensor(prod[:, :, :].rearrange("p (b t) k -> p b t k", t=NT)[:, :, t, :],
                                        ue(t, t + CC), taps[:, ds(c, 1), :].to_broadcast([P, NB, CC]), ALU.mult)\
                         .then_inc(s_dve, 1)
                        st.tick()
                    after()
                    V.tensor_reduce(flat(yc[:, ds(c, 1), TP:T]), prod[:, :, :], AX.X, ALU.add).then_inc(s_dve, 1)
                    st.tick()
                    after()
                    V.tensor_scalar(flat(yc[:, ds(c, 1), TP:T]), flat(yc[:, ds(c, 1), TP:T]), par("conv_cb", c), None,
                                    ALU.add).then_inc(s_dve, 1)
                    st.tick()
                    for tap in range(CC - 1, -1, -1):
                        n = CC - 1 - tap
                        w = par("conv_c", c + tap * DC)
                        yp = tmp[:, b, n:TP] if n % 2 else flat(yc[:, ds(c, 1), n:TP])
                        if n == 0:
                            V.tensor_scalar(yp, u[:, b, 0:TP], w, par("conv_cb", c), ALU.mult, ALU.add).then_inc(s_dve, 1)
                        elif n == 1:
                            V.tensor_scalar(yp, u[:, b, 0:TP - n], w, None, ALU.mult).then_inc(s_dve, 1)
                        else:
                            dve.wait_ge(s_dve, st.now() - 1)
                            V.scalar_tensor_tensor(yp, u[:, b, 0:TP - n], w, yp, ALU.mult, ALU.add).then_inc(s_dve, 1)
                        st.tick()
                    after()
                    V.tensor_tensor(flat(yc[:, ds(c, 1), 1:TP]), flat(yc[:, ds(c, 1), 1:TP]), tmp[:, b, 1:TP], ALU.add)\
                     .then_inc(s_dve, 1)
                    st.tick()
                    after()
                    dve.wait_ge(s_ss, c + (9 * SUM["mean"] + 1))
                    V.tensor_tensor(ssum[:, :], ssum[:, :], flat(yc[:, ds(c, 1), :]), ALU.add).then_inc(s_ss, 1)
            dve.wait_ge(s_stat, SUM["mean"] + 1)
            V.tensor_scalar(halves(r_all[:, :]), psum_s[:, :, 0:HT], 1.0 / D, None, ALU.mult).then_inc(s_mu, 1)
            dve.wait_ge(s_mu, 1)
            clear_sum(SUM["var"])
            def add_squares(m):
                dve.wait_ge(s_sq, 8 * SQ["var"] + m + 1)
                dve.wait_ge(s_ss, 9 * SUM["var"] + m + 1)
                V.tensor_tensor(ssum[:, :], ssum[:, :], sq[:, m % 2, :], ALU.add).then_inc(s_ss, 1)
            for m in range(DC):
                V.tensor_tensor(yc[:, m, :], yc[:, m, :], r_all[:, :], ALU.subtract).then_inc(s_xc, 1)
                if m:
                    add_squares(m - 1)
            add_squares(DC - 1)
            inv_rms(SQ["var"], SUM["var"])
            for m in range(DC + 1):
                if m < DC:
                    dve.wait_ge(s_xc, m + 1)
                    V.tensor_tensor(yc[:, m, :], yc[:, m, :], r_all[:, :], ALU.mult).then_inc(s_ty, 1)
                if m:
                    dve.wait_ge(s_hhi, HB["pw2"] + m)
                    V.tensor_tensor(h_l[:, m - 1, :], tmp[:, (m - 1) % 2, :], h_h[:, m - 1, :].bitcast(F32), ALU.subtract)\
                     .then_inc(s_hlo, 1)
            residual(ph["pw2"], "pw2")
            ffn(1)

        @block.tensor
        def _(pe):
            mm, tr = nc.tensor.matmul, nc.tensor.transpose
            xa = lambda t: (xa_h[:, t, :], xa_l[:, t, :])
            hid = lambda t: (h_h[:, t, :], h_l[:, t, :])

            def slab(phase, i, j, moving, ready=None):
                first, last = j % phase.per_group == 0, j % phase.per_group == phase.per_group - 1
                s, g = phase.slab(i, j), phase.group(i, j)
                pe.wait_ge(s_lo, s + 1)
                if first:
                    bank_free(phase, i, j // phase.per_group, g)
                out = pair[(j // phase.per_group) % 2]
                for t in range(phase.tiles):
                    k = t + (0 if first else phase.tiles)
                    if ready:
                        ready(k)
                    hi, lo = moving(k)
                    wh, wl = w_h[:, j, t * P:(t + 1) * P], w_l[:, j, t * P:(t + 1) * P]
                    for n, (w, v) in enumerate(((wh, hi), (wh, lo), (wl, hi))):
                        for half in range(2):
                            ins = mm(out[:, half, 0:HT], w, v[:, half * HT:(half + 1) * HT],
                                     start=first and t == 0 and n == 0,
                                     stop=last and t == phase.tiles - 1 and n == 2)
                ins.then_inc(s_slab, 1)

            def bank_free(phase, i, q, g):
                if isinstance(i, int) and i == 0 and q < 2:
                    if phase is not order[0]:
                        before = order[order.index(phase) - 1]
                        pe.wait_ge(s_xnew if before.residual else s_free, before.group1 - 1 + q)
                else:
                    pe.wait_ge(s_xnew if phase.residual else s_free, g - 1)

            def sum_channels():
                for half in range(2):
                    ins = mm(psum_s[:, half, 0:HT], ones[:, :], ssum[:, half * HT:(half + 1) * HT], start=True, stop=True)
                ins.then_inc(s_stat, 1)

            pe.wait_ge(s_cst, 15)
            pe.wait_ge(s_prm, 16 * (4 + sum(len(row_blocks(*v)) for name, v in prow.items() if name != "qk")))
            for blk in range(4):
                n = min(P, n_rows - blk * P)
                ins = tr(bank[0][:, blk * P:blk * P + n], p_rows[0:n, blk, :], ident[0:n, 0:n])
            ins.then_inc(s_misc, 1)
            pe.wait_ge(s_xld, 16 * 5)
            for m in range(DC):
                if m >= 2:
                    pe.wait_ge(s_xnew, m - 1)
                for t in range(4):
                    tr(pair[m % 2][:, 0, t * P:(t + 1) * P], x_rows[:, t, m * P:(m + 1) * P], ident[:, :])
                tr(pair[m % 2][:, 1, 0:TS], x_rows[0:TS, 4, m * P:(m + 1) * P], ident[0:TS, 0:TS]).then_inc(s_tp, 1)
            pe.wait_ge(s_st, 16)
            for c in range(4):
                ins = tr(bank[1][:, c * 2 * NB:(c + 1) * 2 * NB], a_row[:, c * P:(c + 1) * P], ident[0:2 * NB, 0:2 * NB])
            ins.then_inc(s_misc, 1)
            pe.wait_ge(s_xnew, DC)

            p = ph["qkv"]
            for i in range(3):
                for j in range(4):
                    slab(p, i, j, xa, (lambda k: pe.wait_ge(s_xlo, k + 1)) if i == j == 0 else None)
                    if i == j == 0:
                        pe.wait_ge(s_ss, 9)
                        sum_channels()
                if i == 0:
                    pe.wait_ge(s_lf, 16)
                    pe.wait_ge(s_var, 1)
                    for h in range(NH):
                        ins = tr(psum_s[:, h // 4, (h % 4) * P:(h % 4 + 1) * P],
                                 lf_pg[:, :].rearrange("p (k h) -> p h k", h=NH)[:, h, :], ident[:, :])
                    ins.then_inc(s_misc, 1)
                if i == 1:
                    pe.wait_ge(s_miscd, 3)
                    pe.wait_ge(s_suf, 1)
                    lf2, suf2 = (ap[:, :, :].rearrange("p h g -> p (h g)") for ap in (lf_k, suf))
                    for half in range(2):
                        at = slice(half * 512, half * 512 + 512)
                        mm(psum_s[:, half, :], later[:, :], lf2[:, at], start=True, stop=False)
                        ins = mm(psum_s[:, half, :], ones[:, :], suf2[:, at], start=False, stop=True)
                    ins.then_inc(s_misc, 1)
            pe.wait_ge(s_fw, 34)
            pe.wait_ge(s_miscd, 5)
            for t in range(DC):
                for n, (w, v) in enumerate(((fw_h, xa_h), (fw_h, xa_l), (fw_l, xa_h))):
                    for half in range(2):
                        ins = mm(psum_s[0:NH, half, 0:HT], w[:, t, :], v[:, t, half * HT:(half + 1) * HT],
                                 start=t == 0 and n == 0, stop=t == DC - 1 and n == 2)
            ins.then_inc(s_misc, 1)
            p = ph["gates"]
            for i in range(3):
                for j in range(4):
                    slab(p, i, j, xa)
                    c = 4 * i + j
                    if c < 8:
                        pe.wait_ge(s_qsq, c + 1)
                        if c:
                            pe.wait_ge(s_hv, c)
                        else:
                            pe.wait_ge(s_miscd, 6)
                        for half in range(2):
                            ins = mm(psum_s[:, half, 0:HT], head_ones[:, :], sq[:, c % 2, half * HT:(half + 1) * HT],
                                     start=True, stop=True)
                        ins.then_inc(s_misc, 1)
                    if c == 8:
                        pe.wait_ge(s_cum, 1)
                        pe.wait_ge(s_miscd, 2)
                        for t in range(4):
                            tr(bank[0][:, t * NH:(t + 1) * NH], cum[:, t * P:(t + 1) * P], ident[0:NH, 0:NH])
                            tr(bank[0][:, 64 + t * NH:64 + (t + 1) * NH], logf[:, t * P:(t + 1) * P], ident[0:NH, 0:NH])
                        tr(bank[0][0:TS, 32:40], cum[:, TP:T], ident[0:NH, 0:NH])
                        tr(bank[0][0:TS, 96:104], logf[:, TP:T], ident[0:NH, 0:NH]).then_inc(s_misc, 1)
                    if c == 9:
                        pe.wait_ge(s_cum, 2)
                        mm(bank[1][:, 0:NH * TS], ones[0:NH, :], cnm[:, :, :].rearrange("p h t -> p (h t)"),
                           start=True, stop=True).then_inc(s_misc, 1)
            pe.wait_ge(s_tail, 2)
            pe.wait_ge(s_miscd, 7)
            for c in range(4):
                ins = tr(bank[0][0:FT, c * P:(c + 1) * P], tail_a[:, c, :], ident[:, :])
            ins.then_inc(s_misc, 1)
            for h in range(NH):
                pe.wait_ge(s_cm, h + 1)
                pe.wait_ge(s_miscd, 8 if h == 0 else 9)
                if h >= 2:
                    pe.wait_ge(s_cb, h - 1)
                mm(bank[(h + 1) % 2][:, :], ones[0:NH, :], cmask[:, h % 2, :], start=True, stop=True).then_inc(s_cbp, 1)
            pe.wait_ge(s_qk, 8)
            pe.wait_ge(s_cb, NH)
            for t in range(5):
                for kv in range(2):
                    n = P if t < 4 else TS
                    if t:
                        pe.wait_ge(s_rowsd, 2 * t + kv - 1)
                    for c in range(4):
                        ins = tr(bank[kv][0:n, c * P:(c + 1) * P], qkv[:, 4 + 4 * kv + c, t * P:t * P + n], ident[:, :])
                    ins.then_inc(s_rows, 1)

            pe.wait_ge(s_rowsd, R["kv"] + 10)
            pe.wait_ge(s_free, ph["gates"].group1)

            def p_score(b, bb, w):
                n = (w + 1) * P
                rows = slice(HD * bb, HD * bb + HD)
                mm(pb[2][:, 0:n], q_s[rows, w * P:(w + 1) * P], k_s[rows, 0:n], start=True, stop=True).then_inc(s_s, 1)

            def p_turn(b, w):
                pe.wait_ge(s_pn, b * 4 + (w + 1))
                for kb in range(w + 1):
                    ins = tr(pb[3][:, kb * P:(kb + 1) * P], sb[:, w, kb * P:(kb + 1) * P], ident[:, :])
                ins.then_inc(s_ptt, 1)

            def p_value(b, bb, w):
                pe.wait_ge(s_ptc, b * 4 + (w + 1))
                rows = slice(HD * bb, HD * bb + HD)
                for kb in range(w + 1):
                    ins = mm(psum_s[rows, 1, w * P:(w + 1) * P], v_s[:, kb, rows], pt[:, w % 2, kb * P:(kb + 1) * P],
                             start=kb == 0, stop=kb == w)
                ins.then_inc(s_po, 1)

            pe.wait_ge(s_qd, 8)

            def turn_page(b, p):
                pe.wait_ge(s_k[p % KS], b * 32 + 16 * (p // KS + 1))
                for c in range(4):
                    ins = tr(pb[p % 2][:, c * P:(c + 1) * P], k_pg[:, p % KS, c * P:(c + 1) * P], ident[:, :])
                ins.then_inc(s_tr, 1)

            def score_page(b, p):
                pe.wait_ge(s_kt, b * PG + (p + 1))
                for c in range(4):
                    ins = mm(psum_s[:, 0, p * 32 + c * 8:p * 32 + c * 8 + 8], kt[:, p % 4, c * P:(c + 1) * P],
                             q_diag[:, c, ds(b, 1), :].rearrange("p a x -> p (a x)"), start=True, stop=True)
                ins.then_inc(s_sp, 1)

            def max_turn(b):
                pe.wait_ge(s_m1, b + 1)
                tr(bank[1][0:32, 0:P], m1, ident[:, :]).then_inc(s_mt, 1)

            def max_spread(b):
                pe.wait_ge(s_dg, b + 1)
                mm(bank[1][:, P:P + 32], ones[0:32, :], diag, start=True, stop=True).then_inc(s_mb, 1)

            def exp_sums(b):
                pe.wait_ge(s_lp, b + 1)
                mm(bank[1][:, 192:224], ones[:, :], p_sum, start=True, stop=True).then_inc(s_l, 1)

            def value_new(b, par):
                if not (isinstance(b, int) and b == 0):
                    pe.wait_ge(s_oev, b)
                for c in range(4):
                    mm(bank[0][:, c * 8:c * 8 + 8], s_row[:, 1, c * P:(c + 1) * P], pr[0:TS, par, PG, c * 8:c * 8 + 8],
                       start=c == 0, stop=False, skip_group_check=True)

            def value_page(b, par, p):
                pe.wait_ge(s_v[p], b * 16 + 16)
                for c in range(4):
                    ins = mm(bank[0][:, c * 8:c * 8 + 8], v_pg[:, p, c * P:(c + 1) * P], pr[:, par, p, c * 8:c * 8 + 8],
                             start=False, stop=p == PG - 1, skip_group_check=True)
                ins.then_inc(s_pvp, 1)

            def batch(i, bb):
                b = i * 2 + bb
                known = isinstance(b, int)
                before = not (known and b == 0)
                for p in range(PG):
                    if before and p == 2:
                        max_turn(b - 1)
                    if before and p == 4:
                        max_spread(b - 1)
                    if before and p == 8:
                        exp_sums(b - 1)
                    turn_page(b, p)
                    if p < 8 and not known:
                        value_page(b - 2, bb, p + 8)
                    if p >= 8 and before:
                        if p == 8:
                            value_new(b - 1, 1 - bb)
                        value_page(b - 1, 1 - bb, p - 8)
                    if p == 1 and before:
                        pe.wait_ge(s_sev, b)
                    if p:
                        score_page(b, p - 1)
                    if p % 4 == 0 and p:
                        if p == 4 and bb == 0:
                            pe.wait_ge(s_qs, i * 3 + 3)
                            if not known:
                                pe.wait_ge(s_pod, i)
                        p_value(b, bb, p // 4 - 1)
                    if p % 4 == 1:
                        if p == 1 and bb == 0:
                            pe.wait_ge(s_qs, i * 3 + 2)
                        p_score(b, bb, p // 4)
                    if p % 4 == 3:
                        p_turn(b, p // 4)
                score_page(b, PG - 1)
                for c in range(4):
                    ins = mm(bank[1][0:TS, 256 + c * 8:256 + c * 8 + 8], qkv[:, 4 + c, TP:T],
                             q_diag[:, c, ds(b, 1), :].rearrange("p a x -> p (a x)"), start=True, stop=True)
                ins.then_inc(s_sc, 1)
                p_value(b, bb, 3)

            batch(0, 0)
            batch(0, 1)
            with pe.Fori(1, NB // 2) as i:
                batch(i, 0)
                batch(i, 1)
            max_turn(NB - 1)
            for p in range(4):
                value_page(NB - 2, 0, 8 + p)
            max_spread(NB - 1)
            for p in range(4, 8):
                value_page(NB - 2, 0, 8 + p)
            exp_sums(NB - 1)
            value_new(NB - 1, 1)
            for p in range(PG):
                value_page(NB - 1, 1, p)

            def gemm(phase, moving, ready, between=None):
                seen = set()

                def once(k):
                    if k not in seen:
                        seen.add(k)
                        ready(k)
                for j in range(4):
                    slab(phase, 0, j, moving, once)
                    if j == 0 and between:
                        between()
                with pe.Fori(1, phase.turns) as i:
                    for j in range(4):
                        slab(phase, i, j, moving)

            def sums(n):
                def go():
                    pe.wait_ge(s_ss, 9 * n + 9)
                    sum_channels()
                return go
            low_ready = lambda base: lambda k: pe.wait_ge(s_hlo, base + k + 1)
            xa_ready = lambda n: lambda k: pe.wait_ge(s_xlo, 8 * n + k + 1)

            gemm(ph["out"], hid, low_ready(HB["out"]))

            def rows_out(group, src, parts, n, busy):
                if busy:
                    pe.wait_ge(s_rowsd, group - 1)
                for c in range(n):
                    ins = tr(bank[group % 2][0:parts, c * P:(c + 1) * P], src(c), ident[:, :])
                ins.then_inc(s_rows, 1)

            def ffn(l):
                pe.wait_ge(s_st, 16 * (2 if l == 0 else 5))
                for c in range(FC):
                    ins = tr(bank[0][:, c * 2 * NB:(c + 1) * 2 * NB], f_row[0:2 * NB, c * P:(c + 1) * P],
                             ident[0:2 * NB, 0:2 * NB])
                ins.then_inc(s_fst, 1)
                n = "out" if l == 0 else "pw2"
                for half in range(2):
                    gemm(ph[f"up{l}{half}"], xa, xa_ready(NORM[n]), sums(SUM[n]) if half == 0 else None)
                    if half == 1:
                        pe.wait_ge(s_tail, 2 + (l + 1) * (FC + 1))
                        for q in range(6):
                            rows_out(R[f"ffn{l}"] + q, lambda c: tail_f[:, 4 * q + c, :], FT, min(4, FC - 4 * q), q >= 2)
                    gemm(ph[f"down{l}{half}"], hid, low_ready(HB[f"up{l}"] + half * HALF[0]))

            ffn(0)
            pe.wait_ge(s_st, 16 * 4)
            for q in range(4):
                if q >= 2:
                    pe.wait_ge(s_fstd, 1 + q - 1)
                for c in range(2):
                    for k in range(2):
                        ins = tr(bank[q % 2][:, c * 240 + k * 120:c * 240 + k * 120 + 120],
                                 c_row[:, k, (2 * q + c) * P:(2 * q + c + 1) * P], ident[0:120, 0:120])
                ins.then_inc(s_fst, 1)
            gemm(ph["pw1"], xa, xa_ready(NORM["down01"]), sums(SUM["down01"]))
            pe.wait_ge(s_ux, DC)
            for q in range(2):
                rows_out(R["conv_c"] + q, lambda c: tail_c[:, 4 * q + c, :], UT, 4, False)
            pe.wait_ge(s_ss, 9 * SUM["mean"] + 9)
            sum_channels()
            pe.wait_ge(s_ss, 9 * SUM["var"] + 9)
            sum_channels()
            gemm(ph["pw2"], hid, low_ready(HB["pw2"]))
            ffn(1)
            pe.wait_ge(s_xnew, XN["down11"] + DC)
            for t in range(5):
                n = P if t < 4 else TS
                for q in range(2):
                    if t:
                        pe.wait_ge(s_rowsd, R["y"] + 2 * t + q - 1)
                    for c in range(4):
                        ins = tr(bank[q][0:n, c * P:(c + 1) * P], x[:, 4 * q + c, t * P:t * P + n], ident[:, :])
                    ins.then_inc(s_rows, 1)


_INS = ["x_prompt", "x_sample", "cache_k", "cache_v", "cache_logf", "page_table", "state_conv_a", "state_conv_c",
        "state_ffn", "norm_mix0", "w_in0", "b_forget", "conv_a_w", "q_norm", "k_norm", "w_out0", "norm_mix1",
        "w_pw1", "b_pw1", "conv_c_w", "conv_c_b", "ln_c_g", "ln_c_b", "w_pw2", "norm_ffn", "w_up", "conv_ffn_w",
        "w_down"]
_OUTS = [("y_prompt", (1, TP, D)), ("y_sample", (NB, NT, D)),
         ("p_conv_a", (1, 1, 2, 512)), ("s_conv_a", (1, NB, 2, 512)),
         ("p_k", (1, 1, TP, NH, HD)), ("s_k", (1, NB, NT, NH, HD)),
         ("p_v", (1, 1, TP, NH, HD)), ("s_v", (1, NB, NT, NH, HD)),
         ("p_logf", (1, 1, TP, NH)), ("s_logf", (1, NB, NT, NH)),
         ("p_conv_c", (1, 1, CC - 1, D)), ("s_conv_c", (1, NB, CC - 1, D)),
         ("p_ffn", (2, 1, 2, DFF)), ("s_ffn", (2, NB, 2, DFF))]


def kernel(**inputs):
    import numpy as np
    import concourse.bacc as bacc
    from concourse.bass_utils import run_bass_kernel_spmd

    nc = bacc.Bacc("TRN2", target_bir_lowering=False, num_devices=1, dynamic_dma_scratch_size=SCRATCH)
    arrays, a, o = {}, {}, {}
    for name in _INS:
        v = np.ascontiguousarray(inputs[name])
        arrays[f"in_{name}"] = v
        a[name] = nc.dram_tensor(f"in_{name}", v.shape, mybir.dt.from_np(v.dtype), kind="ExternalInput").ap()
    for name, shape in _OUTS:
        o[name] = nc.dram_tensor(f"out_{name}", shape, F32, kind="ExternalOutput").ap()
    build(nc, a, o)
    r = run_bass_kernel_spmd(nc, [arrays], core_ids=[0])
    return tuple(r.results[0][f"out_{name}"] for name, _ in _OUTS)
```

```python
from contextlib import ExitStack, contextmanager

import concourse.bass as bass
from concourse import mybir

F32 = mybir.dt.float32
F32R = mybir.dt.float32r
I32 = mybir.dt.int32
ALU = mybir.AluOpType
ACT = mybir.ActivationFunctionType
AX = mybir.AxisListType
ds = bass.ds

P = 128
D = 1024
DC = D // P
TP = 512
NB, NT = 8, 4
TS = NB * NT
T = TP + TS
HT = T // 2
NH, HD = 8, 64
PG = 16
NPOOL = 160
DFF = 2816
FC = DFF // P
HALF = (12, 10)
CA, CF, CC = 3, 3, 31
PE_SHIFTS = list(range(0, 24, 2))
DVE_SHIFTS = [n for n in range(1, CC, 2)] + list(range(24, CC, 2))
PT = len(PE_SHIFTS)
CW = PE_SHIFTS[-1] + 1
EPS = 1e-6
MASKED = -1e30
SLOTS = 4
KS, VS = 8, 8
SCRATCH = 1024
NQ = T - TP
UT = (CC - 1) + TS
FT = 2 + 2 * NB


class Steps:

    def __init__(self):
        self.base, self.local, self.i, self.per = 0, 0, None, 0

    def tick(self):
        self.local += 1
        return self.now()

    def now(self):
        at = self.base + self.local
        return at if self.i is None else self.i * self.per + at

    @contextmanager
    def loop(self, eng, start, end, per):
        self.base += self.local - start * per
        self.local = 0
        with eng.Fori(start, end) as i:
            self.i, self.per = i, per
            yield i
        assert self.local == per, (self.local, per)
        self.base += end * per
        self.local, self.i, self.per = 0, None, 0


class Phase:

    def __init__(self, name, slab0, group0, turns, tiles, per_group, residual):
        self.name, self.slab0, self.group0 = name, slab0, group0
        self.turns, self.tiles, self.per_group = turns, tiles, per_group
        self.slabs = 4 * turns
        self.slab1 = slab0 + self.slabs
        self.group1 = group0 + self.slabs // per_group
        self.residual = residual

    def slab(self, i, j):
        return i * 4 + (self.slab0 + j)

    def group(self, i, j):
        return i * (4 // self.per_group) + (self.group0 + j // self.per_group)


def plan():
    phases, slab = {}, 0
    groups = {False: 0, True: DC}
    rows = [("qkv", 3, DC, 1), ("gates", 3, DC, 1), ("out", 2, DC, 1)]
    ffn = lambda l: [(f"up{l}0", HALF[0] // 2, DC, 1), (f"down{l}0", 4, HALF[0] // 2, 2),
                     (f"up{l}1", HALF[1] // 2, DC, 1), (f"down{l}1", 4, HALF[1] // 2, 2)]
    rows += ffn(0) + [("pw1", 4, DC, 1), ("pw2", 2, DC, 1)] + ffn(1)
    for name, turns, tiles, per in rows:
        residual = name in ("out", "pw2") or name.startswith("down")
        p = phases[name] = Phase(name, slab, groups[residual], turns, tiles, per, residual)
        slab, groups[residual] = p.slab1, p.group1
    return phases


def param_rows():
    at, rows = 0, {}
    for name, n in (("mix0", DC), ("qk", 2), ("conv_a", CA * 4), ("ffn", 2 * DC), ("conv_f", 2 * CF * FC),
                    ("mix1", DC), ("b_pw1", 2 * DC), ("conv_cb", DC), ("ln_g", DC), ("ln_b", DC),
                    ("conv_c", CC * DC)):
        rows[name] = (at, n)
        at += n
    return rows, at


def row_blocks(r0, n):
    out = []
    while n:
        k = min(n, P - r0 % P)
        out.append((r0, k))
        r0, n = r0 + k, n - k
    return out


def build(nc, a, o):
    ph = plan()
    order = list(ph.values())
    prow, n_rows = param_rows()
    with ExitStack() as ctx:
        sem = lambda name: ctx.enter_context(nc.semaphore(name))

        top = [SCRATCH]

        def place(name, shape, dt, at=None):
            size = 4
            for n in shape[1:]:
                size *= n
            if at is None:
                at = top[0]
                top[0] += (size + 31) // 32 * 32
            assert at + size <= 229344, name
            return nc.alloc_sbuf_tensor_at(name, shape, dt, offset=at), at

        CH = T * 4
        x, _ = place("x", [P, DC, T], F32)
        xa_h, xa_at = place("xa_h", [P, DC, T], F32R)
        xa_l, _ = place("xa_l", [P, DC, T], F32R)
        h_h, hh_at = place("h_h", [P, HALF[0], T], F32R)
        h_l, hl_at = place("h_l", [P, HALF[0], T], F32R)
        w_raw, raw_at = place("w_raw", [P, SLOTS, DC * P], F32)
        w_h, wh_at = place("w_h", [P, SLOTS, DC * P], F32R)
        w_l, wl_at = place("w_l", [P, SLOTS, DC * P], F32R)
        ident, _ = place("ident", [P, P], F32)
        ones, _ = place("ones", [P, P], F32)
        head_ones, _ = place("head_ones", [P, P], F32)
        causal, _ = place("causal", [P, P], F32)
        later, _ = place("later", [P, P], F32)
        params, _ = place("params", [P, n_rows], F32)
        r_all, _ = place("r_all", [P, T], F32)
        ssum, ss_at = place("ssum", [P, T], F32)
        sq, sq_at = place("sq", [P, 2, T], F32)
        tmp, tmp_at = place("tmp", [P, 2, T], F32)
        base = top[0]
        x_rows, _ = place("x_rows", [P, 5, D], F32, hh_at)
        p_rows, _ = place("p_rows", [P, 4, P], F32, hh_at + 5 * D * 4)
        qkv, _ = place("qkv", [P, 12, T], F32)
        kt_h, kt_at = place("kt_h", [P, 2, 4 * P], F32R)
        kt_l, _ = place("kt_l", [P, 2, 4 * P], F32R)
        v_tok, vt_at = place("v_tok", [P, 4, 4 * P], F32)
        sc, sc_at = place("sc", [P, PG + 1, 32], F32)
        pr, _ = place("pr", [P, PG + 1, 32], F32, hl_at + 4 * CH)
        pr_h, _ = place("pr_h", [P, 2, PG + 1, 32], F32R, hh_at + 4 * CH)
        pr_l, _ = place("pr_l", [P, 2, PG + 1, 32], F32R, hh_at + 6 * CH)
        vn_h, _ = place("vn_h", [TS, 4 * P], F32R, hl_at + 5 * CH)
        vn_l, _ = place("vn_l", [TS, 4 * P], F32R, hl_at + 5 * CH + 2048)
        own, _ = place("own", [TS, 4 * P], F32, hl_at + 5 * CH + 4096)
        dk, _ = place("dk", [P, NB, PG, NH], F32)
        cn_all, _ = place("cn_all", [P, NH, NB, NT], F32)
        q_diag, _ = place("q_diag", [P, 4, NB, 8], F32)
        qd_h, _ = place("qd_h", [P, 4, NB, 8], F32R)
        qd_l, _ = place("qd_l", [P, 4, NB, 8], F32R)
        nbias, _ = place("nbias", [TS, NB, NH, NT], F32)
        small, _ = place("small", [P, 224], F32)
        fw, fw_at = place("fw", [P, DC, NH], F32)
        fw_h, _ = place("fw_h", [P, DC, NH], F32R)
        fw_l, _ = place("fw_l", [P, DC, NH], F32R)
        ext_a, _ = place("ext_a", [P, 4, NB, CA - 1 + NT], F32)
        tail_a, _ = place("tail_a", [P, 4, FT], F32)
        lf_row, _ = place("lf_row", [P, 5, NH], F32)
        m1, gmax, diag = small[:, 0:32], small[0:32, 32:33], small[0:32, 64:96]
        p_sum, rec = small[:, 96:128], small[0:TS, 128:129]
        pick = small[0:TS, 132:136]
        cq = small[:, 160:192]
        cns = small[0:TS, 192:200]
        b_f = small[0:NH, 200:201]
        rmax, rsum, rinv = small[:, 204:208], small[:, 208:212], small[:, 212:216]
        k_pg, _ = place("k_pg", [P, KS, 4 * P], F32, xa_at)
        cb, _ = place("cb", [P, NH, TP], F32, xa_at + KS * 2048)
        v_pg, _ = place("v_pg", [P, VS, 4 * P], F32, wh_at)
        blocks, _ = place("blocks", [TS, 4 * P], F32, xa_at + KS * 2048 + NH * 2048)
        v_h, _ = place("v_h", [P, 4, 4 * P], F32R, wl_at)
        v_l, _ = place("v_l", [P, 4, 4 * P], F32R, wl_at + 4 * 2048)
        u4, _ = place("u4", [P, 4, T], F32, hh_at + 8 * CH)
        g4, _ = place("g4", [P, 4, T], F32, hl_at + 8 * CH)
        lf_pg, _ = place("lf_pg", [P, D], F32, kt_at)
        lf_k, _ = place("lf_k", [P, NH * NB, PG], F32, kt_at + 4096)
        suf, _ = place("suf", [P, NH * NB, PG], F32, vt_at)
        pgix, _ = place("pgix", [P, 1], I32, vt_at + 4096)
        fz, _ = place("fz", [NH, T], F32, kt_at)
        fe, _ = place("fe", [NH, T], F32, kt_at + CH)
        seg, _ = place("seg", [NH, T], F32, kt_at + 2 * CH)
        cmask, _ = place("cmask", [NH, 2, TP], F32, kt_at)
        logf, _ = place("logf", [NH, T], F32, vt_at)
        cum, _ = place("cum", [NH, T], F32, vt_at + CH)
        cnm, _ = place("cnm", [NH, NH, TS], F32, vt_at + 2 * CH)
        k_row, _ = place("k_row", [P, 2, 4 * P], F32, hh_at + 8 * CH)
        s_row, _ = place("s_row", [TS, 2, 4 * P], F32, hh_at + 8 * CH + 4096)
        qs_h = [place("qs_h0", [P, 4, 40], F32R, hh_at + 8 * CH)[0], place("qs_h1", [P, 4, 40], F32R, fw_at)[0]]
        qs_l = [place(f"qs_l{n}", [P, 4, 40], F32R, hh_at + 8 * CH + 640 * (n + 1))[0] for n in range(2)]
        s_t, _ = place("s_t", [TS, 4 * P], F32, hh_at + 8 * CH + 1920)
        a_row, _ = place("a_row", [2 * NB, 4 * P], F32, sc_at)
        a_out, _ = place("a_out", [FT, 4 * P], F32, sc_at)
        sb, _ = place("sb", [P, 4, TP], F32, hl_at + 8 * CH)
        pt, _ = place("pt", [P, 2, TP], F32, ss_at)
        q_s, _ = place("q_s", [P, TP], F32, ss_at + 4096)
        k_s, _ = place("k_s", [P, TP], F32, ss_at + 6144)
        v_s, _ = place("v_s", [P, 4, P], F32, ss_at + 8192)
        top[0] = base
        gate, _ = place("gate", [P, 2, T], F32)
        cv, _ = place("cv", [P, 2, T], F32)
        sl, _ = place("sl", [P, 2, T], F32)
        sr, sr_at = place("sr", [P, 2, T], F32)
        ext_f, _ = place("ext_f", [P, FC, NB, CF - 1 + NT], F32)
        tail_f, _ = place("tail_f", [P, FC, FT], F32)
        f_row, fr_at = place("f_row", [FT, DFF], F32)
        yc, yc_at = place("yc", [P, DC, T], F32)
        y_row = [place("y_row0", [P, 5, D // 2], F32, yc_at)[0],
                 place("y_row1", [P, 5, D // 2], F32, base)[0]]
        ua, _ = place("ua", [P, 2, T], F32, base)
        u, _ = place("u", [P, 2, T], F32, base + 2 * CH)
        sg, _ = place("sg", [P, 2, T], F32, base + 4 * CH)
        prod, _ = place("prod", [P, TS, CC], F32, sr_at)
        dg_h, _ = place("dg_h", [P, 2, PT, P], F32R, hh_at)
        dg_l, _ = place("dg_l", [P, 2, PT, P], F32R, hl_at)
        u_h, _ = place("u_h", [P, 2, T], F32R, hh_at + 2 * PT * 512)
        u_l, _ = place("u_l", [P, 2, T], F32R, hl_at + 2 * PT * 512)
        cw_h, _ = place("cw_h", [P, CW * DC], F32R, hl_at + 2 * PT * 512 + 2 * CH)
        cw_l, _ = place("cw_l", [P, CW * DC], F32, hh_at + 2 * PT * 512 + 2 * CH)
        ext_c, _ = place("ext_c", [P, DC, NB, CC - 1 + NT], F32, hh_at + 8 * CH)
        c_row, _ = place("c_row", [4 * (CC - 1), 2, D], F32, base)
        tail_c, _ = place("tail_c", [P, DC, UT], F32, fr_at)
        u_row, _ = place("u_row", [UT, D], F32, fr_at + 4096)

        pair = [nc.alloc_psum_tensor(f"pair{n}", [P, 2, 512], F32) for n in range(2)]
        psum_s = nc.alloc_psum_tensor("psum_s", [P, 2, 512], F32)
        bank = [nc.alloc_psum_tensor(f"bank{n}", [P, 512], F32) for n in range(2)]
        pb = [pair[0][:, 0, :], pair[0][:, 1, :], pair[1][:, 0, :], pair[1][:, 1, :]]

        s_raw = [sem(f"raw{j}") for j in range(SLOTS)]
        s_hi, s_lo = sem("hi"), sem("lo")
        s_slab = sem("slab")
        s_free = sem("free")
        s_prm, s_xld, s_st, s_fw, s_ix, s_lf = (sem(n) for n in (
            "params_in", "x_in", "state_in", "fw_in", "index_in", "logf_in"))
        s_cst = sem("constants")
        s_tp = sem("x_turned")
        s_xnew = sem("x_new")
        s_sq, s_ss, s_stat = sem("squares"), sem("added"), sem("sums")
        s_xhi, s_xlo = sem("xa_high"), sem("xa_low")
        s_var, s_rt, s_r = sem("variance"), sem("ln"), sem("inv_root")
        s_dve = sem("dve_step")
        s_ya, s_cv, s_sl, s_sr, s_hhi, s_hlo = (sem(n) for n in (
            "y_a", "conv", "silu", "silu_r", "h_high", "h_low"))
        s_out, s_rowdma, s_aout = sem("written"), sem("row_written"), sem("a_written")
        s_misc, s_miscd = sem("short"), sem("short_read")
        s_suf, s_fz, s_fe, s_cum, s_cm, s_cbp, s_cb = (sem(n) for n in (
            "later_pages", "forget_in", "forget_ln", "cum", "c_masked", "c_spread", "c_copied"))
        s_qsq, s_hv, s_hrt, s_qk, s_tail = (sem(n) for n in ("qk_squares", "qk_var", "qk_inv_root", "qk_normed", "tail"))
        s_k = [sem(f"k{n}") for n in range(KS)]
        s_v = [sem(f"v{n}") for n in range(VS)]
        s_vh, s_vl, s_vn = sem("v_high"), sem("v_low"), sem("new_v")
        s_kl, s_ph, s_pl = sem("page_low"), sem("exps_high"), sem("exps_low")
        s_ow, s_owr = sem("picked"), sem("picked_read")
        s_qb, s_stc = sem("batch_q"), sem("four_copied")
        s_yd = sem("rows_read_too")
        s_sqp = sem("squares_summed")
        s_zero, s_hln = sem("zeros"), sem("qk_ln")
        s_cw, s_dgl, s_uh, s_ul, s_cvp, s_cvr = (sem(n) for n in (
            "tap_parts", "diagonals", "u_high", "u_low", "pe_conv", "pe_conv_read"))
        s_pick, s_blk = sem("pick"), sem("blocks")
        s_tr, s_kt, s_sp, s_sc, s_sev = (sem(n) for n in (
            "page_turned", "page_copied", "page_scored", "batch_scored", "scores_read"))
        s_m1, s_mt, s_dg, s_mb = (sem(n) for n in ("max_keys", "max_turned", "max_diag", "max_spread"))
        s_sm, s_p, s_lp, s_l = (sem(n) for n in ("shifted", "exps", "exps_added", "exps_summed"))
        s_pvp, s_oev, s_rec = sem("page_valued"), sem("values_read"), sem("inv_sum")
        s_qd = sem("q_side_by_side")
        s_qs, s_s, s_sb, s_pe = (sem(n) for n in ("pair_copied", "p_scored", "p_biased", "p_exp"))
        s_sbr, s_pn, s_ptt, s_ptc, s_po, s_pod = (sem(n) for n in (
            "p_read", "p_norm", "p_turned", "p_tcopied", "p_valued", "p_out"))
        s_rows, s_rowsd = sem("rows_turned"), sem("rows_read")
        s_fst, s_fstd = sem("state_turned"), sem("state_read")
        s_sig, s_u, s_ux, s_mu, s_xc, s_ty, s_s32 = (sem(n) for n in (
            "u_sig", "u", "u_kept", "mean", "centred", "scaled", "swish"))
        n_out = [0]

        halves = lambda ap: ap.rearrange("p (h t) -> p h t", h=2)
        gview = lambda b: pair[b][:, :, 0:HT]
        par = lambda name, k: params[:, ds(k + prow[name][0], 1)]
        R = {}
        at = 0
        for name, n in (("kv", 10), ("ffn0", 6), ("conv_c", 2), ("ffn1", 6), ("y", 10)):
            R[name] = at
            at += n
        XN = dict(init=0, **{p.name: p.group0 for p in order if p.residual})
        NORM = dict(init=0, out=1, down01=2, pw2=3)
        ADD = dict(init=0, out=1, down01=2, mean=3, pw2=4)
        SUM = dict(init=0, out=1, down01=2, mean=3, var=4, pw2=5)
        SQ = dict(init=0, out=1, down01=2, var=3, pw2=4)
        GAIN = dict(init=("mix0", 0), out=("ffn", 0), down01=("mix1", 0), pw2=("ffn", DC))
        HB = dict(out=0, up0=8, pw2=8 + FC, up1=16 + FC)

        pe_taps = prow["conv_c"][0] + (CC - CW) * DC

        block = ctx.enter_context(nc.Block())

        def slab_tiles(s):
            for p in order:
                if p.slab0 <= s < p.slab1:
                    return p.tiles

        def turns(eng, phase, body, peel=0, then=None, late=None):
            for i in range(peel):
                body(i, False)
            if then:
                then()
            if phase.turns - 1 > peel:
                with eng.Fori(peel, phase.turns - 1) as i:
                    body(i, False)
            if late:
                late()
            body(phase.turns - 1, True)

        def ahead(split, phase, i, j, last):
            turn, slot = i + (phase.slab0 // 4 + (j + 3) // 4), (j + 3) % 4
            tiles = phase.tiles
            if last and j >= 1:
                tiles = slab_tiles(phase.slab1 + j - 1)
                if tiles is None or phase is ph["gates"]:
                    return
            split(turn, slot, tiles)

        @block.sync
        def _(sp):
            for k in range(4):
                sp.dma_start(x_rows[:, k, :], a["x_prompt"][0, k * P:(k + 1) * P, :]).then_inc(s_xld, 16)
            sp.dma_start(x_rows[0:TS, 4, :], a["x_sample"].rearrange("b t d -> (b t) d")).then_inc(s_xld, 16)
            chunks = lambda ap: ap.rearrange("a (c p) -> (a c) p", p=P)
            sources = dict(mix0=chunks(a["norm_mix0"]), conv_a=chunks(a["conv_a_w"].rearrange("a k d -> (a k) d")),
                           ffn=chunks(a["norm_ffn"]), conv_f=chunks(a["conv_ffn_w"].rearrange("l k d -> (l k) d")),
                           mix1=chunks(a["norm_mix1"]), b_pw1=chunks(a["b_pw1"]), conv_cb=chunks(a["conv_c_b"]),
                           ln_g=chunks(a["ln_c_g"]), ln_b=chunks(a["ln_c_b"]),
                           conv_c=chunks(a["conv_c_w"].rearrange("a k d -> (a k) d")))
            for name, (r0, n) in prow.items():
                if name == "qk":
                    for r, g in enumerate(("q_norm", "k_norm")):
                        for hh in range(2):
                            sp.dma_start(p_rows[r0 + r:r0 + r + 1, 0, hh * HD:(hh + 1) * HD], a[g]).then_inc(s_prm, 16)
                    continue
                for at, k in row_blocks(r0, n):
                    done = at - r0
                    sp.dma_start(p_rows[at % P:at % P + k, at // P, :], sources[name][done:done + k, :])\
                      .then_inc(s_prm, 16)

            def load(phase, i, j, src):
                s = phase.slab(i, j)
                if not (isinstance(s, int) and s < SLOTS):
                    sp.wait_ge(s_lo, s - (SLOTS - 1))
                sp.dma_start(w_raw[:, j, 0:phase.tiles * P].rearrange("p (k n) -> p k n", n=P), src)\
                  .then_inc(s_raw[j], 16)

            def cols(w, at, tiles=DC, k0=0):
                return w.rearrange("(k p) n -> p k n", p=P)[:, k0:k0 + tiles, ds(at, P)]

            def out(dst, src, signal=None):
                sp.dma_start(dst, src).then_inc(signal or s_out, 16)
                if signal is None:
                    n_out[0] += 1

            w_in, w_out = a["w_in0"][0], a["w_out0"][0]
            for j in range(4):
                load(ph["qkv"], 0, j, cols(w_in, 1536 + j * P))
            sp.dma_start(pgix[:, :], a["page_table"].rearrange("b (p a) -> (b p) a", a=1)).then_inc(s_ix, 16)
            sp.dma_start(a_row[:, :], a["state_conv_a"][0].rearrange("b t d -> (b t) d")).then_inc(s_st, 16)
            sp.dma_start(fw[:, :, :], w_in.rearrange("(k p) n -> p k n", p=P)[:, :, 3072:3080]).then_inc(s_fw, 16)
            sp.dma_start(b_f, a["b_forget"].rearrange("a h -> h a")).then_inc(s_fw, 16)
            with sp.Fori(1, 3) as i:
                for j in range(4):
                    load(ph["qkv"], i, j, cols(w_in, i * 512 + (1536 + j * P)))
            for i, at in enumerate((512, 1024, 0)):
                for j in range(4):
                    load(ph["gates"], i, j, cols(w_in, at + j * P))
            for j in range(4):
                load(ph["out"], 0, j, cols(w_out, j * P))
            out(o["s_conv_c"][0, :, 0:CC - 1 - NT, :], a["state_conv_c"][0, :, NT:CC - 1, :])

            sp.wait_ge(s_slab, ph["gates"].slab1)

            def page_ids(b, half):
                return nc.values_load_multi_w_load_instructions(a["page_table"][ds(b, 1), half * 8:half * 8 + 8],
                                                                engines=(mybir.EngineType.SP,), min_val=0,
                                                                max_val=NPOOL - 1)[1]

            def page(b, p, pid, cache, slots, done, first):
                place_, arrived = ((k_pg, s_k) if cache == "cache_k" else (v_pg, s_v))
                if not first:
                    sp.wait_ge(done, b * PG + (p - slots + 1))
                sp.dma_start(place_[:, p % slots, :], a[cache][0, ds(pid, 1)].rearrange("a k h d -> (a k) (h d)"))\
                  .then_inc(arrived[p % slots], 16)

            first_ids = page_ids(0, 0)
            for p in range(KS):
                page(0, p, first_ids[p], "cache_k", KS, s_tr, True)
            for t in range(4):
                sp.wait_ge(s_rowsd, R["kv"] + 2 * t + 1)
                out(o["p_k"][0, 0, t * P:(t + 1) * P].rearrange("t h d -> t (h d)"), k_row[:, t % 2, :], s_rowdma)
                sp.wait_ge(s_rowsd, R["kv"] + 2 * t + 2)
                out(o["p_v"][0, 0, t * P:(t + 1) * P].rearrange("t h d -> t (h d)"), v_tok[:, t, :])
            sp.wait_ge(s_rowsd, R["kv"] + 10)
            out(o["s_k"][0].rearrange("b t h d -> (b t) (h d)"), s_row[:, 0, :])
            out(o["s_v"][0].rearrange("b t h d -> (b t) (h d)"), s_row[:, 1, :])
            sp.wait_ge(s_miscd, 9)
            with nc.allow_non_contiguous_dma(reason="32-byte rows of log forgets"):
                out(o["p_logf"][0, 0].rearrange("(t p) h -> p t h", p=P), lf_row[:, 0:4, :])
                out(o["s_logf"][0].rearrange("b t h -> (b t) h"), lf_row[0:TS, 4, :])
            out(o["p_conv_a"][0, 0], a_out[0:2, :], s_aout)
            out(o["s_conv_a"][0].rearrange("b t d -> (b t) d"), a_out[2:FT, :], s_aout)
            first_ids = page_ids(0, 1)
            for p in range(KS, PG):
                page(0, p, first_ids[p - KS], "cache_k", KS, s_tr, False)

            def batch_pages(b, half):
                known = isinstance(b, int)
                keys = page_ids(b, half)
                vb = b - 1 if half else b - 2
                values = None if known and vb < 0 else page_ids(vb, 1 - half)
                for p in range(8):
                    page(b, half * 8 + p, keys[p], "cache_k", KS, s_tr, False)
                    if values:
                        page(vb, (1 - half) * 8 + p, values[p], "cache_v", VS, s_vl, known and vb == 0 and half == 1)
            for half in range(2):
                batch_pages(1, half)
            with sp.Fori(2, NB) as b:
                for half in range(2):
                    batch_pages(b, half)
            for vb, half in ((NB - 2, 1), (NB - 1, 0), (NB - 1, 1)):
                values = page_ids(vb, half)
                for p in range(8):
                    page(vb, half * 8 + p, values[p], "cache_v", VS, s_vl, False)
            for j in range(4):
                load(ph["out"], 1, j, cols(w_out, 512 + j * P))

            def ffn(l):
                up, down = a["w_up"][l], a["w_down"][l]
                sp.wait_ge(s_xhi, 8 * NORM["out" if l == 0 else "pw2"] + 1)
                sp.wait_ge(s_out, 16 * n_out[0])
                sp.dma_start(f_row[0:2 * NB, :], a["state_ffn"][l].rearrange("b t d -> (b t) d")).then_inc(s_st, 16)
                for half in range(2):
                    pu, pd, k0 = ph[f"up{l}{half}"], ph[f"down{l}{half}"], half * HALF[0]
                    with sp.Fori(0, pu.turns) as i:
                        for j in range(4):
                            load(pu, i, j, cols(up, i * (2 * P) + ((j % 2) * DFF + (k0 + j // 2) * P)))
                    with sp.Fori(0, pd.turns) as i:
                        for j in range(4):
                            load(pd, i, j, cols(down, i * (2 * P) + (j // 2) * P, pd.tiles,
                                                k0 + (j % 2) * pd.tiles))
                    if l == 0 and half == 1:
                        sp.wait_ge(s_hlo, HB["up0"] + FC)
                        for k in range(2):
                            sp.dma_start(c_row[:, k, :], a["state_conv_c"][0, 4 * k:4 * k + 4].rearrange("b t d -> (b t) d"))\
                              .then_inc(s_st, 16)
                sp.wait_ge(s_rowsd, R[f"ffn{l}"] + 6)
                out(o["p_ffn"][l, 0], f_row[0:2, :])
                out(o["s_ffn"][l].rearrange("b t d -> (b t) d"), f_row[2:FT, :])

            ffn(0)
            n_out.append(n_out[0])
            with sp.Fori(0, ph["pw1"].turns) as i:
                for j in range(4):
                    load(ph["pw1"], i, j, cols(a["w_pw1"][0], i * (2 * P) + ((j % 2) * D + (j // 2) * P)))
            for i in range(2):
                for j in range(4):
                    load(ph["pw2"], i, j, cols(a["w_pw2"][0], i * 512 + j * P))
            sp.wait_ge(s_rowsd, R["conv_c"] + 2)
            out(o["p_conv_c"][0, 0], u_row[0:CC - 1, :])
            for b in range(NB):
                out(o["s_conv_c"][0, b, CC - 1 - NT:CC - 1, :],
                    u_row[CC - 1 + NT * b:CC - 1 + NT * (b + 1), :])
            ffn(1)
            for q in range(2):
                for t in range(5):
                    if q == 0:
                        sp.wait_ge(s_rowsd, R["y"] + t + 1)
                    elif t % 2 == 0:
                        sp.wait_ge(s_rowsd, R["y"] + 5 + t // 2 + 1)
                    else:
                        sp.wait_ge(s_yd, t // 2 + 1)
                    cols_q = slice(q * 512, q * 512 + 512)
                    if t < 4:
                        out(o["y_prompt"][0, t * P:(t + 1) * P, cols_q], y_row[q][:, t, :])
                    else:
                        out(o["y_sample"].rearrange("b t d -> (b t) d")[:, cols_q], y_row[q][0:TS, t, :])
            sp.wait_ge(s_rowdma, 16 * 4)
            sp.wait_ge(s_aout, 16 * 2)
            sp.wait_ge(s_out, 16 * n_out[0])

        @block.gpsimd
        def _(pool):
            g = nc.gpsimd
            g.memset(ident[:, :], 0.0).then_inc(s_cst, 1)
            g.memset(ones[:, :], 1.0).then_inc(s_cst, 1)
            g.memset(head_ones[:, :], 0.0).then_inc(s_cst, 1)
            g.memset(causal[:, :], 0.0).then_inc(s_cst, 1)
            g.memset(later[:, :], 1.0).then_inc(s_cst, 1)
            g.memset(nbias[:, :, :, :], 0.0).then_inc(s_cst, 1)
            g.memset(q_diag[:, :, :, :], 0.0).then_inc(s_cst, 1)
            g.memset(sc[:, PG, :], MASKED).then_inc(s_cst, 1)
            pool.wait_ge(s_cst, 8)
            g.memset(head_ones[0:HD, 0:HD], 1.0).then_inc(s_cst, 1)
            g.memset(head_ones[HD:P, HD:P], 1.0).then_inc(s_cst, 1)
            pool.wait_ge(s_cst, 10)
            g.affine_select(out=ident[:, :], in_=ident[:, :], compare_op=ALU.not_equal, fill=1.0, base=0,
                            pattern=[[-1, P]], channel_multiplier=1).then_inc(s_cst, 1)
            g.affine_select(out=causal[:, :], in_=causal[:, :], compare_op=ALU.is_ge, fill=MASKED, base=0,
                            pattern=[[-1, P]], channel_multiplier=1).then_inc(s_cst, 1)
            g.affine_select(out=later[:, :], in_=later[:, :], compare_op=ALU.is_gt, fill=0.0, base=0,
                            pattern=[[-1, P]], channel_multiplier=1).then_inc(s_cst, 1)
            g.affine_select(out=nbias[:, :, :, :], in_=nbias[:, :, :, :], compare_op=ALU.is_ge, fill=MASKED, base=0,
                            pattern=[[-NT, NB], [0, NH], [0, NT]], channel_multiplier=1).then_inc(s_cst, 1)
            pool.wait_ge(s_cst, 14)
            g.affine_select(out=nbias[:, :, :, :], in_=nbias[:, :, :, :], compare_op=ALU.is_ge, fill=MASKED, base=0,
                            pattern=[[NT, NB], [0, NH], [1, NT]], channel_multiplier=-1).then_inc(s_cst, 1)
            pool.wait_ge(s_ix, 16)
            g.indirect_dma_start(out=lf_pg[:, :], out_offset=None,
                                 in_=a["cache_logf"][0].rearrange("n k h -> n (k h)"),
                                 in_offset=bass.IndirectOffsetOnAxis(ap=pgix[:, 0:1], axis=0)).then_inc(s_lf, 16)

            def split_low(turn, slot, tiles):
                n = tiles * P
                pool.wait_ge(s_hi, turn * 4 + (slot + 1))
                g.tensor_tensor(w_l[:, slot, 0:n], w_raw[:, slot, 0:n], w_h[:, slot, 0:n].bitcast(F32),
                                ALU.subtract).then_inc(s_lo, 1)

            for slot in range(3):
                split_low(0, slot, DC)
            pool.wait_ge(s_fw, 33)
            g.tensor_tensor(fw_l[:, :, :], fw[:, :, :], fw_h[:, :, :].bitcast(F32), ALU.subtract).then_inc(s_fw, 1)
            for phase in (ph["qkv"], ph["gates"]):
                def turn(i, last, phase=phase):
                    for j in range(4):
                        ahead(split_low, phase, i, j, last)
                turns(pool, phase, turn)
            pool.wait_ge(s_slab, ph["gates"].slab1)
            g.memset(blocks[:, :], 1.0).then_inc(s_blk, 1)
            for k, (step, base, row) in enumerate(((-NT, 0, 1), (NT, NT - 1, -1))):
                pool.wait_ge(s_blk, k + 1)
                g.affine_select(out=blocks[:, :], in_=blocks[:, :], compare_op=ALU.is_ge, fill=0.0, base=base,
                                pattern=[[step, NH], [0, HD]], channel_multiplier=row).then_inc(s_blk, 1)
            with pool.Fori(0, NB * PG // VS) as i:
                for n in range(VS):
                    pool.wait_ge(s_vh, i * VS + (n + 1))
                    g.tensor_tensor(v_l[:, n % 4, :], v_pg[:, n, :], v_h[:, n % 4, :].bitcast(F32), ALU.subtract)\
                     .then_inc(s_vl, 1)
            for slot in range(3):
                split_low(ph["out"].slab0 // 4, slot, DC)
            def turn(i, last):
                for j in range(4):
                    ahead(split_low, ph["out"], i, j, last)
            turns(pool, ph["out"], turn)

            def ffn(l):
                for half in range(2):
                    pu, pd = ph[f"up{l}{half}"], ph[f"down{l}{half}"]

                    def turn(i, last):
                        for j in range(4):
                            if j % 2 == 0:
                                ahead(split_low, pu, i, j, last)
                            else:
                                k = i * 2 + (l * FC + half * HALF[0] + j // 2)
                                pool.wait_ge(s_sl, k + 1)
                                pool.wait_ge(s_r, SQ["out" if l == 0 else "pw2"] + 1)
                                pool.wait_ge(s_free, pu.group(i, j) - 3)
                                g.tensor_tensor(sr[:, j // 2, :], sl[:, j // 2, :], r_all[:, :], ALU.mult)\
                                 .then_inc(s_sr, 1)
                                ahead(split_low, pu, i, j, last)
                    turns(pool, pu, turn)

                    def turn(i, last):
                        for j in range(4):
                            ahead(split_low, pd, i, j, last)
                    turns(pool, pd, turn)
            ffn(0)
            for phase in (ph["pw1"], ph["pw2"]):
                def turn(i, last, phase=phase):
                    for j in range(4):
                        ahead(split_low, phase, i, j, last)
                        if phase is ph["pw1"] and j % 2:
                            pool.wait_ge(s_uh, i * 2 + (j // 2 + 1))
                            g.tensor_tensor(u_l[:, j // 2, 0:TP], u[:, j // 2, 0:TP], u_h[:, j // 2, 0:TP].bitcast(F32),
                                            ALU.subtract).then_inc(s_ul, 1)
                turns(pool, phase, turn)
            ffn(1)

        @block.scalar
        def _(act):
            A = nc.scalar.activation

            def apart(i):
                if not isinstance(i, int):
                    act.wait_ge(s_cst, 15)

            def split_high(turn, slot, tiles):
                n = tiles * P
                act.wait_ge(s_raw[slot], turn * 16 + 16)
                if not (isinstance(turn, int) and turn == 0):
                    act.wait_ge(s_slab, turn * 4 + (slot - 3))
                A(w_h[:, slot, 0:n], w_raw[:, slot, 0:n], ACT.Copy).then_inc(s_hi, 1)

            def norm_work(stage, m, b):
                name, g0 = GAIN[stage]
                act.wait_ge(s_xnew, m + (XN[stage] + 1))
                if not (isinstance(m, int) and m < 2):
                    act.wait_ge(s_ss, m + 9 * ADD[stage])
                apart(m)
                A(sq[:, b, :], x[:, ds(m, 1), :].rearrange("p a t -> p (a t)"), ACT.Square).then_inc(s_sq, 1)
                A(xa_h[:, ds(m, 1), :].rearrange("p a t -> p (a t)"), x[:, ds(m, 1), :].rearrange("p a t -> p (a t)"),
                  ACT.Copy, scale=par(name, m + g0)).then_inc(s_xhi, 1)

            def root(k):
                act.wait_ge(s_var, k + 1)
                A(r_all[:, :], r_all[:, :], ACT.Ln).then_inc(s_rt, 1)
                act.wait_ge(s_rt, k + 1)
                A(r_all[:, :], r_all[:, :], ACT.Exp, scale=-0.5).then_inc(s_r, 1)

            act.wait_ge(s_miscd, 1)
            for m in range(DC):
                norm_work("init", m, m % 2)
                if m in (2, 4, 6):
                    split_high(0, m // 2 - 1, DC)
            act.wait_ge(s_fw, 32)
            A(fw_h[:, :, :], fw[:, :, :], ACT.Copy).then_inc(s_fw, 1)
            root(0)
            for i in range(3):
                for j in range(4):
                    ahead(split_high, ph["qkv"], i, j, i == 2)
            act.wait_ge(s_fz, 1)
            A(fe[:, :], fz[:, :], ACT.Abs).then_inc(s_fe, 1)
            act.wait_ge(s_fe, 1)
            A(fe[:, :], fe[:, :], ACT.Exp, scale=-1.0).then_inc(s_fe, 1)
            act.wait_ge(s_fe, 2)
            A(fe[:, :], fe[:, :], ACT.Ln, bias=1.0).then_inc(s_fe, 1)
            for i in range(3):
                for j in range(4):
                    ahead(split_high, ph["gates"], i, j, i == 2)
                    c = 4 * i + j
                    if c < 8:
                        act.wait_ge(s_free, c + 1)
                        if c >= 2:
                            act.wait_ge(s_misc, 6 + c - 2)
                        A(sq[:, c % 2, :], qkv[:, c, :], ACT.Square).then_inc(s_qsq, 1)
                        act.wait_ge(s_hv, c + 1)
                        A(tmp[:, c % 2, :], tmp[:, c % 2, :], ACT.Ln).then_inc(s_hln, 1)
                        act.wait_ge(s_hln, c + 1)
                        A(tmp[:, c % 2, :], tmp[:, c % 2, :], ACT.Exp, scale=-0.5).then_inc(s_hrt, 1)
                    else:
                        m = c - 8
                        act.wait_ge(s_ya, m + 1)
                        A(h_h[:, m, :], g4[:, m, :], ACT.Copy).then_inc(s_hhi, 1)
            for h in range(NH):
                act.wait_ge(s_cbp, h + 1)
                A(cb[:, h, :], bank[(h + 1) % 2][:, :], ACT.Copy).then_inc(s_cb, 1)
            for t in range(5):
                for kv in range(2):
                    n = P if t < 4 else TS
                    act.wait_ge(s_rows, R["kv"] + 2 * t + kv + 1)
                    if t == 4:
                        dst = s_row[:, kv, :]
                    elif kv:
                        dst = v_tok[:, t, :]
                    else:
                        if t >= 2:
                            act.wait_ge(s_rowdma, 16 * t)
                        dst = k_row[:, t % 2, :]
                    A(dst, bank[kv][0:n, :], ACT.Copy).then_inc(s_rowsd, 1)

            act.wait_ge(s_qk, 8)
            act.wait_ge(s_rowsd, R["kv"] + 10)
            one = lambda ap: ap.rearrange("p a t -> p (a t)")

            def batch_exps(b, par):
                act.wait_ge(s_sm, b + 1)
                A(pr[:, :, :], sc[:, :, :], ACT.Exp).then_inc(s_p, 1)
                act.wait_ge(s_p, b + 1)
                A(pr_h[:, par, :, :], pr[:, :, :], ACT.Copy).then_inc(s_ph, 1)

            def batch_q(b, bb):
                for dst, src in ((qs_h, q_diag[:, :, :, :]), (qs_l, qd_l[:, :, :, :].bitcast(F32))):
                    A(dst[bb][:, :, 0:8], src[:, :, ds(b, 1), :].rearrange("p c b x -> p c (b x)"), ACT.Copy)\
                     .then_inc(s_qb, 1)

            def four_scored(b, g):
                act.wait_ge(s_sp, b * PG + (g * 4 + 4))
                A(s_t[:, :], pb[3][0:TS, :], ACT.Copy).then_inc(s_stc, 1)

            def value_high(b, p):
                act.wait_ge(s_v[p % VS], b * 32 + 16 * (p // VS + 1))
                if not (isinstance(b, int) and b * PG + p < 4):
                    act.wait_ge(s_pvp, b * PG + (p - 3))
                A(v_h[:, p % 4, :], v_pg[:, p % VS, :], ACT.Copy).then_inc(s_vh, 1)

            act.wait_ge(s_qd, 8)
            A(qd_h[:, :, :, :], q_diag[:, :, :, :], ACT.Copy).then_inc(s_qd, 1)
            A(vn_h[:, :], s_row[:, 1, :], ACT.Copy).then_inc(s_vn, 1)
            act.wait_ge(s_rowdma, 16 * 4)
            for dst in (*qs_h, *qs_l):
                A(dst[:, :, :], ones[:, 0:40].unsqueeze(1).to_broadcast([P, 4, 40]), ACT.Copy, scale=0.0)\
                 .then_inc(s_zero, 1)
            act.wait_ge(s_zero, 4)
            act.wait_ge(s_qd, 10)

            def batch(i, bb):
                b = i * 2 + bb

                def turned_p(w):
                    n = (w + 1) * P
                    act.wait_ge(s_ptt, b * 4 + (w + 1))
                    if not (isinstance(b, int) and b * 4 + w < 2):
                        act.wait_ge(s_po, b * 4 + (w - 1))
                    A(pt[:, w % 2, 0:n], pb[2][:, 0:n], ACT.Copy).then_inc(s_ptc, 1)

                for p in range(PG):
                    if p % 4 == 0 and p:
                        turned_p(p // 4 - 1)
                    if not (isinstance(b, int) and b * PG + p < 2):
                        act.wait_ge(s_sp, b * PG + (p - 1))
                    act.wait_ge(s_tr, b * PG + (p + 1))
                    A(kt_h[:, p % 2, :], pb[p % 2], ACT.Copy).then_inc(s_kt, 1)
                    if p == 0:
                        batch_q(b, bb)
                    if p % 4 == 0 and p:
                        four_scored(b, p // 4 - 1)
                    if p < 6 and not isinstance(b, int):
                        value_high(b - 2, p + 10)
                    if p >= 6 and not (isinstance(b, int) and b == 0):
                        value_high(b - 1, p - 6)
                    if bb == 0 and p == 0:
                        A(q_s[:, :], one(qkv[:, ds(i, 1), 0:TP]), ACT.Copy, scale=HD ** -0.5).then_inc(s_qs, 1)
                        A(k_s[:, :], one(qkv[:, ds(i + 4, 1), 0:TP]), ACT.Copy).then_inc(s_qs, 1)
                    if bb == 0 and p == 1:
                        A(v_s[:, :, :], v_tok[:, :, ds(i * P, P)], ACT.Copy).then_inc(s_qs, 1)
                    if p % 4 == 2:
                        w = p // 4
                        n = (w + 1) * P
                        act.wait_ge(s_sb, b * 4 + (w + 1))
                        A(sb[:, w, 0:n], sb[:, w, 0:n], ACT.Exp, bias=rmax[:, w:w + 1],
                          accum_out=rsum[:, w:w + 1]).then_inc(s_pe, 1)
                    if p == 6 and not (isinstance(b, int) and b == 0):
                        batch_exps(b - 1, 1 - bb)
                turned_p(3)
                four_scored(b, 3)
            batch(0, 0)
            batch(0, 1)
            with act.Fori(1, NB // 2) as i:
                batch(i, 0)
                batch(i, 1)
            for p in range(10, 14):
                value_high(NB - 2, p)
            batch_exps(NB - 1, 1)
            for p in range(14, PG):
                value_high(NB - 2, p)
            for p in range(PG):
                value_high(NB - 1, p)
            act.wait_ge(s_pod, 4)
            act.wait_ge(s_owr, NB)
            for c in range(4):
                A(h_h[:, 4 + c, :], qkv[:, c, :], ACT.Copy).then_inc(s_hhi, 1)

            act.wait_ge(s_pvp, NB * PG)
            for slot in range(3):
                split_high(ph["out"].slab0 // 4, slot, DC)

            def residual(phase, stage, then=None, late=None):
                def turn(i, last):
                    for j in range(4):
                        ahead(split_high, phase, i, j, last)
                        if stage in NORM and j % phase.per_group == phase.per_group - 1:
                            m = i * (4 // phase.per_group) + j // phase.per_group
                            norm_work(stage, m, (j // phase.per_group) % 2)
                turns(act, phase, turn, 1 if stage in NORM or then else 0, then, late)

            residual(ph["out"], "out")

            def rows_of(n, parts, group, dst):
                act.wait_ge(s_rows, group + 1)
                A(dst, bank[(group) % 2][0:parts, 0:n], ACT.Copy).then_inc(s_rowsd, 1)

            def ffn(l):
                root(SQ["out" if l == 0 else "pw2"])
                for half in range(2):
                    pu, pd = ph[f"up{l}{half}"], ph[f"down{l}{half}"]

                    def turn(i, last):
                        for j in range(4):
                            ahead(split_high, pu, i, j, last)
                            k = i * 2 + (l * FC + half * HALF[0] + j // 2)
                            b = j // 2
                            if j % 2 == 0:
                                act.wait_ge(s_cv, k + 1)
                                if not (isinstance(k, int) and k < 2):
                                    act.wait_ge(s_sr, k - 1)
                                A(sl[:, b, :], cv[:, b, :], ACT.Silu).then_inc(s_sl, 1)
                            else:
                                act.wait_ge(s_free, pu.group(i, j) + 1)
                                apart(i)
                                A(h_h[:, ds(i * 2 + b, 1), :].rearrange("p a t -> p (a t)"), tmp[:, b, :],
                                  ACT.Copy).then_inc(s_hhi, 1)
                    turns(act, pu, turn, peel=1 if l == 0 and half == 0 else 0)

                    def state_rows():
                        for q in range(6):
                            n = min(4, FC - 4 * q) * P
                            rows_of(n, FT, R[f"ffn{l}"] + q, f_row[0:FT, q * 512:q * 512 + n])

                    def first_rows():
                        for t in range(5):
                            rows_of(512, P if t < 4 else TS, R["y"] + t, y_row[0][0:P if t < 4 else TS, t, :])
                    residual(pd, f"down{l}{half}", state_rows if half == 1 else None,
                             first_rows if half == 1 and l == 1 else None)

            ffn(0)

            root(SQ["down01"])
            A(cw_h[:, :], params[:, pe_taps:pe_taps + CW * DC], ACT.Copy).then_inc(s_cw, 1)
            act.wait_ge(s_cw, 2)

            def diagonals(c, b):
                if not (isinstance(c, int) and c < 2):
                    act.wait_ge(s_cvp, c - 1)
                apart(c)
                for n, shift in enumerate(PE_SHIFTS):
                    at = (CW - 1 - shift) * DC
                    A(dg_h[:, b, n, :], ident[:, :], ACT.Copy, scale=params[:, ds(c + (pe_taps + at), 1)]).then_inc(s_dgl, 1)
                    A(dg_l[:, b, n, :], ident[:, :], ACT.Copy, scale=cw_l[:, ds(c + at, 1)]).then_inc(s_dgl, 1)

            def turn(i, last):
                for j in range(4):
                    ahead(split_high, ph["pw1"], i, j, last)
                    if j % 2 == 0:
                        diagonals(i * 2 + j // 2, j // 2)
                    if j % 2:
                        c, b = i * 2 + j // 2, j // 2
                        act.wait_ge(s_free, ph["pw1"].group(i, j) + 1)
                        apart(i)
                        A(sg[:, b, :], sg[:, b, :], ACT.Sigmoid, bias=par("b_pw1", c + DC)).then_inc(s_sig, 1)
                        act.wait_ge(s_u, c + 1)
                        A(u_h[:, b, 0:TP], u[:, b, 0:TP], ACT.Copy).then_inc(s_uh, 1)
            turns(act, ph["pw1"], turn, peel=1)
            for q in range(2):
                rows_of(512, UT, R["conv_c"] + q, u_row[:, q * 512:q * 512 + 512])
            for m in range(DC):
                act.wait_ge(s_xc, m + 1)
                if m >= 2:
                    act.wait_ge(s_sqp, m - 1)
                A(sq[:, m % 2, :], yc[:, m, :], ACT.Square).then_inc(s_sq, 1)
            root(SQ["var"])
            for m in range(DC):
                act.wait_ge(s_ty, m + 1)
                if m >= 2:
                    act.wait_ge(s_hlo, HB["pw2"] + m - 1)
                A(tmp[:, m % 2, :], yc[:, m, :], ACT.Silu, scale=par("ln_g", m), bias=par("ln_b", m)).then_inc(s_s32, 1)
                act.wait_ge(s_s32, m + 1)
                A(h_h[:, m, :], tmp[:, m % 2, :], ACT.Copy).then_inc(s_hhi, 1)
            residual(ph["pw2"], "pw2")
            ffn(1)
            for t in (0, 2, 4):
                n = P if t < 4 else TS
                act.wait_ge(s_rows, R["y"] + 5 + t + 1)
                A(y_row[1][0:n, t, :], bank[(R["y"] + 5 + t) % 2][0:n, :], ACT.Copy).then_inc(s_rowsd, 1)

        @block.vector
        def _(dve):
            V = nc.vector
            st = Steps()
            flat = lambda ap: ap.rearrange("p a t -> p (a t)")

            def after():
                dve.wait_ge(s_dve, st.now())

            dve.wait_ge(s_misc, 1)
            V.tensor_copy(params[:, :], bank[0][:, 0:n_rows]).then_inc(s_miscd, 1)
            dve.wait_ge(s_miscd, 1)

            def clear_sum(n):
                if n:
                    dve.wait_ge(s_stat, n)
                V.memset(ssum[:, :], 0.0).then_inc(s_ss, 1)

            def norm_work(stage, m, b):
                name, g0 = GAIN[stage]
                dve.wait_ge(s_sq, m + (8 * SQ[stage] + 1))
                dve.wait_ge(s_ss, m + (9 * ADD[stage] + 1))
                V.tensor_tensor(ssum[:, :], ssum[:, :], sq[:, b, :], ALU.add).then_inc(s_ss, 1)
                dve.wait_ge(s_xhi, m + (8 * NORM[stage] + 1))
                V.scalar_tensor_tensor(flat(xa_l[:, ds(m, 1), :]), flat(x[:, ds(m, 1), :]), par(name, m + g0),
                                       flat(xa_h[:, ds(m, 1), :]).bitcast(F32), ALU.mult, ALU.subtract)\
                 .then_inc(s_xlo, 1)

            def inv_rms(k, n):
                dve.wait_ge(s_stat, n + 1)
                V.tensor_scalar(halves(r_all[:, :]), psum_s[:, :, 0:HT], 1.0 / D, EPS, ALU.mult, ALU.add)\
                 .then_inc(s_var, 1)
                dve.wait_ge(s_r, k + 1)

            def scaled(dst, s, b):
                dve.wait_ge(s_slab, s + 1)
                V.tensor_tensor(halves(dst), gview(b), halves(r_all[:, :]), ALU.mult).then_inc(s_free, 1)

            clear_sum(0)
            for m in range(DC + 1):
                if m < DC:
                    dve.wait_ge(s_tp, m + 1)
                    V.tensor_copy(x[:, m, 0:TP], pair[m % 2][:, 0, :]).then_inc(s_dve, 1)
                    st.tick()
                    V.tensor_copy(x[:, m, TP:T], pair[m % 2][:, 1, 0:TS]).then_inc(s_xnew, 1)
                if m:
                    dve.wait_ge(s_xnew, m)
                    norm_work("init", m - 1, (m - 1) % 2)
            dve.wait_ge(s_misc, 2)
            V.tensor_copy(ext_a[:, :, :, 0:CA - 1],
                          bank[1][:, 0:8 * NB].rearrange("p (c b t) -> p c b t", c=4, b=NB)).then_inc(s_miscd, 1)
            inv_rms(0, 0)
            for g in range(4):
                scaled(qkv[:, g, :], g, g % 2)
            dve.wait_ge(s_misc, 3)
            V.tensor_copy(lf_k[:, :, :].rearrange("p (s h) g -> p s (h g)", s=2), psum_s[:, :, :]).then_inc(s_miscd, 1)
            V.memset(suf[:, :, PG - 1:PG], 0.0).then_inc(s_dve, 1)
            st.tick()
            dve.wait_ge(s_miscd, 3)
            for p in range(PG - 2, -1, -1):
                after()
                V.tensor_tensor(suf[:, :, p:p + 1], suf[:, :, p + 1:p + 2], lf_k[:, :, p + 1:p + 2], ALU.add)\
                 .then_inc(s_dve if p else s_suf, 1)
                if p:
                    st.tick()
            for g in range(4, 8):
                scaled(qkv[:, g, :], g, g % 2)
            dve.wait_ge(s_misc, 4)
            for half in range(2):
                V.tensor_copy(dk[:, :, :, 4 * half:4 * half + 4].rearrange("p b g h -> p h (b g)"),
                              psum_s[:, half, :].rearrange("p (h g) -> p h g", h=4)).then_inc(s_miscd, 1)
            V.memset(seg[:, :], 1.0).then_inc(s_dve, 1)
            st.tick()
            after()
            V.memset(seg[:, TP:T].rearrange("p (b t) -> p b t", t=NT)[:, :, 0:1], 0.0).then_inc(s_dve, 1)
            st.tick()
            for g in range(8, 12):
                scaled(qkv[:, g, :], g, g % 2)
            dve.wait_ge(s_misc, 5)
            V.tensor_tensor(halves(fz[:, :]), psum_s[0:NH, :, 0:HT], halves(r_all[0:NH, :]), ALU.mult)\
             .then_inc(s_miscd, 1)
            dve.wait_ge(s_miscd, 6)
            V.tensor_scalar(fz[:, :], fz[:, :], b_f, None, ALU.add).then_inc(s_fz, 1)
            dve.wait_ge(s_fe, 3)
            V.scalar_tensor_tensor(logf[:, :], fz[:, :], 0.0, fe[:, :], ALU.min, ALU.subtract).then_inc(s_dve, 1)
            st.tick()
            after()
            V.tensor_tensor_scan(cum[:, :], seg[:, :], logf[:, :], 0.0, ALU.mult, ALU.add).then_inc(s_cum, 1)
            dve.wait_ge(s_cum, 1)
            V.tensor_tensor(cnm[:, :, :], ident[0:NH, 0:NH].unsqueeze(2).to_broadcast([NH, NH, TS]),
                            cum[:, TP:T].unsqueeze(1).to_broadcast([NH, NH, TS]), ALU.mult).then_inc(s_cum, 1)

            def head_norm(c):
                dve.wait_ge(s_misc, 6 + c)
                if c >= 2:
                    dve.wait_ge(s_qk, c - 1)
                V.tensor_scalar(halves(tmp[:, c % 2, :]), psum_s[:, :, 0:HT], 1.0 / HD, EPS, ALU.mult, ALU.add)\
                 .then_inc(s_hv, 1)
                dve.wait_ge(s_hrt, c + 1)
                V.scalar_tensor_tensor(qkv[:, c, :], qkv[:, c, :], params[:, prow["qk"][0] + c // 4:prow["qk"][0] + c // 4 + 1],
                                       tmp[:, c % 2, :], ALU.mult, ALU.mult).then_inc(s_qk, 1)

            for c in range(4):
                scaled(u4[:, c, :], 12 + c, c % 2)
                head_norm(c)
            for c in range(4):
                scaled(ssum[:, :], 16 + c, c % 2)
                dve.wait_ge(s_free, 17 + c)
                V.tensor_tensor(u4[:, c, :], ssum[:, :], u4[:, c, :], ALU.mult).then_inc(s_dve, 1)
                st.tick()
                after()
                V.tensor_copy(ext_a[:, c, :, CA - 1:], u4[:, c, TP:T].rearrange("p (b t) -> p b t", t=NT))\
                 .then_inc(s_dve, 1)
                st.tick()
                after()
                for tap in range(CA - 1, -1, -1):
                    k = CA - 1 - tap
                    w = params[:, prow["conv_a"][0] + tap * 4 + c:prow["conv_a"][0] + tap * 4 + c + 1]
                    yp, ys = g4[:, c, k:TP], g4[:, c, TP:T].rearrange("p (b t) -> p b t", t=NT)
                    es = ext_a[:, c, :, tap:tap + NT]
                    if k == 0:
                        V.tensor_scalar(yp, u4[:, c, 0:TP], w, None, ALU.mult).then_inc(s_dve, 1)
                        V.tensor_scalar(ys, es, w, None, ALU.mult).then_inc(s_dve, 1)
                    else:
                        V.scalar_tensor_tensor(yp, u4[:, c, 0:TP - k], w, yp, ALU.mult, ALU.add).then_inc(s_dve, 1)
                        V.scalar_tensor_tensor(ys, es, w, ys, ALU.mult, ALU.add).then_inc(s_dve, 1)
                    st.tick()
                    st.tick()
                    after()
                head_norm(4 + c)
            V.tensor_copy(tail_a[:, :, 0:2], u4[:, :, TP - 2:TP]).then_inc(s_tail, 1)
            V.tensor_copy(tail_a[:, :, 2:FT].rearrange("p c (b t) -> p c b t", b=NB), ext_a[:, :, :, NT:])\
             .then_inc(s_tail, 1)
            for c in range(4):
                scaled(ssum[:, :], 20 + c, c % 2)
                dve.wait_ge(s_free, 21 + c)
                V.tensor_tensor(g4[:, c, :], ssum[:, :], g4[:, c, :], ALU.mult).then_inc(s_ya, 1)
                dve.wait_ge(s_hhi, c + 1)
                V.tensor_tensor(h_l[:, c, :], g4[:, c, :], h_h[:, c, :].bitcast(F32), ALU.subtract).then_inc(s_hlo, 1)
                if c == 0:
                    dve.wait_ge(s_misc, 14)
                    V.tensor_copy(cq, bank[0][:, 0:32]).then_inc(s_dve, 1)
                    V.tensor_copy(cns, bank[0][0:TS, 32:40]).then_inc(s_dve, 1)
                    V.tensor_copy(lf_row[:, 0:4, :], bank[0][:, 64:96].rearrange("p (t h) -> p t h", h=NH))\
                     .then_inc(s_dve, 1)
                    for _ in range(3):
                        st.tick()
                    V.tensor_copy(lf_row[0:TS, 4, :], bank[0][0:TS, 96:104]).then_inc(s_miscd, 1)
                if c == 1:
                    dve.wait_ge(s_misc, 15)
                    V.tensor_copy(cn_all[:, :, :, :].rearrange("p h b t -> p (h b t)"), bank[1][:, 0:NH * TS])\
                     .then_inc(s_miscd, 1)
            dve.wait_ge(s_misc, 16)
            V.tensor_copy(a_out[:, :], bank[0][0:FT, :]).then_inc(s_miscd, 1)
            for h in range(NH):
                if h >= 2:
                    dve.wait_ge(s_cbp, h - 1)
                V.tensor_scalar(cmask[:, h % 2, :], cum[:, 0:TP], ident[0:NH, h:h + 1], None, ALU.mult).then_inc(s_cm, 1)
            dve.wait_ge(s_qk, 8)
            for c in range(4):
                for hh in range(2):
                    V.tensor_scalar(q_diag[HD * hh:HD * hh + HD, c, :, NT * hh:NT * hh + NT],
                                    qkv[HD * hh:HD * hh + HD, c, TP:T].rearrange("p (b t) -> p b t", t=NT),
                                    HD ** -0.5, None, ALU.mult).then_inc(s_qd, 1)
            V.tensor_tensor(nbias[:, :, :, :], nbias[:, :, :, :],
                            cns.unsqueeze(1).unsqueeze(3).to_broadcast([TS, NB, NH, NT]), ALU.subtract)\
             .then_inc(s_dve, 1)
            st.tick()
            after()
            def attended(i):
                dve.wait_ge(s_po, i * 8 + 8)
                V.tensor_scalar(flat(qkv[:, ds(i, 1), 0:TP]), psum_s[:, 1, :], 1.0, None, ALU.mult).then_inc(s_pod, 1)

            def bias(b, w):
                n = (w + 1) * P
                dve.wait_ge(s_s, b * 4 + (w + 1))
                V.scalar_tensor_tensor(sb[:, w, 0:n], pb[2][:, 0:n], small[:, ds(b + (160 + w * NH), 1)],
                                       flat(cb[:, ds(b, 1), 0:n]), ALU.add, ALU.subtract).then_inc(s_sbr, 1)
                dve.wait_ge(s_sbr, b * 4 + (w + 1))
                V.tensor_tensor(sb[:, w, n - P:n], sb[:, w, n - P:n], causal[:, :], ALU.add).then_inc(s_dve, 1)
                st.tick()
                after()
                V.tensor_reduce(rmax[:, w:w + 1], sb[:, w, 0:n], AX.X, ALU.max, negate=True).then_inc(s_sb, 1)

            def norm(b, w):
                n = (w + 1) * P
                dve.wait_ge(s_pe, b * 4 + (w + 1))
                V.reciprocal(rinv[:, w:w + 1], rsum[:, w:w + 1]).then_inc(s_dve, 1)
                st.tick()
                after()
                V.tensor_scalar(sb[:, w, 0:n], sb[:, w, 0:n], rinv[:, w:w + 1], None, ALU.mult).then_inc(s_pn, 1)

            wide = lambda ap, n: ap.unsqueeze(1).to_broadcast([P, n, 32])

            def logits(b):
                dve.wait_ge(s_sc, b + 1)
                V.tensor_tensor(sc[:, 0:PG, :].rearrange("p g (h q) -> p (g h) q", q=NT),
                                psum_s[:, 0, :].rearrange("p (g q) -> p g q", q=NT),
                                dk[:, ds(b, 1), :, :].rearrange("p b g h -> p (b g h)").unsqueeze(2)
                                .to_broadcast([P, PG * NH, NT]), ALU.add).then_inc(s_dve, 1)
                st.tick()
                V.tensor_tensor(sc[0:TS, PG, :], bank[1][0:TS, 256:288],
                                nbias[:, ds(b, 1), :, :].rearrange("p b h q -> p (b h q)"), ALU.add).then_inc(s_sev, 1)
                dve.wait_ge(s_sev, b + 1)
                after()
                V.tensor_tensor(sc[:, :, :].rearrange("p g (h q) -> p g h q", q=NT),
                                sc[:, :, :].rearrange("p g (h q) -> p g h q", q=NT),
                                cn_all[:, :, ds(b, 1), :].rearrange("p h b t -> p (h b) t").unsqueeze(1)
                                .to_broadcast([P, PG + 1, NH, NT]), ALU.add).then_inc(s_dve, 1)
                st.tick()
                after()
                V.tensor_reduce(m1, sc[:, :, :].rearrange("p g x -> p x g"), AX.X, ALU.max).then_inc(s_m1, 1)

            def biggest(b):
                dve.wait_ge(s_mt, b + 1)
                V.tensor_reduce(gmax, bank[1][0:32, 0:P], AX.X, ALU.max).then_inc(s_dve, 1)
                st.tick()
                after()
                V.tensor_scalar(diag, ident[0:32, 0:32], gmax, None, ALU.mult).then_inc(s_dg, 1)

            def shift(b):
                dve.wait_ge(s_mb, b + 1)
                V.tensor_tensor(sc[:, :, :], sc[:, :, :], wide(bank[1][:, P:P + 32], PG + 1), ALU.subtract)\
                 .then_inc(s_sm, 1)

            def total(b, par):
                dve.wait_ge(s_p, b + 1)
                V.tensor_reduce(p_sum, pr[:, :, :].rearrange("p g x -> p x g"), AX.X, ALU.add).then_inc(s_lp, 1)
                dve.wait_ge(s_ph, b + 1)
                V.tensor_tensor(pr_l[:, par, :, :], pr[:, :, :], pr_h[:, par, :, :].bitcast(F32), ALU.subtract)\
                 .then_inc(s_pl, 1)

            def key_low(b, p):
                dve.wait_ge(s_kt, b * PG + (p + 1))
                V.tensor_tensor(kt_l[:, p % 2, :], pb[p % 2], kt_h[:, p % 2, :].bitcast(F32), ALU.subtract)\
                 .then_inc(s_kl, 1)

            def inverse(b):
                dve.wait_ge(s_l, b + 1)
                if not (isinstance(b, int) and b == 0):
                    dve.wait_ge(s_oev, b)
                V.reciprocal(rec, bank[1][0:TS, 192:193]).then_inc(s_rec, 1)

            def values(b):
                dve.wait_ge(s_pvp, b * PG + PG)
                dve.wait_ge(s_rec, b + 1)
                if not (isinstance(b, int) and b == 0):
                    dve.wait_ge(s_ow, b)
                V.scalar_tensor_tensor(own[:, :], bank[0][0:TS, :], rec, blocks[:, :], ALU.mult, ALU.mult)\
                 .then_inc(s_oev, 1)

            def placed(b):
                dve.wait_ge(s_ow, b + 1)
                V.tensor_scalar(qkv[:, 0:4, ds(b * NT + TP, NT)], bank[1][:, 320:336].rearrange("p (c t) -> p c t", t=NT),
                                1.0, None, ALU.mult).then_inc(s_owr, 1)

            V.tensor_reduce(pick, ident[0:TS, 0:TS].rearrange("p (h t) -> p t h", t=NT), AX.X, ALU.add).then_inc(s_pick, 1)
            dve.wait_ge(s_qd, 9)
            V.tensor_tensor(qd_l[:, :, :, :], q_diag[:, :, :, :], qd_h[:, :, :, :].bitcast(F32), ALU.subtract)\
             .then_inc(s_qd, 1)
            dve.wait_ge(s_vn, 1)
            V.tensor_tensor(vn_l[:, :], s_row[:, 1, :], vn_h[:, :].bitcast(F32), ALU.subtract).then_inc(s_vn, 1)
            dve.wait_ge(s_blk, 3)
            dve.wait_ge(s_aout, 32)

            def batch(i, bb):
                b = i * 2 + bb
                known = isinstance(b, int)
                before = not (known and b == 0)
                if bb == 0 and not known:
                    attended(i - 1)
                for p in range(PG):
                    if p == 2 and before:
                        biggest(b - 1)
                    if p == 4 and before:
                        shift(b - 1)
                    key_low(b, p)
                    if p % 4 == 1:
                        bias(b, p // 4)
                    if p % 4 == 2:
                        norm(b, p // 4)
                    if p == 6 and before:
                        total(b - 1, 1 - bb)
                    if p == 7 and not known:
                        values(b - 2)
                    if p == 8 and before:
                        inverse(b - 1)
                    if p == 10 and not known:
                        placed(b - 2)
                logits(b)
            batch(0, 0)
            batch(0, 1)
            with st.loop(dve, 1, NB // 2, 22) as i:
                batch(i, 0)
                batch(i, 1)
            attended(3)
            biggest(NB - 1)
            shift(NB - 1)
            total(NB - 1, 1)
            values(NB - 2)
            inverse(NB - 1)
            placed(NB - 2)
            values(NB - 1)
            placed(NB - 1)
            after()
            for c in range(4):
                dve.wait_ge(s_hhi, 5 + c)
                V.tensor_tensor(h_l[:, 4 + c, :], qkv[:, c, :], h_h[:, 4 + c, :].bitcast(F32), ALU.subtract)\
                 .then_inc(s_hlo, 1)

            def residual(phase, stage):
                if stage in NORM:
                    clear_sum(SUM[stage])
                per_turn = 4 // phase.per_group
                with dve.Fori(0, phase.turns) as i:
                    for q in range(per_turn):
                        m = i * per_turn + q
                        dve.wait_ge(s_slab, phase.slab(i, (q + 1) * phase.per_group - 1) + 1)
                        V.tensor_tensor(halves(flat(x[:, ds(m, 1), :])), gview(q % 2), halves(flat(x[:, ds(m, 1), :])),
                                        ALU.add).then_inc(s_xnew, 1)
                        dve.wait_ge(s_xnew, m + (XN[stage] + 1))
                        if stage in NORM:
                            norm_work(stage, m, q % 2)

            residual(ph["out"], "out")

            def ffn(l):
                dve.wait_ge(s_fst, 1 + 5 * l)
                V.tensor_copy(ext_f[:, :, :, 0:CF - 1].rearrange("p c b t -> p c b t"),
                              bank[0][:, 0:FC * 2 * NB].rearrange("p (c b t) -> p c b t", c=FC, b=NB)).then_inc(s_fstd, 1)
                dve.wait_ge(s_fstd, 1 + 5 * l)
                inv_rms(SQ["out" if l == 0 else "pw2"], SUM["out" if l == 0 else "pw2"])
                for half in range(2):
                    pu, pd = ph[f"up{l}{half}"], ph[f"down{l}{half}"]
                    with st.loop(dve, 0, pu.turns, 2 * 6) as i:
                        for b in range(2):
                            kc = i * 2 + (half * HALF[0] + b)
                            k = i * 2 + (half * HALF[0] + b + HB[f"up{l}"])
                            e = lambda lo, hi: ext_f[:, ds(kc, 1), :, lo:hi].rearrange("p a b t -> p (a b) t")
                            scaled(gate[:, b, :], pu.slab(i, 2 * b), 0)
                            dve.wait_ge(s_free, pu.group(i, 2 * b) + 1)
                            V.tensor_copy(e(CF - 1, CF - 1 + NT), gate[:, b, TP:T].rearrange("p (b t) -> p b t", t=NT))\
                             .then_inc(s_dve, 1)
                            st.tick()
                            V.tensor_copy(flat(tail_f[:, ds(kc, 1), 0:2]), gate[:, b, TP - 2:TP]).then_inc(s_tail, 1)
                            after()
                            ys = cv[:, b, TP:T].rearrange("p (b t) -> p b t", t=NT)
                            for tap in range(CF - 1, -1, -1):
                                n = CF - 1 - tap
                                w = par("conv_f", kc + (l * CF * FC + tap * FC))
                                yp = cv[:, b, n:TP]
                                if n == 0:
                                    V.tensor_scalar(yp, gate[:, b, 0:TP], w, None, ALU.mult).then_inc(s_dve, 1)
                                    st.tick()
                                    V.tensor_scalar(ys, e(tap, tap + NT), w, None, ALU.mult).then_inc(s_dve, 1)
                                    st.tick()
                                    after()
                                    continue
                                V.scalar_tensor_tensor(yp, gate[:, b, 0:TP - n], w, yp, ALU.mult, ALU.add)\
                                 .then_inc(s_dve, 1)
                                st.tick()
                                if n < CF - 1:
                                    V.scalar_tensor_tensor(ys, e(tap, tap + NT), w, ys, ALU.mult, ALU.add)\
                                     .then_inc(s_dve, 1)
                                    st.tick()
                                    after()
                                else:
                                    V.scalar_tensor_tensor(ys, e(tap, tap + NT), w, ys, ALU.mult, ALU.add)\
                                     .then_inc(s_cv, 1)
                            dve.wait_ge(s_slab, pu.slab(i, 2 * b + 1) + 1)
                            dve.wait_ge(s_sr, i * 2 + (l * FC + half * HALF[0] + b + 1))
                            V.tensor_tensor(halves(tmp[:, b, :]), gview(1), halves(sr[:, b, :]), ALU.mult).then_inc(s_free, 1)
                            dve.wait_ge(s_hhi, k + 1)
                            V.tensor_tensor(flat(h_l[:, ds(i * 2 + b, 1), :]), tmp[:, b, :],
                                            flat(h_h[:, ds(i * 2 + b, 1), :]).bitcast(F32), ALU.subtract).then_inc(s_hlo, 1)
                    if half == 1:
                        V.tensor_copy(tail_f[:, :, 2:FT].rearrange("p c (b t) -> p c b t", b=NB), ext_f[:, :, :, NT:])\
                         .then_inc(s_tail, 1)
                    residual(pd, f"down{l}{half}")

            ffn(0)

            for q in range(4):
                dve.wait_ge(s_fst, 2 + q)
                V.tensor_copy(ext_c[:, 2 * q:2 * q + 2, :, 0:CC - 1],
                              bank[q % 2][:, 0:480].rearrange("p (c b t) -> p c b t", c=2, b=NB)).then_inc(s_fstd, 1)
            inv_rms(SQ["down01"], SUM["down01"])
            clear_sum(SUM["mean"])
            dve.wait_ge(s_out, 16 * n_out[1])
            dve.wait_ge(s_cw, 1)
            V.tensor_tensor(cw_l[:, :], params[:, pe_taps:pe_taps + CW * DC], cw_h[:, :].bitcast(F32), ALU.subtract)\
             .then_inc(s_cw, 1)
            taps = params[:, prow["conv_c"][0]:prow["conv_c"][0] + CC * DC].rearrange("p (k c) -> p c k", c=DC)
            def combine(c, b):
                after()
                n0, n1 = DVE_SHIFTS[0:2]
                V.tensor_tensor(tmp[:, b, n1:TP], tmp[:, b, n1:TP], sg[:, b, n1:TP], ALU.add)\
                 .then_inc(s_dve, 1)
                st.tick()
                after()
                dve.wait_ge(s_cvp, c + 1)
                V.tensor_scalar(flat(yc[:, ds(c, 1), 0:n0]), bank[b][:, 0:n0], par("conv_cb", c), None, ALU.add)\
                 .then_inc(s_dve, 1)
                st.tick()
                V.scalar_tensor_tensor(flat(yc[:, ds(c, 1), n0:TP]), bank[b][:, n0:TP], par("conv_cb", c),
                                       tmp[:, b, n0:TP], ALU.add, ALU.add).then_inc(s_cvr, 1)
                dve.wait_ge(s_cvr, c + 1)
                dve.wait_ge(s_ss, c + (9 * ADD["mean"] + 1))
                V.tensor_tensor(ssum[:, :], ssum[:, :], flat(yc[:, ds(c, 1), :]), ALU.add).then_inc(s_ss, 1)

            def chunk(i, b):
                c = i * 2 + b
                known = isinstance(c, int)
                ue = lambda lo, hi: ext_c[:, ds(c, 1), :, lo:hi].rearrange("p a b t -> p (a b) t")
                scaled(ua[:, b, :], ph["pw1"].slab(i, 2 * b), 0)
                dve.wait_ge(s_slab, ph["pw1"].slab(i, 2 * b + 1) + 1)
                V.tensor_tensor(halves(sg[:, b, :]), gview(1), halves(r_all[:, :]), ALU.mult).then_inc(s_free, 1)
                if not (known and c == 0):
                    combine(c - 1, 1 - b)
                dve.wait_ge(s_sig, c + 1)
                V.scalar_tensor_tensor(u[:, b, :], ua[:, b, :], par("b_pw1", c), sg[:, b, :], ALU.add, ALU.mult)\
                 .then_inc(s_u, 1)
                dve.wait_ge(s_u, c + 1)
                V.tensor_copy(flat(tail_c[:, ds(c, 1), :]), u[:, b, T - UT:T]).then_inc(s_ux, 1)
                V.tensor_copy(ue(CC - 1, CC - 1 + NT), u[:, b, TP:T].rearrange("p (b t) -> p b t", t=NT))\
                 .then_inc(s_dve, 1)
                st.tick()
                after()
                for t in range(NT):
                    V.tensor_tensor(prod[:, :, :].rearrange("p (b t) k -> p b t k", t=NT)[:, :, t, :],
                                    ue(t, t + CC), taps[:, ds(c, 1), :].to_broadcast([P, NB, CC]), ALU.mult)\
                     .then_inc(s_dve, 1)
                    st.tick()
                after()
                V.tensor_reduce(flat(yc[:, ds(c, 1), TP:T]), prod[:, :, :], AX.X, ALU.add).then_inc(s_dve, 1)
                st.tick()
                after()
                V.tensor_scalar(flat(yc[:, ds(c, 1), TP:T]), flat(yc[:, ds(c, 1), TP:T]), par("conv_cb", c), None,
                                ALU.add).then_inc(s_dve, 1)
                st.tick()
                for k, n in enumerate(DVE_SHIFTS):
                    w = par("conv_c", c + (CC - 1 - n) * DC)
                    yp = (tmp, sg)[k % 2][:, b, n:TP]
                    if k < 2:
                        V.tensor_scalar(yp, u[:, b, 0:TP - n], w, None, ALU.mult).then_inc(s_dve, 1)
                    else:
                        dve.wait_ge(s_dve, st.now() - 1)
                        V.scalar_tensor_tensor(yp, u[:, b, 0:TP - n], w, yp, ALU.mult, ALU.add).then_inc(s_dve, 1)
                    st.tick()

            chunk(0, 0)
            chunk(0, 1)
            with st.loop(dve, 1, ph["pw1"].turns, 2 * (7 + CC - PT + 2)) as i:
                chunk(i, 0)
                chunk(i, 1)
            combine(DC - 1, 1)
            dve.wait_ge(s_stat, SUM["mean"] + 1)
            V.tensor_scalar(halves(r_all[:, :]), psum_s[:, :, 0:HT], 1.0 / D, None, ALU.mult).then_inc(s_mu, 1)
            dve.wait_ge(s_mu, 1)
            for m in range(DC):
                V.tensor_tensor(yc[:, m, :], yc[:, m, :], r_all[:, :], ALU.subtract).then_inc(s_xc, 1)
            inv_rms(SQ["var"], SUM["var"])
            for m in range(DC + 1):
                if m < DC:
                    dve.wait_ge(s_xc, m + 1)
                    V.tensor_tensor(yc[:, m, :], yc[:, m, :], r_all[:, :], ALU.mult).then_inc(s_ty, 1)
                if m:
                    dve.wait_ge(s_hhi, HB["pw2"] + m)
                    V.tensor_tensor(h_l[:, m - 1, :], tmp[:, (m - 1) % 2, :], h_h[:, m - 1, :].bitcast(F32), ALU.subtract)\
                     .then_inc(s_hlo, 1)
            residual(ph["pw2"], "pw2")
            ffn(1)
            for t in (1, 3):
                dve.wait_ge(s_rows, R["y"] + 5 + t + 1)
                V.tensor_copy(y_row[1][:, t, :], bank[(R["y"] + 5 + t) % 2][:, :]).then_inc(s_yd, 1)

        @block.tensor
        def _(pe):
            mm, tr = nc.tensor.matmul, nc.tensor.transpose
            xa = lambda t: (xa_h[:, t, :], xa_l[:, t, :])
            hid = lambda t: (h_h[:, t, :], h_l[:, t, :])

            def slab(phase, i, j, moving, ready=None):
                first, last = j % phase.per_group == 0, j % phase.per_group == phase.per_group - 1
                s, g = phase.slab(i, j), phase.group(i, j)
                pe.wait_ge(s_lo, s + 1)
                if first:
                    bank_free(phase, i, j // phase.per_group, g)
                out = pair[(j // phase.per_group) % 2]
                for t in range(phase.tiles):
                    k = t + (0 if first else phase.tiles)
                    if ready:
                        ready(k)
                    hi, lo = moving(k)
                    wh, wl = w_h[:, j, t * P:(t + 1) * P], w_l[:, j, t * P:(t + 1) * P]
                    for n, (w, v) in enumerate(((wh, hi), (wh, lo), (wl, hi))):
                        for half in range(2):
                            ins = mm(out[:, half, 0:HT], w, v[:, half * HT:(half + 1) * HT],
                                     start=first and t == 0 and n == 0,
                                     stop=last and t == phase.tiles - 1 and n == 2)
                ins.then_inc(s_slab, 1)

            def bank_free(phase, i, q, g):
                if isinstance(i, int) and i == 0 and q < 2:
                    if phase is not order[0]:
                        before = order[order.index(phase) - 1]
                        pe.wait_ge(s_xnew if before.residual else s_free, before.group1 - 1 + q)
                else:
                    pe.wait_ge(s_xnew if phase.residual else s_free, g - 1)

            def sum_channels():
                for half in range(2):
                    ins = mm(psum_s[:, half, 0:HT], ones[:, :], ssum[:, half * HT:(half + 1) * HT], start=True, stop=True)
                ins.then_inc(s_stat, 1)

            pe.wait_ge(s_cst, 15)
            pe.wait_ge(s_prm, 16 * (4 + sum(len(row_blocks(*v)) for name, v in prow.items() if name != "qk")))
            for blk in range(4):
                n = min(P, n_rows - blk * P)
                ins = tr(bank[0][:, blk * P:blk * P + n], p_rows[0:n, blk, :], ident[0:n, 0:n])
            ins.then_inc(s_misc, 1)
            pe.wait_ge(s_xld, 16 * 5)
            for m in range(DC):
                if m >= 2:
                    pe.wait_ge(s_xnew, m - 1)
                for t in range(4):
                    tr(pair[m % 2][:, 0, t * P:(t + 1) * P], x_rows[:, t, m * P:(m + 1) * P], ident[:, :])
                tr(pair[m % 2][:, 1, 0:TS], x_rows[0:TS, 4, m * P:(m + 1) * P], ident[0:TS, 0:TS]).then_inc(s_tp, 1)
            pe.wait_ge(s_st, 16)
            for c in range(4):
                ins = tr(bank[1][:, c * 2 * NB:(c + 1) * 2 * NB], a_row[:, c * P:(c + 1) * P], ident[0:2 * NB, 0:2 * NB])
            ins.then_inc(s_misc, 1)
            pe.wait_ge(s_xnew, DC)

            p = ph["qkv"]
            for i in range(3):
                for j in range(4):
                    slab(p, i, j, xa, (lambda k: pe.wait_ge(s_xlo, k + 1)) if i == j == 0 else None)
                    if i == j == 0:
                        pe.wait_ge(s_ss, 9)
                        sum_channels()
                if i == 0:
                    pe.wait_ge(s_lf, 16)
                    pe.wait_ge(s_var, 1)
                    for h in range(NH):
                        ins = tr(psum_s[:, h // 4, (h % 4) * P:(h % 4 + 1) * P],
                                 lf_pg[:, :].rearrange("p (k h) -> p h k", h=NH)[:, h, :], ident[:, :])
                    ins.then_inc(s_misc, 1)
                if i == 1:
                    pe.wait_ge(s_miscd, 3)
                    pe.wait_ge(s_suf, 1)
                    lf2, suf2 = (ap[:, :, :].rearrange("p h g -> p (h g)") for ap in (lf_k, suf))
                    for half in range(2):
                        at = slice(half * 512, half * 512 + 512)
                        mm(psum_s[:, half, :], later[:, :], lf2[:, at], start=True, stop=False)
                        ins = mm(psum_s[:, half, :], ones[:, :], suf2[:, at], start=False, stop=True)
                    ins.then_inc(s_misc, 1)
            pe.wait_ge(s_fw, 34)
            pe.wait_ge(s_miscd, 5)
            for t in range(DC):
                for n, (w, v) in enumerate(((fw_h, xa_h), (fw_h, xa_l), (fw_l, xa_h))):
                    for half in range(2):
                        ins = mm(psum_s[0:NH, half, 0:HT], w[:, t, :], v[:, t, half * HT:(half + 1) * HT],
                                 start=t == 0 and n == 0, stop=t == DC - 1 and n == 2)
            ins.then_inc(s_misc, 1)
            p = ph["gates"]
            for i in range(3):
                for j in range(4):
                    slab(p, i, j, xa)
                    c = 4 * i + j
                    if c < 8:
                        pe.wait_ge(s_qsq, c + 1)
                        if c:
                            pe.wait_ge(s_hv, c)
                        else:
                            pe.wait_ge(s_miscd, 6)
                        for half in range(2):
                            ins = mm(psum_s[:, half, 0:HT], head_ones[:, :], sq[:, c % 2, half * HT:(half + 1) * HT],
                                     start=True, stop=True)
                        ins.then_inc(s_misc, 1)
                    if c == 8:
                        pe.wait_ge(s_cum, 1)
                        pe.wait_ge(s_miscd, 2)
                        for t in range(4):
                            tr(bank[0][:, t * NH:(t + 1) * NH], cum[:, t * P:(t + 1) * P], ident[0:NH, 0:NH])
                            tr(bank[0][:, 64 + t * NH:64 + (t + 1) * NH], logf[:, t * P:(t + 1) * P], ident[0:NH, 0:NH])
                        tr(bank[0][0:TS, 32:40], cum[:, TP:T], ident[0:NH, 0:NH])
                        tr(bank[0][0:TS, 96:104], logf[:, TP:T], ident[0:NH, 0:NH]).then_inc(s_misc, 1)
                    if c == 9:
                        pe.wait_ge(s_cum, 2)
                        mm(bank[1][:, 0:NH * TS], ones[0:NH, :], cnm[:, :, :].rearrange("p h t -> p (h t)"),
                           start=True, stop=True).then_inc(s_misc, 1)
            pe.wait_ge(s_tail, 2)
            pe.wait_ge(s_miscd, 7)
            for c in range(4):
                ins = tr(bank[0][0:FT, c * P:(c + 1) * P], tail_a[:, c, :], ident[:, :])
            ins.then_inc(s_misc, 1)
            for h in range(NH):
                pe.wait_ge(s_cm, h + 1)
                pe.wait_ge(s_miscd, 8 if h == 0 else 9)
                if h >= 2:
                    pe.wait_ge(s_cb, h - 1)
                mm(bank[(h + 1) % 2][:, :], ones[0:NH, :], cmask[:, h % 2, :], start=True, stop=True).then_inc(s_cbp, 1)
            pe.wait_ge(s_qk, 8)
            pe.wait_ge(s_cb, NH)
            for t in range(5):
                for kv in range(2):
                    n = P if t < 4 else TS
                    if t:
                        pe.wait_ge(s_rowsd, 2 * t + kv - 1)
                    for c in range(4):
                        ins = tr(bank[kv][0:n, c * P:(c + 1) * P], qkv[:, 4 + 4 * kv + c, t * P:t * P + n], ident[:, :])
                    ins.then_inc(s_rows, 1)

            pe.wait_ge(s_rowsd, R["kv"] + 10)
            pe.wait_ge(s_free, ph["gates"].group1)

            def p_score(b, bb, w):
                n = (w + 1) * P
                rows = slice(HD * bb, HD * bb + HD)
                mm(pb[2][:, 0:n], q_s[rows, w * P:(w + 1) * P], k_s[rows, 0:n], start=True, stop=True).then_inc(s_s, 1)

            def p_turn(b, w):
                pe.wait_ge(s_pn, b * 4 + (w + 1))
                for kb in range(w + 1):
                    ins = tr(pb[2][:, kb * P:(kb + 1) * P], sb[:, w, kb * P:(kb + 1) * P], ident[:, :])
                ins.then_inc(s_ptt, 1)

            def p_value(b, bb, w):
                pe.wait_ge(s_ptc, b * 4 + (w + 1))
                rows = slice(HD * bb, HD * bb + HD)
                for kb in range(w + 1):
                    ins = mm(psum_s[rows, 1, w * P:(w + 1) * P], v_s[:, kb, rows], pt[:, w % 2, kb * P:(kb + 1) * P],
                             start=kb == 0, stop=kb == w)
                ins.then_inc(s_po, 1)

            pe.wait_ge(s_qd, 10)
            pe.wait_ge(s_vn, 2)
            pe.wait_ge(s_pick, 1)

            def turn_page(b, p):
                pe.wait_ge(s_k[p % KS], b * 32 + 16 * (p // KS + 1))
                for c in range(4):
                    ins = tr(pb[p % 2][:, c * P:(c + 1) * P], k_pg[:, p % KS, c * P:(c + 1) * P], ident[:, :])
                ins.then_inc(s_tr, 1)

            def score_page(b, bb, p):
                pe.wait_ge(s_kl, b * PG + (p + 1))
                for c in range(4):
                    for n, (q, k) in enumerate(((qs_h, kt_h), (qs_l, kt_h), (qs_h, kt_l))):
                        ins = mm(pb[3][0:TS, (p % 4) * P:(p % 4 + 1) * P],
                                 q[bb][:, :, :].rearrange("p c x -> p (c x)")[:, c * 32:(c + 1) * 32],
                                 k[:, p % 2, c * P:(c + 1) * P], start=c == 0 and n == 0, stop=c == 3 and n == 2)
                ins.then_inc(s_sp, 1)

            def keys_back(g):
                for n in range(4):
                    p = g * 4 + n
                    ins = tr(psum_s[:, 0, p * 32:(p + 1) * 32], s_t[:, n * P:(n + 1) * P], ident[0:TS, 0:TS])
                return ins

            def max_turn(b):
                pe.wait_ge(s_m1, b + 1)
                tr(bank[1][0:32, 0:P], m1, ident[:, :]).then_inc(s_mt, 1)

            def max_spread(b):
                pe.wait_ge(s_dg, b + 1)
                mm(bank[1][:, P:P + 32], ones[0:32, :], diag, start=True, stop=True).then_inc(s_mb, 1)

            def exp_sums(b):
                pe.wait_ge(s_lp, b + 1)
                pe.wait_ge(s_pl, b + 1)
                if not (isinstance(b, int) and b == 0):
                    pe.wait_ge(s_oev, b)
                mm(bank[1][0:TS, 192:193], p_sum, ones[:, 0:1], start=True, stop=True).then_inc(s_l, 1)

            def values_of(p, v, n, first, last):
                for k, (e, w) in enumerate(((pr_h, v[0]), (pr_h, v[1]), (pr_l, v[0]))):
                    ins = mm(bank[0][0:TS, :], e[0:n, p[0], p[1], :], w, start=first and k == 0, stop=last and k == 2)
                return ins

            def value_new(b, par):
                values_of((par, PG), (vn_h[:, :], vn_l[:, :]), TS, True, False)

            def value_page(b, par, p):
                if p == 0:
                    value_new(b, par)
                pe.wait_ge(s_vl, b * PG + (p + 1))
                values_of((par, p), (v_h[:, p % 4, :], v_l[:, p % 4, :]), P, False, p == PG - 1).then_inc(s_pvp, 1)

            def own_heads(b):
                pe.wait_ge(s_oev, b + 1)
                pe.wait_ge(s_rec, NB if isinstance(b, int) and b == NB - 1 else b + 2)
                for c in range(4):
                    ins = mm(bank[1][:, 320 + c * NT:320 + (c + 1) * NT], own[:, c * P:(c + 1) * P], pick,
                             start=True, stop=True)
                ins.then_inc(s_ow, 1)

            def batch(i, bb):
                b = i * 2 + bb
                known = isinstance(b, int)
                before = not (known and b == 0)
                for p in range(PG):
                    if before and p == 2:
                        max_turn(b - 1)
                    if before and p == 4:
                        max_spread(b - 1)
                    if before and p == 8:
                        exp_sums(b - 1)
                    turn_page(b, p)
                    if p < 8 and not known:
                        value_page(b - 2, bb, p + 8)
                    if p >= 8 and before:
                        value_page(b - 1, 1 - bb, p - 8)
                    if p == 10 and not known:
                        own_heads(b - 2)
                    if p == 5 and before:
                        pe.wait_ge(s_sev, b)
                    if p % 4 == 1 and p > 1:
                        pe.wait_ge(s_stc, b * 4 + p // 4)
                    if p == 1:
                        pe.wait_ge(s_qb, b * 2 + 2)
                    if p:
                        score_page(b, bb, p - 1)
                    if p % 4 == 1 and p > 1:
                        keys_back(p // 4 - 1)
                    if p % 4 == 0 and p:
                        if p == 4 and bb == 0:
                            pe.wait_ge(s_qs, i * 3 + 3)
                            if not known:
                                pe.wait_ge(s_pod, i)
                        p_value(b, bb, p // 4 - 1)
                    if p % 4 == 1:
                        if p == 1 and bb == 0:
                            pe.wait_ge(s_qs, i * 3 + 2)
                        p_score(b, bb, p // 4)
                    if p % 4 == 3:
                        p_turn(b, p // 4)
                score_page(b, bb, PG - 1)
                p_value(b, bb, 3)
                pe.wait_ge(s_stc, b * 4 + 4)
                if not known:
                    pe.wait_ge(s_owr, b - 1)
                for c in range(4):
                    ins = mm(bank[1][0:TS, 256 + c * 8:256 + c * 8 + 8], qkv[:, 4 + c, TP:T],
                             q_diag[:, c, ds(b, 1), :].rearrange("p a x -> p (a x)"), start=True, stop=True)
                keys_back(3).then_inc(s_sc, 1)

            batch(0, 0)
            batch(0, 1)
            with pe.Fori(1, NB // 2) as i:
                batch(i, 0)
                batch(i, 1)
            max_turn(NB - 1)
            for p in range(4):
                value_page(NB - 2, 0, 8 + p)
            max_spread(NB - 1)
            for p in range(4, 8):
                value_page(NB - 2, 0, 8 + p)
            exp_sums(NB - 1)
            own_heads(NB - 2)
            for p in range(PG):
                value_page(NB - 1, 1, p)
            own_heads(NB - 1)

            def gemm(phase, moving, ready, between=None, after_two=None, then=None, late=None):
                seen = set()

                def once(k):
                    if k not in seen:
                        seen.add(k)
                        ready(k)
                for j in range(4):
                    slab(phase, 0, j, moving, once)
                    if j == 0 and between:
                        between()
                    if after_two and j % 2:
                        after_two(0, j // 2)
                if then:
                    then()
                with pe.Fori(1, phase.turns - (1 if late else 0)) as i:
                    for j in range(4):
                        slab(phase, i, j, moving)
                        if after_two and j % 2:
                            after_two(i, j // 2)
                if late:
                    late()
                    for j in range(4):
                        slab(phase, phase.turns - 1, j, moving)

            def sums(name):
                def go():
                    pe.wait_ge(s_ss, 9 * ADD[name] + 9)
                    sum_channels()
                return go
            low_ready = lambda base: lambda k: pe.wait_ge(s_hlo, base + k + 1)
            xa_ready = lambda n: lambda k: pe.wait_ge(s_xlo, 8 * n + k + 1)

            gemm(ph["out"], hid, low_ready(HB["out"]))

            def rows_out(group, src, parts, n, busy):
                if busy:
                    pe.wait_ge(s_rowsd, group - 1)
                for c in range(n):
                    ins = tr(bank[group % 2][0:parts, c * P:(c + 1) * P], src(c), ident[:, :])
                ins.then_inc(s_rows, 1)

            def ffn(l):
                pe.wait_ge(s_st, 16 * (2 if l == 0 else 5))
                for c in range(FC):
                    ins = tr(bank[0][:, c * 2 * NB:(c + 1) * 2 * NB], f_row[0:2 * NB, c * P:(c + 1) * P],
                             ident[0:2 * NB, 0:2 * NB])
                ins.then_inc(s_fst, 1)
                n = "out" if l == 0 else "pw2"
                for half in range(2):
                    gemm(ph[f"up{l}{half}"], xa, xa_ready(NORM[n]), sums(n) if half == 0 else None)

                    def state_rows():
                        pe.wait_ge(s_tail, 2 + (l + 1) * (FC + 1))
                        for q in range(6):
                            rows_out(R[f"ffn{l}"] + q, lambda c: tail_f[:, 4 * q + c, :], FT, min(4, FC - 4 * q), q >= 2)

                    def first_rows():
                        pe.wait_ge(s_xnew, XN["down11"] + 4)
                        for t in range(5):
                            rows_out(R["y"] + t, lambda c: x[:, c, t * P:t * P + (P if t < 4 else TS)],
                                     P if t < 4 else TS, 4, True)
                    gemm(ph[f"down{l}{half}"], hid, low_ready(HB[f"up{l}"] + half * HALF[0]),
                         then=state_rows if half == 1 else None, late=first_rows if half == 1 and l == 1 else None)

            ffn(0)
            pe.wait_ge(s_st, 16 * 4)
            for q in range(4):
                if q >= 2:
                    pe.wait_ge(s_fstd, 1 + q - 1)
                for c in range(2):
                    for k in range(2):
                        ins = tr(bank[q % 2][:, c * 240 + k * 120:c * 240 + k * 120 + 120],
                                 c_row[:, k, (2 * q + c) * P:(2 * q + c + 1) * P], ident[0:120, 0:120])
                ins.then_inc(s_fst, 1)
            def pe_conv(c, b):
                pe.wait_ge(s_dgl, c * (2 * PT) + 2 * PT)
                if not (isinstance(c, int) and c < 2):
                    pe.wait_ge(s_cvr, c - 1)
                pe.wait_ge(s_ul, c + 1)
                for n, shift in enumerate(PE_SHIFTS):
                    for k, (d, v) in enumerate(((dg_h, u_h), (dg_h, u_l), (dg_l, u_h))):
                        ins = mm(bank[b][:, shift:TP], d[:, b, n, :], v[:, b, 0:TP - shift], start=n == 0 and k == 0,
                                 stop=n == PT - 1 and k == 2)
                ins.then_inc(s_cvp, 1)

            def conv_before(i, b):
                if isinstance(i, int) and b == 0:
                    return
                pe_conv(i * 2 + (b - 1), 1 - b)
            gemm(ph["pw1"], xa, xa_ready(NORM["down01"]), sums("down01"), conv_before)
            pe_conv(DC - 1, 1)
            pe.wait_ge(s_ux, DC)
            pe.wait_ge(s_cvr, DC)
            for q in range(2):
                rows_out(R["conv_c"] + q, lambda c: tail_c[:, 4 * q + c, :], UT, 4, False)
            pe.wait_ge(s_ss, 9 * ADD["mean"] + 9)
            sum_channels()
            pe.wait_ge(s_mu, 1)
            for m in range(DC):
                pe.wait_ge(s_sq, 8 * SQ["var"] + m + 1)
                for half in range(2):
                    ins = mm(psum_s[:, half, 0:HT], ones[:, :], sq[:, m % 2, half * HT:(half + 1) * HT],
                             start=m == 0, stop=m == DC - 1)
                ins.then_inc(s_sqp if m < DC - 1 else s_stat, 1)
            gemm(ph["pw2"], hid, low_ready(HB["pw2"]))
            ffn(1)
            pe.wait_ge(s_xnew, XN["down11"] + DC)
            pe.wait_ge(s_rowsd, R["y"] + 5)
            for t in range(5):
                if t >= 2:
                    pe.wait_ge(*((s_yd, t // 2) if t % 2 else (s_rowsd, R["y"] + 5 + t // 2)))
                rows_out(R["y"] + 5 + t, lambda c: x[:, 4 + c, t * P:t * P + (P if t < 4 else TS)],
                         P if t < 4 else TS, 4, False)


_INS = ["x_prompt", "x_sample", "cache_k", "cache_v", "cache_logf", "page_table", "state_conv_a", "state_conv_c",
        "state_ffn", "norm_mix0", "w_in0", "b_forget", "conv_a_w", "q_norm", "k_norm", "w_out0", "norm_mix1",
        "w_pw1", "b_pw1", "conv_c_w", "conv_c_b", "ln_c_g", "ln_c_b", "w_pw2", "norm_ffn", "w_up", "conv_ffn_w",
        "w_down"]
_OUTS = [("y_prompt", (1, TP, D)), ("y_sample", (NB, NT, D)),
         ("p_conv_a", (1, 1, 2, 512)), ("s_conv_a", (1, NB, 2, 512)),
         ("p_k", (1, 1, TP, NH, HD)), ("s_k", (1, NB, NT, NH, HD)),
         ("p_v", (1, 1, TP, NH, HD)), ("s_v", (1, NB, NT, NH, HD)),
         ("p_logf", (1, 1, TP, NH)), ("s_logf", (1, NB, NT, NH)),
         ("p_conv_c", (1, 1, CC - 1, D)), ("s_conv_c", (1, NB, CC - 1, D)),
         ("p_ffn", (2, 1, 2, DFF)), ("s_ffn", (2, NB, 2, DFF))]


def kernel(**inputs):
    import numpy as np
    import concourse.bacc as bacc
    from concourse.bass_utils import run_bass_kernel_spmd

    nc = bacc.Bacc("TRN2", target_bir_lowering=False, num_devices=1, dynamic_dma_scratch_size=SCRATCH)
    arrays, a, o = {}, {}, {}
    for name in _INS:
        v = np.ascontiguousarray(inputs[name])
        arrays[f"in_{name}"] = v
        a[name] = nc.dram_tensor(f"in_{name}", v.shape, mybir.dt.from_np(v.dtype), kind="ExternalInput").ap()
    for name, shape in _OUTS:
        o[name] = nc.dram_tensor(f"out_{name}", shape, F32, kind="ExternalOutput").ap()
    build(nc, a, o)
    r = run_bass_kernel_spmd(nc, [arrays], core_ids=[0])
    return tuple(r.results[0][f"out_{name}"] for name, _ in _OUTS)
```
